# Optimizing a Trainium2 kernel written in Bass

```python
import jax, jax.numpy as jnp
from jax import lax
import numpy as np

D_MODEL = 1024
BATCH = 1
SEQ = 4096
DEPTH = 1

N_MIXERS = 2
GRID_W = 64
N_FOURIER_GROUPS = 4
FOURIER_GROUP_DIM = D_MODEL // N_FOURIER_GROUPS
N_HEADS = 16
HEAD_DIM = D_MODEL // N_HEADS
WIN_ROWS = 8
WIN_COLS = 16
N_EXPERTS = 32
N_GROUPS = 4
EXPERTS_PER_GROUP = N_EXPERTS // N_GROUPS
TOP_K = 2
D_EXPERT = D_MODEL // 2
ROUTE_BLOCK = 256
DEEPNORM_ALPHA = (2 * DEPTH) ** 0.25
DEEPNORM_BETA = (8 * DEPTH) ** -0.25
LN_EPS = 1e-5
N_FOURIER_LAYERS = (DEPTH + N_MIXERS - 1) // N_MIXERS
N_NA_LAYERS = DEPTH // N_MIXERS

kernel_name = 'hybrid_fnet_natten_grouped_moe_deepnorm'

def layer_norm(x, g, b):
    xf = x.astype(jnp.float32)
    mu = xf.mean(-1, keepdims=True)
    var = jnp.square(xf - mu).mean(-1, keepdims=True)
    y = (xf - mu) * lax.rsqrt(var + LN_EPS) * g.astype(jnp.float32) + b.astype(jnp.float32)
    return y.astype(x.dtype)

def fourier_mixer(x, w_in, w_out):
    B, S, _ = x.shape
    u = (x @ w_in).reshape(B, S, N_FOURIER_GROUPS, FOURIER_GROUP_DIM)
    f = jnp.fft.fft2(u.astype(jnp.float32), axes=(1, 3), norm='ortho').real
    return f.reshape(B, S, D_MODEL).astype(x.dtype) @ w_out

def neighbourhood_attention_mixer(x, w_qkv, rpb, w_out):
    B, S, _ = x.shape
    rows = S // GRID_W
    kr = min(WIN_ROWS, rows)
    kc = min(WIN_COLS, GRID_W)
    qkv = (x @ w_qkv).reshape(B, S, 3, N_HEADS, HEAD_DIM)
    q = qkv[:, :, 0] * (HEAD_DIM ** -0.5)
    k = qkv[:, :, 1]
    v = qkv[:, :, 2]
    row_start = jnp.clip(jnp.arange(rows) - kr // 2, 0, rows - kr)
    cols = jnp.arange(GRID_W)
    col_start = jnp.clip(cols - kc // 2, 0, GRID_W - kc)
    col_mask = (cols[None, :] >= col_start[:, None]) & (cols[None, :] < col_start[:, None] + kc)
    mask = jnp.broadcast_to(col_mask[:, None, :], (GRID_W, kr, GRID_W)).reshape(GRID_W, kr * GRID_W)
    col_idx = jnp.clip(cols[None, :] - cols[:, None] + WIN_COLS - 1, 0, 2 * WIN_COLS - 2)

    def one_row(r):
        rs = row_start[r]
        q_r = lax.dynamic_slice_in_dim(q, r * GRID_W, GRID_W, axis=1)
        k_r = lax.dynamic_slice_in_dim(k, rs * GRID_W, kr * GRID_W, axis=1)
        v_r = lax.dynamic_slice_in_dim(v, rs * GRID_W, kr * GRID_W, axis=1)
        s = jnp.einsum('bqhd,bkhd->bhqk', q_r, k_r).astype(jnp.float32)
        row_idx = rs + jnp.arange(kr) - r + WIN_ROWS - 1
        bias = rpb[:, row_idx][:, :, col_idx]
        bias = bias.transpose(0, 2, 1, 3).reshape(N_HEADS, GRID_W, kr * GRID_W)
        s = jnp.where(mask, s + bias.astype(jnp.float32), -jnp.inf)
        p = jax.nn.softmax(s, axis=-1).astype(v.dtype)
        return jnp.einsum('bhqk,bkhd->bqhd', p, v_r)

    o = lax.map(one_row, jnp.arange(rows))
    o = o.transpose(1, 0, 2, 3, 4).reshape(B, S, D_MODEL)
    return o @ w_out

def grouped_moe(h, w_router, b_router, w_gate, w_up, w_down):
    B, S, D = h.shape
    T = B * S
    xt = h.reshape(T, D)
    scores = jax.nn.sigmoid((xt @ w_router).astype(jnp.float32))
    sel = (scores + b_router.astype(jnp.float32)).reshape(T, N_GROUPS, EXPERTS_PER_GROUP)
    group_score = lax.top_k(sel, TOP_K)[0].sum(-1)
    group = jnp.argmax(group_score, axis=-1)
    in_group = jnp.take_along_axis(sel, group[:, None, None], axis=1)[:, 0]
    _, local = lax.top_k(in_group, TOP_K)
    expert_idx = group[:, None] * EXPERTS_PER_GROUP + local
    gate = jnp.take_along_axis(scores, expert_idx, axis=1)
    gate = gate / gate.sum(-1, keepdims=True)
    A = T * TOP_K
    flat_e = expert_idx.reshape(A)
    order = jnp.argsort(flat_e, stable=True)
    sorted_e = flat_e[order]
    sorted_tok = order // TOP_K
    sorted_gate = gate.reshape(A)[order]
    counts = jnp.bincount(flat_e, length=N_EXPERTS)
    padded = (counts + ROUTE_BLOCK - 1) // ROUTE_BLOCK * ROUTE_BLOCK
    pad_end = jnp.cumsum(padded)
    pad_start = pad_end - padded
    seg_start = jnp.cumsum(counts) - counts
    dest = pad_start[sorted_e] + jnp.arange(A) - seg_start[sorted_e]
    n_blocks = -(-A // ROUTE_BLOCK) + N_EXPERTS
    P = n_blocks * ROUTE_BLOCK
    slot_tok = jnp.full((P,), T, jnp.int32).at[dest].set(sorted_tok.astype(jnp.int32))
    x_pad = jnp.concatenate([xt, jnp.zeros((1, D), xt.dtype)], axis=0)
    xs = x_pad[slot_tok].reshape(n_blocks, ROUTE_BLOCK, D)
    block_expert = jnp.minimum(
        jnp.searchsorted(pad_end, jnp.arange(n_blocks) * ROUTE_BLOCK, side='right'), N_EXPERTS - 1)

    def expert_block(args):
        xb, e = args
        hb = jax.nn.silu(xb @ w_gate[e]) * (xb @ w_up[e])
        return hb @ w_down[e]

    ys = lax.map(expert_block, (xs, block_expert)).reshape(P, D)
    contrib = ys[dest] * sorted_gate[:, None].astype(ys.dtype)
    out = jax.ops.segment_sum(contrib, sorted_tok, num_segments=T)
    return out.reshape(B, S, D)

def setup_inputs(seed: int = 0) -> dict:
    key = jax.random.key(seed)
    ks = jax.random.split(key, 14)
    f32 = jnp.float32

    def nrm(k, shape, scale):
        return jax.random.normal(k, shape, f32) * scale

    d_inv = D_MODEL ** -0.5
    return {
        'x': nrm(ks[0], (BATCH, SEQ, D_MODEL), 1.0),
        'fourier_w_in': nrm(ks[1], (N_FOURIER_LAYERS, D_MODEL, D_MODEL), d_inv),
        'fourier_w_out': nrm(ks[2], (N_FOURIER_LAYERS, D_MODEL, D_MODEL), d_inv * DEEPNORM_BETA),
        'na_w_qkv': nrm(ks[3], (N_NA_LAYERS, D_MODEL, 3 * D_MODEL), d_inv),
        'na_rpb': nrm(ks[4], (N_NA_LAYERS, N_HEADS, 2 * WIN_ROWS - 1, 2 * WIN_COLS - 1), 0.02),
        'na_w_out': nrm(ks[5], (N_NA_LAYERS, D_MODEL, D_MODEL), d_inv * DEEPNORM_BETA),
        'router_w': nrm(ks[6], (D_MODEL, N_EXPERTS), d_inv),
        'router_b': nrm(ks[7], (N_EXPERTS,), 0.01),
        'expert_w_gate': nrm(ks[8], (DEPTH, N_EXPERTS, D_MODEL, D_EXPERT), d_inv),
        'expert_w_up': nrm(ks[9], (DEPTH, N_EXPERTS, D_MODEL, D_EXPERT), d_inv),
        'expert_w_down': nrm(ks[10], (DEPTH, N_EXPERTS, D_EXPERT, D_MODEL), D_EXPERT ** -0.5 * DEEPNORM_BETA),
        'ln_g': 1.0 + nrm(ks[11], (DEPTH, 2, D_MODEL), 0.02),
        'ln_b': nrm(ks[12], (DEPTH, 2, D_MODEL), 0.02),
    }

def reference(x, fourier_w_in, fourier_w_out, na_w_qkv, na_rpb, na_w_out, router_w, router_b,
              expert_w_gate, expert_w_up, expert_w_down, ln_g, ln_b):
    for i in range(DEPTH):
        j = i // N_MIXERS
        if i % N_MIXERS == 0:
            y = fourier_mixer(x, fourier_w_in[j], fourier_w_out[j])
        else:
            y = neighbourhood_attention_mixer(x, na_w_qkv[j], na_rpb[j], na_w_out[j])
        x = layer_norm(DEEPNORM_ALPHA * x + y, ln_g[i, 0], ln_b[i, 0])
        y = grouped_moe(x, router_w, router_b, expert_w_gate[i], expert_w_up[i], expert_w_down[i])
        x = layer_norm(DEEPNORM_ALPHA * x + y, ln_g[i, 1], ln_b[i, 1])
    return x


_drawn_inputs = setup_inputs


def setup_inputs(seed=0):
    import zlib

    import numpy as np

    out = dict(_drawn_inputs(seed))
    spreads = {}
    factors = {}
    for name, (base, spread) in spreads.items():
        noise = np.random.default_rng([zlib.crc32(name.encode()), seed]).standard_normal(out[name].shape)
        drawn = base * np.exp(spread * noise) if base else spread * noise
        out[name] = __import__('jax').numpy.asarray(drawn.astype(out[name].dtype))
    for name, factor in factors.items():
        out[name] = (out[name] * factor).astype(out[name].dtype)
    return out
```

```python
from contextlib import ExitStack

import numpy as np

import concourse.bass as bass
from concourse import mybir


P = 128
S, D = 4096, 1024
N2 = S // P
GROUP_DIM = 256
NG = D // GROUP_DIM
CH = D // P
HALF = 512
E, EG, EPG = 32, 4, 8
F = 512
FC = F // P
PAIRS = P // 2
GROUPS = PAIRS // 4
TILES = S // P
RANKS = S
ALPHA = 2.0 ** 0.25
EPS = 1e-5

F32 = mybir.dt.float32
I32 = mybir.dt.int32
ALU = mybir.AluOpType
ACT = mybir.ActivationFunctionType
AX = mybir.AxisListType.X
ds = bass.ds


def shape_constants():
    n1 = np.arange(P)[:, None]
    f1 = np.zeros((P, P))
    for p in range(PAIRS):
        f1[:, 2 * p] = np.cos(2 * np.pi * n1[:, 0] * p / P)
        f1[:, 2 * p + 1] = -np.sin(2 * np.pi * n1[:, 0] * p / P)
    f1[:, 1] = np.cos(np.pi * n1[:, 0])
    f1 /= np.sqrt(S * GROUP_DIM)

    def freqs(p):
        return np.arange(N2) * (P // 2) if p == 0 else p + P * np.arange(N2)

    m2 = np.zeros((P, PAIRS // 2, 2, 2, N2))
    n2 = np.arange(N2)[:, None]
    for p in range(PAIRS):
        th = 2 * np.pi * n2 * freqs(p)[None, :] / S
        c, s = np.cos(th), np.sin(th)
        q, j = p // 2, p % 2
        re, im = slice(j * 64, j * 64 + 32), slice(j * 64 + 32, j * 64 + 64)
        if p:
            m2[re, q, 0, j], m2[im, q, 0, j] = c, s
            m2[re, q, 1, j], m2[im, q, 1, j] = -s, c
        else:
            m2[re, q, 0, j, 0::2], m2[im, q, 0, j, 1::2] = c[:, 0::2], c[:, 1::2]
            m2[re, q, 1, j, 0::2], m2[im, q, 1, j, 1::2] = -s[:, 0::2], -s[:, 1::2]
            alt = (-1.0) ** n2[:, 0]
            m2[re, q, 0, j, 0] = (1 + alt) / 2
            m2[re, q, 1, j, 0] = (1 - alt) / 2
    m2 = m2.reshape(P, PAIRS // 2, P)

    k = np.arange(P)[:, None, None] + P * np.arange(2)[None, :, None]
    ang = 2 * np.pi * k * np.arange(P)[None, None, :] / GROUP_DIM
    cs = np.stack([np.cos(ang), np.sin(ang)], 1)
    alt = np.zeros((P, NG, NG))
    for g in range(NG):
        alt[:, g, g] = (-1.0) ** np.arange(P)
    row_of = np.zeros((P, TILES), np.int32)
    for t in range(TILES):
        for m in range(P):
            kk = freqs(4 * (t // 2) + m // N2)[m % N2]
            row_of[m, t] = kk if t % 2 == 0 else (S - kk if kk else S // 2)
    before = (np.arange(P)[:, None] < np.arange(P)[None, :]) * 1.0
    first = np.tile(EPG - np.arange(EPG), EG)[None, :] * np.ones((P, 1))
    firstg = (EG - np.arange(EG))[None, :] * np.ones((P, 1))
    ebase = (np.arange(E) * RANKS)[None, :] * np.ones((P, 1))
    steps = (np.arange(S // P) * P)[None, :] * np.ones((P, 1))
    parts = [("f1", f1), ("ident", np.eye(P)), ("before", before), ("ones", np.ones((P, P))),
             ("cs", cs), ("alt", alt), ("first", first), ("firstg", firstg),
             ("ebase", ebase), ("steps", steps)]
    at, cols, off = {}, [], 0
    for name, a in parts:
        a = a.reshape(P, -1)
        at[name] = (off, off + a.shape[1])
        off += a.shape[1]
        cols.append(a)
    packed = np.concatenate(cols, 1).astype(np.float32)
    return packed, at, m2.astype(np.float32), row_of


def own_wait(eng, sem, value, gate):
    eng.wait_ge(sem, value)
    eng.sem_inc(gate, 1)


class Steps:

    def __init__(self, eng, sem):
        self.eng, self.sem, self.start, self.k = eng, sem, 0, 0

    def begin(self, start):
        self.start, self.k = start, 0

    def link(self, ins):
        self.k += 1
        ins.then_inc(self.sem, 1)
        self.eng.wait_ge(self.sem, self.start + self.k)


def jobs_even(j):
    return j // 2 + 1


def jobs_odd(j):
    return (j + 1) // 2


def is_first(g, n=1):
    return isinstance(g, int) and g < n


def s2_base(g):
    if isinstance(g, int):
        return 0 if g == 0 else 4 if g == 1 else 8 * (g - 1)
    return 8 * g - 8


def tr_base(g):
    if isinstance(g, int) and g >= GROUPS - 1:
        return 8 * g if g == GROUPS - 1 else 8 * (GROUPS - 1) + 4
    return 8 * g + 4


def bcast(v, n):
    return bass.AP(v.tensor, v.offset, [[0, n]] + [list(d) for d in v.ap])


def rep_mid(v, n):
    return bass.AP(v.tensor, v.offset, [list(v.ap[0]), [0, n]] + [list(d) for d in v.ap[1:]])


def rep_last(v, n):
    return bass.AP(v.tensor, v.offset, [list(d) for d in v.ap] + [[0, n]])


def trunk_kernel(nc, x, w_in, w_out, router_w, router_b, w_gate, w_up, w_down, ln_g, ln_b,
                 consts, const_at, m2, row_of, out):
    yd = nc.dram_tensor("first_stage", [P, N2, D], F32).ap()
    hd = nc.dram_tensor("h_rows", [S, D], F32).ap()
    lists = nc.dram_tensor("expert_lists", [E * RANKS, 2], I32).ap()
    ye = nc.dram_tensor("expert_out", [2 * S + P, D], F32).ap()

    with ExitStack() as ctx:
        def sb(name, cols, dt=F32):
            return ctx.enter_context(nc.sbuf_tensor(name, [P, cols], dt))

        def sem(name):
            return ctx.enter_context(nc.semaphore(name))

        reg_a = sb("reg_a", CH * D)
        reg_b = sb("reg_b", CH * D)
        reg_c = sb("reg_c", 2 * CH * D)
        reg_d = sb("reg_d", CH * D)
        reg_e = sb("reg_e", 4 * D)

        cst = sb("cst", consts.shape[1])
        rowix = sb("rowix", TILES, I32)
        lng = sb("lng", D)
        lnb = sb("lnb", D)
        rw = sb("rw", CH * E)
        rb = sb("rb", E)
        m2s = sb("m2s", 2 * 2 * P)
        pay = sb("pay", TILES * 2 * 2, I32)
        gates = sb("gates", TILES * 2)
        base = sb("base", E)
        mid = sb("mid", CH * NG)
        edge = sb("edge", CH)
        padl = sb("padl", 2 * P, I32)[:, :]
        tstart = sb("tstart", E + 1, I32)
        desti = sb("desti", 4, I32)
        payg = sb("payg", 8, I32)
        rowg = sb("rowg", 4, I32)
        ix = sb("ix", 2, I32)
        sx = sb("sx", 1, I32)
        eps_c = sb("eps_c", 1)[:, :]
        zer = sb("zer", E)[:, :]

        def small(name, *dims):
            v = sb(name, int(np.prod(dims)))[:, :]
            if len(dims) == 2:
                return v.rearrange("p (a b) -> p a b", a=dims[0])
            if len(dims) == 3:
                return v.rearrange("p (a b c) -> p a b c", a=dims[0], b=dims[1])
            return v

        lnst, lnmv = small("lnst", 2, 2, 6), small("lnmv", 2, 2)
        lnstd, lnrs, lnsh = small("lnstd", 2), small("lnrs", 2), small("lnsh", 2)
        sc, sel, sel2, eq, rank, msum = (small(n, 2, E) for n in ("sc", "sel", "sel2", "eq", "rank", "msum"))
        onehot = [small("onehot0", 2, E), small("onehot1", 2, E)]
        top = [small("top0", 2, EG), small("top1", 2, EG)]
        kmax, gsum, geq = (small(n, 2, EG) for n in ("kmax", "gsum", "geq"))
        gmax, gden = small("gmax", 2), small("gden", 2)
        gk, destf = small("gk", 2, 2), small("destf", 2, 2)
        ntile, cum = small("ntile", E), small("cum", E + 1)

        def cview(name):
            lo, hi = const_at[name]
            return cst[:, lo:hi]

        f1, ident, before, ones = (cview(n) for n in ("f1", "ident", "before", "ones"))
        first, firstg, ebase, steps = (cview(n) for n in ("first", "firstg", "ebase", "steps"))
        cs = cview("cs").rearrange("p (m k n) -> p m k n", m=2, k=2)
        alt = cview("alt").rearrange("p (g n) -> p g n", g=NG)
        m2t = m2s[:, :].rearrange("p (b q n) -> p b q n", b=2, q=2)
        payv = pay[:, :].rearrange("p (t k w) -> p t k w", t=TILES, k=2)
        gatev = gates[:, :].rearrange("p (t k) -> p t k", t=TILES)
        rwv = rw[:, :].rearrange("p (c e) -> p c e", c=CH)

        w_in_s = reg_a[:, :].rearrange("p (c n) -> p c n", c=CH)
        w_in_g = reg_a[:, :].rearrange("p (q n) -> p q n", n=GROUP_DIM)
        w_out_s = reg_b[:, :].rearrange("p (c n) -> p c n", c=CH)
        A, B = w_in_s, w_out_s
        fold = reg_d[:, :].rearrange("p (m c g n) -> p m c g n", m=2, c=CH, g=NG)
        foldq = reg_d[:, :].rearrange("p (m q n) -> p m q n", m=2, n=P)
        foldT = reg_c[:, 0:CH * D].rearrange("p (m g d) -> p m g d", m=2, g=NG)
        T = reg_c[:, CH * D:].rearrange("p (m g d) -> p m g d", m=2, g=NG)
        midv = mid[:, :].rearrange("p (c g) -> p c g", c=CH)
        midT, T128 = lnb[:, :], lng[:, :]
        xch = reg_e[:, :].rearrange("p (b n d) -> p b n d", b=2, n=2)
        ych = reg_d[:, 0:4 * D].rearrange("p (b n d) -> p b n d", b=2, n=2)

        yt = reg_e[:, :].rearrange("p (b q d) -> p b q d", b=2, q=2)
        xt = reg_c[:, 3 * CH * F:].rearrange("p (b m c n) -> p b m c n", b=2, m=2, c=CH)
        rows = reg_d[:, 0:4 * D].rearrange("p (b s d) -> p b s d", b=2, s=2)
        qs = reg_d[:, 4 * D:5 * D]
        hT = reg_d[:, 5 * D:6 * D].rearrange("p (c n) -> p c n", c=CH)
        cmp = reg_d[0:1, 6 * D:7 * D].rearrange("p (e j) -> p e j", e=E)

        wg = [reg_c[:, 0:4096].rearrange("p (c f) -> p c f", c=CH), reg_a[:, 0:4096].rearrange("p (c f) -> p c f", c=CH)]
        wu = [reg_c[:, 4096:8192].rearrange("p (c f) -> p c f", c=CH), reg_a[:, 4096:8192].rearrange("p (c f) -> p c f", c=CH)]
        wd = [reg_c[:, 8192:12288].rearrange("p (c f) -> p c f", c=FC), reg_b[:, 0:4096].rearrange("p (c f) -> p c f", c=FC)]
        xrow = reg_b[:, 4096:5120]
        xrow_s = xrow.rearrange("p (d c) -> p c d", c=CH)
        mxT = reg_b[:, 5120:6144].rearrange("p (c n) -> p c n", c=CH)
        sgate = reg_b[:, 6144:6656]
        hid = reg_b[:, 6656:7168]
        hid_s = hid.rearrange("p (d c) -> p c d", c=FC)
        hidT = reg_b[:, 7168:7680].rearrange("p (c n) -> p c n", c=FC)
        yrow = reg_c[:, 12288:13312]

        fin_h = reg_a[:, 0:2 * D].rearrange("p (b d) -> p b d", b=2)
        fin_y = reg_a[:, 2 * D:6 * D].rearrange("p (b k d) -> p b k d", b=2, k=2)
        fin_r = reg_a[:, 6 * D:8 * D].rearrange("p (b d) -> p b d", b=2)

        pairs = [ctx.enter_context(nc.psum_tensor(f"ps{i}", [P, D], F32)) for i in range(4)]
        bank = [pairs[i // 2][:, (i % 2) * HALF:(i % 2 + 1) * HALF] for i in range(8)]
        psP, psQ, psX, psR = pairs

        c_in = sem("c_in")
        rb_in = sem("rb_in")
        wo_in, wi_in = sem("wo_in"), sem("wi_in")
        folded_e, folded_o = sem("folded_e"), sem("folded_o")
        x_in = [sem("x_in0"), sem("x_in1")]
        y1_out = [sem("y1_out0"), sem("y1_out1")]
        job_ps, job_act, job_dve = sem("job_ps"), sem("job_act"), sem("job_dve")
        yt_in = [sem("yt_in0"), sem("yt_in1")]
        rows_in = [sem("rows_in0"), sem("rows_in1")]
        xj_ps, xj_ev = sem("xj_ps"), sem("xj_ev")
        q_ps, p_ps, q_ev, p_ev, q_used = (sem(n) for n in ("q_ps", "p_ps", "q_ev", "p_ev", "q_used"))
        var_ok, std_ok, nrm_ok, hn_ok, hg_ok, h_ok = (
            sem(n) for n in ("var_ok", "std_ok", "nrm_ok", "hn_ok", "hg_ok", "h_ok"))
        h_out = [sem("h_out0"), sem("h_out1")]
        lg_ps, sg_ok, m_ok, rk_ps, dest_ok, list_out = (
            sem(n) for n in ("lg_ps", "sg_ok", "m_ok", "rk_ps", "dest_ok", "list_out"))
        pad_made, pad_out, pay_made = sem("pad_made"), sem("pad_out"), sem("pay_made")
        ln_in, rowg_ok, payg_ok, made = (sem(n) for n in ("ln_in", "rowg_ok", "payg_ok", "made"))
        dve_step = sem("dve_step")
        dve_gate, pool_gate = sem("dve_gate"), sem("pool_gate")
        act_step = sem("act_step")
        tab_ok = sem("tab_ok")
        wg_in = [sem("wg_in0"), sem("wg_in1")]
        wu_in = [sem("wu_in0"), sem("wu_in1")]
        wd_in = [sem("wd_in0"), sem("wd_in1")]
        ix_in, xrow_in, y_out, sx_ok = sem("ix_in"), sem("xrow_in"), sem("y_out"), sem("sx_ok")
        g_ps, u_ps, x0_ps, x1_ps, x0_ev, x1_ev = (
            sem(n) for n in ("g_ps", "u_ps", "x0_ps", "x1_ps", "x0_ev", "x1_ev"))
        silu_ok, hid_ok, ht_ps, ht_ev, y_ps, ya_ok, yd_ok = (
            sem(n) for n in ("silu_ok", "hid_ok", "ht_ps", "ht_ev", "y_ps", "ya_ok", "yd_ok"))
        ln2_in = sem("ln2_in")
        fin_in = [sem("fin_in0"), sem("fin_in1")]
        fa_ok, fs_ok, fstd_ok, fn_ok, fnn_ok, fg_ok, fb_ok, fh_ok = (
            sem(n) for n in ("fa_ok", "fs_ok", "fstd_ok", "fn_ok", "fnn_ok", "fg_ok", "fb_ok", "fh_ok"))
        fin_out = [sem("fin_out0"), sem("fin_out1")]

        JOB_TR = 18
        JOB_S1 = JOB_TR + 18
        JOB_AB = JOB_S1 + 2 * N2
        JOBS = JOB_AB + 4 * CH

        def phase0_dst(j):
            h = slice(j % 2 * HALF, (j % 2 + 1) * HALF)
            if j < JOB_TR - 2:
                return T[:, j // 8, j % 8 // 2, h]
            if j < JOB_TR:
                return T128[0:NG, h]
            t = j - JOB_TR
            return foldT[:, t // 8, t % 8 // 2, h] if t < 16 else midT[0:NG, h]

        def ab_dst(j):
            return (A, B)[j // 16][:, j % 16 // 2, j % 2 * HALF:(j % 2 + 1) * HALF]

        def expert_tiles(eng, tile):
            with eng.Fori(0, E // 2) as i:
                for b in range(2):
                    lo = eng.value_load(tstart[0:1, ds(2 * i + b, 1)], min_val=0, max_val=96)
                    hi = eng.value_load(tstart[0:1, ds(2 * i + b + 1, 1)], min_val=1, max_val=96)
                    with eng.Fori(lo, hi) as t:
                        tile(t, i, b, lo)

        block = ctx.enter_context(nc.Block())

        @block.sync
        def _(sp):
            for b in range(2):
                sp.sem_inc(y1_out[b], 16)
            sp.dma_start(cst[:, :], consts).then_inc(c_in, 16)
            sp.dma_start(w_out_s, w_out.rearrange("(c p) n -> p c n", p=P)).then_inc(wo_in, 16)
            sp.dma_start(w_in_s, w_in.rearrange("(c p) n -> p c n", p=P)).then_inc(wi_in, 16)
            x_v = x.rearrange("(p n) d -> p n d", n=N2)

            def load_x(i, b):
                sp.dma_start(xch[:, b], x_v[:, ds(4 * i + 2 * b, 2), :]).then_inc(x_in[b], 16)

            load_x(0, 0)
            load_x(0, 1)
            sp.dma_start(rowix[:, :], row_of).then_inc(c_in, 16)
            sp.dma_start(rw[:, :].rearrange("p (c e) -> p c e", c=CH),
                         router_w.rearrange("(c p) e -> p c e", p=P)).then_inc(rb_in, 16)
            sp.dma_start(rb[:, :], bcast(router_b, P)).then_inc(rb_in, 16)
            sp.wait_ge(pad_made, 1)
            pads = lists.rearrange("(b p r) w -> b p (r w)", p=P, r=P)
            for b in range(E * RANKS // (P * P)):
                sp.dma_start(pads[b], padl).then_inc(pad_out, 16)

            def store_y(i, b):
                sp.wait_ge(job_act, jobs_even(JOB_S1 + 4 * b + 3) + 4 * i)
                sp.wait_ge(job_dve, jobs_odd(JOB_S1 + 4 * b + 3) + 4 * i)
                sp.dma_start(yd[:, ds(4 * i + 2 * b, 2), :], ych[:, b]).then_inc(y1_out[b], 16)

            STEPS = N2 // 4
            with sp.Fori(0, STEPS - 1) as i:
                for b in range(2):
                    sp.wait_ge(job_ps, JOB_S1 + 8 * i + 4 * b + 4)
                    load_x(i + 1, b)
                    store_y(i, b)
            for b in range(2):
                store_y(STEPS - 1, b)
            for b in range(2):
                sp.wait_ge(y1_out[b], 16 * STEPS + 16)

            def load_yt(g, i, b, first=False):
                if not first:
                    sp.wait_ge(xj_ps, s2_base(g - 2) + 4)
                sp.dma_start(yt[:, b], yd_v[:, ds(2 * g, 2), :]).then_inc(yt_in[b], 16)
                sp.dma_start(m2t[:, b], m2[:, ds(2 * g, 2), :]).then_inc(yt_in[b], 16)

            yd_v = yd.rearrange("(q a) n d -> (a n) q d", a=4)

            def store_h(g, b):
                sp.wait_ge(h_ok, 2 * g + 2)
                sp.dma_start(hd_v[:, ds(2 * g, 2), :], rows[:, b]).then_inc(h_out[b], 16)

            hd_v = hd.rearrange("(t p) d -> p t d", p=P)
            load_yt(0, 0, 0, first=True)
            load_yt(1, 0, 1, first=True)
            sp.wait_ge(job_ps, JOBS)
            sp.dma_start(lng[:, :], bcast(ln_g[0], P)).then_inc(ln_in, 16)
            sp.dma_start(lnb[:, :], bcast(ln_b[0], P)).then_inc(ln_in, 16)
            for b in range(2):
                load_yt(2 + b, 1, b)
                store_h(b, b)
            wg_v = w_gate.rearrange("e (p c) f -> p e (c f)", p=P)
            wu_v = w_up.rearrange("e (p c) f -> p e (c f)", p=P)
            wd_v = w_down.rearrange("e (p c) f -> p e (c f)", p=P)

            def flat(v):
                return v.rearrange("p c f -> p (c f)").rearrange("p (o n) -> p o n", o=1)

            def load_w(e, b, first=False):
                if first:
                    if b == 1:
                        sp.wait_ge(p_ps, GROUPS)
                else:
                    done = sp.value_load(tstart[0:1, ds(e - 1, 1)], min_val=1, max_val=96)
                    sp.wait_ge(u_ps, done)
                sp.dma_start(flat(wg[b]), wg_v[:, ds(e, 1), :]).then_inc(wg_in[b], 16)
                sp.dma_start(flat(wu[b]), wu_v[:, ds(e, 1), :]).then_inc(wu_in[b], 16)
                if not first:
                    sp.wait_ge(y_ps, done)
                sp.dma_start(flat(wd[b]), wd_v[:, ds(e, 1), :]).then_inc(wd_in[b], 16)

            load_w(0, 0, first=True)
            with sp.Fori(1, GROUPS // 2 - 1) as i:
                for b in range(2):
                    load_yt(2 * i + 2 + b, i + 1, b)
                    store_h(2 * i + b, b)
            for b in range(2):
                store_h(GROUPS - 2 + b, b)

            load_w(1, 1, first=True)
            sp.wait_ge(tab_ok, 1)
            with sp.Fori(1, E // 2) as i:
                for b in range(2):
                    load_w(2 * i + b, b)

            total = sp.value_load(tstart[0:1, E:E + 1], min_val=E, max_val=96)
            sp.wait_ge(u_ps, total)
            sp.wait_ge(y_out, total * 16 + 16)
            for b in range(2):
                sp.wait_ge(h_out[b], 16 * GROUPS // 2)
            sp.dma_start(lng[:, :], bcast(ln_g[1], P)).then_inc(ln2_in, 16)
            sp.dma_start(lnb[:, :], bcast(ln_b[1], P)).then_inc(ln2_in, 16)
            ye_v = ye[0:2 * S, :].rearrange("(t p k) d -> p t k d", p=P, k=2)

            def load_fin(i, b, first=False):
                t = 2 * i + b
                if not first:
                    sp.wait_ge(fs_ok, t - 1)
                sp.dma_start(fin_h[:, b:b + 1, :], hd_v[:, ds(t, 1), :]).then_inc(fin_in[b], 16)
                sp.dma_start(fin_y[:, b:b + 1], ye_v[:, ds(t, 1)]).then_inc(fin_in[b], 16)

            load_fin(0, 0, first=True)
            load_fin(0, 1, first=True)
            with sp.Fori(1, TILES // 2) as i:
                for b in range(2):
                    load_fin(i, b)

        @block.tensor
        def _(pe):
            def bank_free(j):
                if j < 8:
                    return
                if j % 2 == 0:
                    pe.wait_ge(job_act, jobs_even(j - 8))
                else:
                    pe.wait_ge(job_dve, jobs_odd(j - 8))

            pe.wait_ge(c_in, 32)
            pe.wait_ge(wo_in, 16)
            j = 0
            for m in range(2):
                for g in range(NG):
                    for h in range(2):
                        bank_free(j)
                        for k in range(2):
                            mm = nc.tensor.matmul(bank[j % 8], cs[:, m, k, :],
                                                  w_out_s[:, 2 * g + k, h * HALF:(h + 1) * HALF],
                                                  start=(k == 0), stop=(k == 1))
                        mm.then_inc(job_ps, 1)
                        j += 1
            for h in range(2):
                bank_free(j)
                for c in range(CH):
                    mm = nc.tensor.matmul(bank[j % 8][0:NG, :], alt[:, c // 2, :],
                                          w_out_s[:, c, h * HALF:(h + 1) * HALF],
                                          start=(c == 0), stop=(c == CH - 1))
                mm.then_inc(job_ps, 1)
                j += 1
            for m in range(2):
                pe.wait_ge(folded_e if m == 0 else folded_o, 3 if m == 0 else 2)
                for g in range(NG):
                    for h in range(2):
                        bank_free(j)
                        for c in range(4):
                            mm = nc.tensor.transpose(bank[j % 8][:, c * P:(c + 1) * P],
                                                     fold[:, m, 4 * h + c, g, :], ident)
                        mm.then_inc(job_ps, 1)
                        j += 1
            for h in range(2):
                bank_free(j)
                for c in range(4):
                    mm = nc.tensor.transpose(bank[j % 8][0:NG, c * P:(c + 1) * P],
                                             midv[:, 4 * h + c, :], ident)
                mm.then_inc(job_ps, 1)
                j += 1
            with pe.Fori(0, N2 // 4) as i:
                for b in range(2):
                    pe.wait_ge(x_in[b], 16 * i + 16)
                    for n in range(2):
                        for h in range(2):
                            jj = 4 * b + 2 * n + h
                            if (JOB_S1 + jj) % 2 == 0:
                                pe.wait_ge(job_act, jobs_even(JOB_S1 + jj - 8) + 4 * i)
                            else:
                                pe.wait_ge(job_dve, jobs_odd(JOB_S1 + jj - 8) + 4 * i)
                            nc.tensor.matmul(bank[(JOB_S1 + jj) % 8], f1,
                                             xch[:, b, n, h * HALF:(h + 1) * HALF],
                                             start=True, stop=True).then_inc(job_ps, 1)
            j = JOB_AB
            pe.wait_ge(job_act, jobs_even(JOB_S1 - 1))
            pe.wait_ge(job_dve, jobs_odd(JOB_S1 - 1))
            for m in range(2):
                for c in range(CH):
                    for h in range(2):
                        bank_free(j)
                        for g in range(NG):
                            mm = nc.tensor.matmul(bank[j % 8], foldT[:, m, g, c * P:(c + 1) * P],
                                                  T[:, m, g, h * HALF:(h + 1) * HALF],
                                                  start=(g == 0), stop=(m == 1 and g == NG - 1))
                        if m == 0:
                            mm = nc.tensor.matmul(bank[j % 8], midT[0:NG, c * P:(c + 1) * P],
                                                  T128[0:NG, h * HALF:(h + 1) * HALF],
                                                  start=False, stop=True)
                        mm.then_inc(job_ps, 1)
                        j += 1
            pe.wait_ge(job_act, jobs_even(JOBS - 1))
            pe.wait_ge(job_dve, jobs_odd(JOBS - 1))

            def second_stage(g, i, b):
                base_j = s2_base(g)
                pe.wait_ge(yt_in[b], 32 * i + 32)
                for jj in range(4):
                    if not is_first(base_j, 2 - jj):
                        pe.wait_ge(xj_ev, base_j + jj - 1)
                    for c in range(2):
                        for q in range(2):
                            lo = (jj % 2) * HALF + c * 256 + q * P
                            cc = 2 * jj + c
                            mm = nc.tensor.matmul(psX[:, lo:lo + P],
                                                  yt[:, b, q, cc * P:(cc + 1) * P],
                                                  m2t[:, b, q, :], start=True, stop=True)
                    mm.then_inc(xj_ps, 1)

            def product(g, b, m, ps, w, free, done, edge_row=False):
                if not is_first(g):
                    pe.wait_ge(free, g)
                for h in range(2):
                    for c in range(CH):
                        if edge_row and c == CH - 1:
                            for ce in range(CH):
                                nc.tensor.matmul(ps[0:1, h * HALF:(h + 1) * HALF],
                                                 edge[:, ce:ce + 1],
                                                 A[:, ce, h * HALF:(h + 1) * HALF],
                                                 start=False, stop=False, skip_group_check=True)
                        mm = nc.tensor.matmul(ps[:, h * HALF:(h + 1) * HALF], xt[:, b, m, c, :],
                                              w[:, c, h * HALF:(h + 1) * HALF],
                                              start=(c == 0), stop=(c == CH - 1),
                                              skip_group_check=edge_row)
                mm.then_inc(done, 1)

            def turn_rows(g, b, base_j):
                for s in range(2):
                    pe.wait_ge(h_ok, 2 * g + 1 + s)
                    for hh in range(2):
                        jj = 2 * s + hh
                        pe.wait_ge(xj_ev, base_j + jj - 1)
                        for c in range(4):
                            lo = (jj % 2) * HALF + c * P
                            cc = 4 * hh + c
                            mm = nc.tensor.transpose(psX[:, lo:lo + P],
                                                     rows[:, b, s, cc * P:(cc + 1) * P], ident)
                        mm.then_inc(xj_ps, 1)
                    pe.wait_ge(xj_ev, base_j + 2 * s + 2)
                    if s == 0 and not is_first(g):
                        pe.wait_ge(sg_ok, g)
                    for c in range(CH):
                        mm = nc.tensor.matmul(psR[:, s * E:(s + 1) * E], hT[:, c, :], rwv[:, c, :],
                                              start=(c == 0), stop=(c == CH - 1))
                    mm.then_inc(lg_ps, 1)

            def ranks(g):
                pe.wait_ge(m_ok, g + 1)
                r0, r1, r2 = (psR[:, HALF + i * E:HALF + (i + 1) * E] for i in range(3))
                nc.tensor.matmul(r0, before, msum[:, 0], start=True, stop=True)
                nc.tensor.matmul(r1, before, msum[:, 1], start=True, stop=False)
                nc.tensor.matmul(r1, ones, msum[:, 0], start=False, stop=True)
                nc.tensor.matmul(r2, ones, msum[:, 0], start=True, stop=False)
                nc.tensor.matmul(r2, ones, msum[:, 1], start=False, stop=True).then_inc(rk_ps, 1)

            def group(g, i, b):
                pe.wait_ge(xj_ev, s2_base(g) + 4)
                if isinstance(g, int) and g == 0:
                    pe.wait_ge(act_step, 2)
                product(g, b, 1, psQ, B, q_ev, q_ps, edge_row=isinstance(g, int) and g == 0)
                if not is_first(g, 2):
                    ranks(g - 2)
                product(g, b, 0, psP, A, p_ev, p_ps)
                if not (isinstance(g, int) and g == GROUPS - 1):
                    second_stage(g + 1, i if b == 0 else i + 1, 1 - b)
                if not is_first(g):
                    turn_rows(g - 1, 1 - b, tr_base(g))

            second_stage(0, 0, 0)
            pe.wait_ge(rb_in, 32)
            group(0, 0, 0)
            group(1, 0, 1)
            with pe.Fori(1, GROUPS // 2 - 1) as i:
                for b in range(2):
                    group(2 * i + b, i, b)
            for b in range(2):
                group(GROUPS - 2 + b, GROUPS // 2 - 1, b)
            ranks(GROUPS - 2)
            turn_rows(GROUPS - 1, 1, tr_base(GROUPS))
            ranks(GROUPS - 1)

            psG, psU = bank[0], bank[1]
            psY, psX0, psX1, psH = pairs[1], bank[4], bank[5], bank[6]
            pe.sem_inc(x1_ps, 1)
            pe.wait_ge(p_ev, GROUPS)
            pe.wait_ge(q_ev, GROUPS)
            pe.wait_ge(xj_ev, tr_base(GROUPS) + 4)
            pe.wait_ge(tab_ok, 1)

            def turn_x(half, ps, done):
                for c in range(4):
                    mm = nc.tensor.transpose(ps[:, c * P:(c + 1) * P],
                                             xrow_s[:, 4 * half + c, :], ident)
                mm.then_inc(done, 1)

            def tile(t, i, b, lo):
                pe.wait_ge(x0_ev, t + 1)
                pe.wait_ge(x1_ev, t + 1)
                pe.wait_ge(wg_in[b], 16 * i + 16)
                for c in range(CH):
                    mm = nc.tensor.matmul(psG, mxT[:, c, :], wg[b][:, c, :],
                                          start=(c == 0), stop=(c == CH - 1))
                mm.then_inc(g_ps, 1)
                pe.wait_ge(wu_in[b], 16 * i + 16)
                for c in range(CH):
                    mm = nc.tensor.matmul(psU, mxT[:, c, :], wu[b][:, c, :],
                                          start=(c == 0), stop=(c == CH - 1))
                mm.then_inc(u_ps, 1)
                pe.wait_ge(xrow_in, 16 * t + 32)
                turn_x(0, psX0, x0_ps)
                pe.wait_ge(hid_ok, t + 1)
                for c in range(FC):
                    mm = nc.tensor.transpose(psH[:, c * P:(c + 1) * P], hid_s[:, c, :], ident)
                mm.then_inc(ht_ps, 1)
                turn_x(1, psX1, x1_ps)
                pe.wait_ge(ht_ev, t + 1)
                pe.wait_ge(wd_in[b], 16 * i + 16)
                pe.wait_ge(ya_ok, t + 1)
                pe.wait_ge(yd_ok, t + 1)
                for h in range(2):
                    for c in range(FC):
                        mm = nc.tensor.matmul(psY[:, h * HALF:(h + 1) * HALF], hidT[:, c, :],
                                              wd[b][:, c, h * HALF:(h + 1) * HALF],
                                              start=(c == 0), stop=(c == FC - 1))
                mm.then_inc(y_ps, 1)

            pe.wait_ge(xrow_in, 16)
            turn_x(0, psX0, x0_ps)
            turn_x(1, psX1, x1_ps)
            expert_tiles(pe, tile)

        @block.scalar
        def _(act):
            def empty(dst, src, j):
                act.wait_ge(job_ps, j + 1)
                nc.scalar.copy(dst, src).then_inc(job_act, 1)

            for j in range(0, JOB_S1, 2):
                dst = phase0_dst(j)
                empty(dst, bank[j % 8][0:dst.shape[0], :], j)
            with act.Fori(0, N2 // 4) as i:
                for b in range(2):
                    for jj in range(4 * b, 4 * b + 4):
                        if (JOB_S1 + jj) % 2 == 0:
                            if jj % 4 < 2:
                                act.wait_ge(y1_out[b], 16 * i + 16)
                            act.wait_ge(job_ps, JOB_S1 + 8 * i + jj + 1)
                            n, h = (jj % 4) // 2, jj % 2
                            nc.scalar.copy(ych[:, b, n, h * HALF:(h + 1) * HALF],
                                           bank[(JOB_S1 + jj) % 8]).then_inc(job_act, 1)
            for j in range(JOB_AB, JOBS, 2):
                empty(ab_dst(j - JOB_AB), bank[j % 8], j)

            def empty_s2(g, b):
                for jj in range(4):
                    act.wait_ge(xj_ps, s2_base(g) + jj + 1)
                    src = psX[:, (jj % 2) * HALF:(jj % 2 + 1) * HALF].rearrange(
                        "p (c q m n) -> p c q m n", c=2, q=2, m=2)
                    for m in range(2):
                        dst = xt[:, b, m, 2 * jj:2 * jj + 2, :].rearrange("p c (q n) -> p c q n", q=2)
                        a = nc.scalar.copy(dst, src[:, :, :, m, :])
                    a.then_inc(xj_ev, 1)

            def empty_turn(base_j, g):
                for jj in range(4):
                    act.wait_ge(xj_ps, base_j + jj + 1)
                    if jj == 2 or (jj == 0 and not is_first(g)):
                        act.wait_ge(lg_ps, 2 * g + jj // 2)
                    hh = jj % 2
                    nc.scalar.copy(hT[:, 4 * hh:4 * hh + 4, :].rearrange("p c n -> p (c n)"),
                                   psX[:, (jj % 2) * HALF:(jj % 2 + 1) * HALF]).then_inc(xj_ev, 1)

            def scores(g):
                act.wait_ge(lg_ps, 2 * g + 2)
                if not is_first(g):
                    act.wait_ge(dest_ok, g)
                nc.scalar.activation(sc.rearrange("p s e -> p (s e)"), psR[:, 0:2 * E],
                                     ACT.Sigmoid).then_inc(sg_ok, 1)

            def group(g, b, last=False):
                act.wait_ge(q_ps, g + 1)
                if not is_first(g):
                    act.wait_ge(q_used, g)
                nc.scalar.copy(qs, psQ[:, :]).then_inc(q_ev, 1)
                if not last:
                    empty_s2(g + 1, 1 - b)
                if not is_first(g):
                    empty_turn(tr_base(g), g - 1)
                    scores(g - 1)
                act.wait_ge(var_ok, g + 1)
                nc.scalar.activation(lnstd, lnmv[:, :, 1], ACT.Sqrt, bias=eps_c).then_inc(std_ok, 1)
                act.wait_ge(nrm_ok, g + 1)
                for s in range(2):
                    nc.scalar.activation(rows[:, b, s, :], rows[:, b, s, :], ACT.Identity,
                                         bias=lnsh[:, s:s + 1], scale=lnrs[:, s:s + 1]
                                         ).then_inc(hn_ok, 1)

            empty_s2(0, 0)
            act.wait_ge(xj_ev, 4)
            nc.scalar.copy(edge[:, :], xt[:, 0, 1, :, 0]).then_inc(act_step, 1)
            act.wait_ge(act_step, 1)
            act.wait_ge(made, 1)
            nc.scalar.copy(xt[:, 0, 1, :, 0], zer[:, 0:CH]).then_inc(act_step, 1)
            group(0, 0)
            group(1, 1)
            with act.Fori(1, GROUPS // 2 - 1) as i:
                for b in range(2):
                    group(2 * i + b, b)
            group(GROUPS - 2, 0)
            group(GROUPS - 1, 1, last=True)
            empty_turn(tr_base(GROUPS), GROUPS - 1)
            scores(GROUPS - 1)

            psG = bank[0]
            psX0 = bank[4]
            act.wait_ge(tab_ok, 1)

            def turn_x():
                nc.scalar.copy(mxT[:, 0:4, :].rearrange("p c n -> p (c n)"), psX0).then_inc(x0_ev, 1)

            def tile(t, i, b, lo):
                act.wait_ge(g_ps, t + 1)
                nc.scalar.activation(sgate, psG, ACT.Silu).then_inc(silu_ok, 1)
                act.wait_ge(x0_ps, t + 2)
                turn_x()
                act.wait_ge(y_ps, t + 1)
                act.wait_ge(y_out, 16 * t + 16)
                nc.scalar.copy(yrow[:, 0:HALF], pairs[1][:, 0:HALF]).then_inc(ya_ok, 1)

            act.wait_ge(x0_ps, 1)
            turn_x()
            expert_tiles(act, tile)

            def fin(t, i, b):
                act.wait_ge(fin_in[b], 32 * i + 32)
                if not (isinstance(i, int) and i == 0):
                    act.wait_ge(fin_out[b], 16 * i)
                nc.scalar.mul(fin_r[:, b, :], fin_h[:, b, :], ALPHA).then_inc(fa_ok, 1)
                act.wait_ge(fn_ok, t + 1)
                nc.scalar.activation(lnstd[:, b:b + 1], lnmv[:, b, 1:2], ACT.Sqrt,
                                     bias=eps_c).then_inc(fstd_ok, 1)
                act.wait_ge(fnn_ok, t + 1)
                nc.scalar.activation(fin_r[:, b, :], fin_r[:, b, :], ACT.Identity,
                                     bias=lnsh[:, b:b + 1], scale=lnrs[:, b:b + 1]).then_inc(fg_ok, 1)

            for b in range(2):
                fin(b, 0, b)
            with act.Fori(1, TILES // 2) as i:
                for b in range(2):
                    fin(2 * i + b, i, b)

        @block.vector
        def _(dve):
            step = Steps(dve, dve_step)
            link = step.link
            nc.vector.memset(eps_c, EPS)
            nc.vector.memset(base[:, :], 0.0)
            nc.vector.memset(zer, 0.0).then_inc(made, 1)
            dve.wait_ge(wi_in, 16)
            nc.vector.tensor_tensor(foldq[:, 0, :, 1:P], w_in_g[:, :, 1:P],
                                    w_in_g[:, :, GROUP_DIM - 1:P:-1], ALU.add).then_inc(folded_e, 1)
            nc.vector.tensor_copy(foldq[:, 0, :, 0:1], w_in_g[:, :, 0:1]).then_inc(folded_e, 1)
            nc.vector.tensor_copy(midv.rearrange("p c g -> p (c g)").rearrange("p (q o) -> p q o", o=1),
                                  w_in_g[:, :, P:P + 1]).then_inc(folded_e, 1)

            def empty(dst, src, j):
                dve.wait_ge(job_ps, j + 1)
                nc.vector.tensor_copy(dst, src).then_inc(job_dve, 1)

            for j in range(1, JOB_S1, 2):
                dst = phase0_dst(j)
                empty(dst, bank[j % 8][0:dst.shape[0], :], j)
            with dve.Fori(0, N2 // 4) as i:
                for b in range(2):
                    for jj in range(4 * b, 4 * b + 4):
                        if (JOB_S1 + jj) % 2 == 1:
                            if jj % 4 < 2:
                                dve.wait_ge(y1_out[b], 16 * i + 16)
                            dve.wait_ge(job_ps, JOB_S1 + 8 * i + jj + 1)
                            n, h = (jj % 4) // 2, jj % 2
                            nc.vector.tensor_copy(ych[:, b, n, h * HALF:(h + 1) * HALF],
                                                  bank[(JOB_S1 + jj) % 8]).then_inc(job_dve, 1)
            for j in range(JOB_AB + 1, JOBS, 2):
                empty(ab_dst(j - JOB_AB), bank[j % 8], j)

            def statistics(src, s):
                nc.vector.bn_stats(lnst[:, s, 0, :], src[:, 0:HALF])
                link(nc.vector.bn_stats(lnst[:, s, 1, :], src[:, HALF:D]))
                dve.sem_inc(dve_gate, 1)
                return nc.vector.bn_aggr(lnmv[:, s, :], lnst[:, s].rearrange("p h w -> p (h w)"))

            def rows_ready(g, b, i):
                dve.wait_ge(p_ps, g + 1)
                dve.wait_ge(rows_in[b], 32 * i + 32)
                for s in range(2):
                    a = nc.vector.scalar_tensor_tensor(rows[:, b, s, :], rows[:, b, s, :], ALPHA,
                                                       psP[:, :], ALU.mult, ALU.add)
                a.then_inc(p_ev, 1)
                dve.wait_ge(p_ev, g + 1)
                dve.wait_ge(q_ev, g + 1)
                nc.vector.tensor_tensor(rows[:, b, 0, :], rows[:, b, 0, :], qs, ALU.add)
                nc.vector.tensor_tensor(rows[:, b, 1, :], rows[:, b, 1, :], qs,
                                        ALU.subtract).then_inc(q_used, 1)
                dve.wait_ge(q_used, g + 1)
                for s in range(2):
                    a = statistics(rows[:, b, s, :], s)
                a.then_inc(var_ok, 1)
                dve.wait_ge(std_ok, g + 1)
                link(nc.vector.reciprocal(lnrs, lnstd))
                nc.vector.scalar_tensor_tensor(lnsh, lnmv[:, :, 0], -1.0, lnrs,
                                               ALU.mult, ALU.mult).then_inc(nrm_ok, 1)
                for s in range(2):
                    dve.wait_ge(hn_ok, 2 * g + s + 1)
                    nc.vector.tensor_tensor(rows[:, b, s, :], rows[:, b, s, :], lng[:, :],
                                            ALU.mult).then_inc(hg_ok, 1)

            def grp(v):
                return v.rearrange("p s (g j) -> p s g j", j=EPG)

            first_g = bass.AP(first.tensor, first.offset,
                              [list(first.ap[0]), [0, 2], [EPG, EG], [1, EPG]])

            def choose(g):
                dve.wait_ge(sg_ok, g + 1)
                link(nc.vector.tensor_tensor(sel, sc, rep_mid(rb[:, :], 2), ALU.add))
                cur = sel
                for k in range(2):
                    link(nc.vector.tensor_reduce(top[k], grp(cur), AX, ALU.max))
                    link(nc.vector.tensor_tensor(grp(eq), grp(cur), rep_last(top[k], EPG), ALU.is_equal))
                    link(nc.vector.tensor_tensor(eq, eq, rep_mid(first, 2), ALU.mult))
                    link(nc.vector.tensor_reduce(kmax, grp(eq), AX, ALU.max))
                    link(nc.vector.tensor_tensor(grp(onehot[k]), first_g, rep_last(kmax, EPG),
                                                 ALU.is_equal))
                    if k == 0:
                        link(nc.vector.scalar_tensor_tensor(
                            sel2.rearrange("p s e -> p (s e)"), onehot[0].rearrange("p s e -> p (s e)"),
                            -1e30, sel.rearrange("p s e -> p (s e)"), ALU.mult, ALU.add))
                        cur = sel2
                link(nc.vector.tensor_tensor(gsum, top[0], top[1], ALU.add))
                link(nc.vector.tensor_reduce(gmax, gsum, AX, ALU.max))
                link(nc.vector.tensor_tensor(geq, gsum, rep_last(gmax, EG), ALU.is_equal))
                link(nc.vector.tensor_tensor(geq, geq, rep_mid(firstg, 2), ALU.mult))
                link(nc.vector.tensor_reduce(gmax, geq, AX, ALU.max))
                link(nc.vector.tensor_tensor(geq, rep_mid(firstg, 2), rep_last(gmax, EG), ALU.is_equal))
                for k in range(2):
                    link(nc.vector.tensor_tensor(grp(onehot[k]), grp(onehot[k]), rep_last(geq, EPG),
                                                 ALU.mult))
                nc.vector.tensor_tensor(msum, onehot[0], onehot[1], ALU.add).then_inc(m_ok, 1)

            def place(g):
                for k in range(2):
                    link(nc.vector.tensor_tensor(eq, sc, onehot[k], ALU.mult))
                    link(nc.vector.tensor_reduce(gk[:, :, k], eq, AX, ALU.add))
                link(nc.vector.tensor_tensor(gden, gk[:, :, 0], gk[:, :, 1], ALU.add))
                link(nc.vector.reciprocal(gden, gden))
                nc.vector.tensor_tensor(gatev[:, ds(2 * g, 2), :], gk, rep_last(gden, 2), ALU.mult)
                dve.wait_ge(rk_ps, g + 1)
                link(nc.vector.tensor_tensor(
                    rank, psR[:, HALF:HALF + 2 * E].rearrange("p (s e) -> p s e", s=2),
                    rep_mid(base[:, :], 2), ALU.add))
                link(nc.vector.tensor_tensor(base[:, :], base[:, :],
                                             psR[:, HALF + 2 * E:HALF + 3 * E], ALU.add))
                link(nc.vector.tensor_tensor(rank, rank, rep_mid(ebase, 2), ALU.add))
                for k in range(2):
                    link(nc.vector.tensor_tensor(eq, rank, onehot[k], ALU.mult))
                    link(nc.vector.tensor_reduce(
                        destf[:, :, k], eq, AX, ALU.add))
                if not is_first(g):
                    dve.wait_ge(list_out, 64 * g)
                nc.vector.tensor_copy(desti[:, :], destf.rearrange("p s k -> p (s k)")).then_inc(dest_ok, 1)
                dve.wait_ge(dest_ok, g + 1)

            ROWS_STEPS, ROUTE_STEPS = 3, 33

            def group(g, b, i):
                if not is_first(g, 2):
                    step.begin(2 * ROWS_STEPS + (ROUTE_STEPS + ROWS_STEPS) * (g - 2))
                    choose(g - 2)
                    place(g - 2)
                    assert step.k == ROUTE_STEPS, step.k
                    rows_ready(g, b, i)
                    assert step.k == ROUTE_STEPS + ROWS_STEPS
                else:
                    rows_ready(g, b, i)

            dve.wait_ge(rb_in, 32)
            dve.wait_ge(c_in, 32)
            dve.wait_ge(ln_in, 32)
            group(0, 0, 0)
            group(1, 1, 0)
            with dve.Fori(1, GROUPS // 2 - 1) as i:
                for b in range(2):
                    group(2 * i + b, b, i)
            for b in range(2):
                group(GROUPS - 2 + b, b, GROUPS // 2 - 1)
            for g in (GROUPS - 2, GROUPS - 1):
                choose(g)
                place(g)
            link(nc.vector.tensor_tensor(
                cmp, rep_last(base[0:1, :], S // P), rep_mid(steps[0:1, :], E), ALU.is_gt))
            link(nc.vector.tensor_reduce(ntile[0:1, :], cmp, AX, ALU.add))
            link(nc.vector.tensor_scalar_max(ntile[0:1, :], ntile[0:1, :], 1.0))
            nc.vector.memset(cum[0:1, 0:1], 0.0)
            link(nc.vector.tensor_tensor_scan(cum[0:1, 1:E + 1], ntile[0:1, :], zer[0:1, 0:E], 0.0,
                                              ALU.add, ALU.add))
            nc.vector.tensor_copy(tstart[0:1, :], cum[0:1, :]).then_inc(tab_ok, 1)
            dve.wait_ge(tab_ok, 1)

            psU, psX1, psH = bank[1], bank[5], bank[6]

            def turn_x():
                nc.vector.tensor_copy(mxT[:, 4:8, :].rearrange("p c n -> p (c n)"), psX1
                                      ).then_inc(x1_ev, 1)

            def tile(t, i, b, lo):
                dve.wait_ge(u_ps, t + 1)
                dve.wait_ge(silu_ok, t + 1)
                nc.vector.tensor_tensor(hid, sgate, psU, ALU.mult).then_inc(hid_ok, 1)
                dve.wait_ge(ht_ps, t + 1)
                nc.vector.tensor_copy(hidT.rearrange("p c n -> p (c n)"), psH).then_inc(ht_ev, 1)
                dve.wait_ge(x1_ps, t + 3)
                turn_x()
                dve.wait_ge(y_ps, t + 1)
                dve.wait_ge(y_out, 16 * t + 16)
                nc.vector.tensor_copy(yrow[:, HALF:D], pairs[1][:, HALF:D]).then_inc(yd_ok, 1)

            dve.wait_ge(x1_ps, 2)
            turn_x()
            expert_tiles(dve, tile)

            dve.wait_ge(ln2_in, 32)

            def fin(t, i, b):
                dve.wait_ge(fa_ok, t + 1)
                for k in range(2):
                    a = nc.vector.scalar_tensor_tensor(fin_r[:, b, :], fin_y[:, b, k, :],
                                                       gates[:, ds(2 * t + k, 1)], fin_r[:, b, :],
                                                       ALU.mult, ALU.add)
                    if k == 0:
                        link(a)
                a.then_inc(fs_ok, 1)
                dve.wait_ge(fs_ok, t + 1)
                statistics(fin_r[:, b, :], b).then_inc(fn_ok, 1)
                dve.wait_ge(fstd_ok, t + 1)
                link(nc.vector.reciprocal(lnrs[:, b:b + 1], lnstd[:, b:b + 1]))
                nc.vector.scalar_tensor_tensor(lnsh[:, b:b + 1], lnmv[:, b, 0:1], -1.0,
                                               lnrs[:, b:b + 1], ALU.mult, ALU.mult).then_inc(fnn_ok, 1)
                dve.wait_ge(fg_ok, t + 1)
                nc.vector.tensor_tensor(fin_r[:, b, :], fin_r[:, b, :], lng[:, :],
                                        ALU.mult).then_inc(fb_ok, 1)

            FIN_STEPS = 3
            start = step.start + step.k
            with dve.Fori(0, TILES // 2) as i:
                for b in range(2):
                    step.begin(start + FIN_STEPS * (2 * i + b))
                    fin(2 * i + b, i, b)
                    assert step.k == FIN_STEPS

        @block.gpsimd
        def _(pool):
            nc.gpsimd.iota(padl.rearrange("p (r w) -> p r w", w=2), [[1, P], [2 * S, 2]], base=0,
                           channel_multiplier=0).then_inc(pad_made, 1)
            nc.gpsimd.iota(payv[:, :, :, 0], [[P, TILES], [0, 2]], base=0,
                           channel_multiplier=1).then_inc(pay_made, 1)
            nc.gpsimd.iota(payv[:, :, :, 1], [[2 * P, TILES], [1, 2]], base=0,
                           channel_multiplier=2).then_inc(pay_made, 1)
            pool.wait_ge(wi_in, 16)
            nc.gpsimd.memset(foldq[:, 1, :, 0:1], 0.0).then_inc(folded_o, 1)
            nc.gpsimd.tensor_tensor(foldq[:, 1, :, 1:P], w_in_g[:, :, 1:P],
                                    w_in_g[:, :, GROUP_DIM - 1:P:-1], ALU.subtract).then_inc(folded_o, 1)

            def fetch(g, i, b):
                if not is_first(g, 2):
                    pool.wait_ge(xj_ps, tr_base(g - 1) + 4)
                    pool.wait_ge(h_out[b], 16 * i)
                nc.gpsimd.tensor_copy(rowg[:, 2 * b:2 * b + 2], rowix[:, ds(2 * g, 2)]
                                      ).then_inc(rowg_ok, 1)
                own_wait(pool, rowg_ok, g + 1, pool_gate)
                for s in range(2):
                    pool.indirect_dma_start(
                        rows[:, b, s, :], None, x,
                        bass.IndirectOffsetOnAxis(ap=rowg[:, 2 * b + s:2 * b + s + 1], axis=0)
                    ).then_inc(rows_in[b], 16)

            def list_tokens(g):
                if not is_first(g):
                    pool.wait_ge(list_out, 64 * g)
                nc.gpsimd.tensor_copy(payg[:, :], pay[:, ds(8 * g, 8)]).then_inc(payg_ok, 1)
                pool.wait_ge(payg_ok, g + 1)
                own_wait(pool, dest_ok, g + 1, pool_gate)
                for s in range(2):
                    for k in range(2):
                        pool.indirect_dma_start(
                            lists, bass.IndirectOffsetOnAxis(ap=desti[:, 2 * s + k:2 * s + k + 1], axis=0),
                            payg[:, 4 * s + 2 * k:4 * s + 2 * k + 2], None).then_inc(list_out, 16)

            def shift(g, b):
                for s in range(2):
                    pool.wait_ge(hg_ok, 2 * g + s + 1)
                    nc.gpsimd.tensor_tensor(rows[:, b, s, :], rows[:, b, s, :], lnb[:, :],
                                            ALU.add).then_inc(h_ok, 1)

            def group(g, b, i):
                fetch(g, i, b)
                if not is_first(g, 2):
                    list_tokens(g - 2)
                shift(g, b)

            pool.wait_ge(c_in, 32)
            pool.wait_ge(pay_made, 2)
            for b in range(2):
                pool.wait_ge(y1_out[b], 16 * (N2 // 4) + 16)
            pool.wait_ge(ln_in, 32)
            pool.wait_ge(pad_out, 16 * (E * RANKS // (P * P)))
            group(0, 0, 0)
            group(1, 1, 0)
            with pool.Fori(1, GROUPS // 2 - 1) as i:
                for b in range(2):
                    group(2 * i + b, b, i)
            for b in range(2):
                group(GROUPS - 2 + b, b, GROUPS // 2 - 1)
            list_tokens(GROUPS - 2)
            list_tokens(GROUPS - 1)

            lists_v = lists.rearrange("(r p) w -> r p w", p=P)
            pool.wait_ge(p_ps, GROUPS)
            pool.wait_ge(list_out, 64 * GROUPS)
            for b in range(2):
                pool.wait_ge(h_out[b], 16 * (GROUPS // 2))
            nc.gpsimd.memset(yrow[:, 0:HALF], 0.0).then_inc(ya_ok, 1)
            nc.gpsimd.memset(yrow[:, HALF:D], 0.0).then_inc(yd_ok, 1)
            nc.gpsimd.iota(sx[:, :], [[0, 1]], base=2 * S, channel_multiplier=1).then_inc(sx_ok, 1)
            pool.wait_ge(sx_ok, 1)
            pool.wait_ge(tab_ok, 1)

            def gather(t):
                own_wait(pool, x1_ps, t + 1, pool_gate)
                pool.indirect_dma_start(xrow, None, hd, bass.IndirectOffsetOnAxis(ap=ix[:, 0:1], axis=0)
                                        ).then_inc(xrow_in, 16)

            def scatter(t):
                pool.wait_ge(ya_ok, t + 1)
                own_wait(pool, yd_ok, t + 1, pool_gate)
                pool.indirect_dma_start(ye, bass.IndirectOffsetOnAxis(ap=sx[:, 0:1], axis=0),
                                        yrow, None).then_inc(y_out, 16)
                pool.wait_ge(y_out, 16 * t + 16)

            def tile(t, i, b, lo):
                r = ((2 * i + b) * (RANKS // P) + (t - lo)).with_bounds(
                    min_val=0, max_val=E * RANKS // P - 1)
                pool.dma_start(ix[:, :].rearrange("p (o w) -> p o w", o=1),
                               lists_v[ds(r, 1)].rearrange("o p w -> p o w")).then_inc(ix_in, 16)
                pool.wait_ge(ix_in, 16 * t + 16)
                gather(t)
                scatter(t)
                own_wait(pool, xrow_in, 16 * t + 16, pool_gate)
                nc.gpsimd.tensor_copy(sx[:, :], ix[:, 1:2]).then_inc(sx_ok, 1)
                pool.wait_ge(sx_ok, t + 2)

            expert_tiles(pool, tile)
            total = pool.value_load(tstart[0:1, E:E + 1], min_val=E, max_val=96)
            gather(total)
            scatter(total)

            pool.wait_ge(ln2_in, 32)

            def fin(t, i, b):
                pool.wait_ge(fb_ok, t + 1)
                nc.gpsimd.tensor_tensor(fin_r[:, b, :], fin_r[:, b, :], lnb[:, :],
                                        ALU.add).then_inc(fh_ok, 1)
                if not is_first(i):
                    own_wait(pool, fin_out[b], 16 * i, pool_gate)
                nc.gpsimd.tensor_copy(rowg[:, b:b + 1], rowix[:, ds(t, 1)]).then_inc(rowg_ok, 1)
                pool.wait_ge(fh_ok, t + 1)
                own_wait(pool, rowg_ok, GROUPS + t + 1, pool_gate)
                pool.indirect_dma_start(
                    out, bass.IndirectOffsetOnAxis(ap=rowg[:, b:b + 1], axis=0),
                    fin_r[:, b, :], None).then_inc(fin_out[b], 16)

            for b in range(2):
                fin(b, 0, b)
            with pool.Fori(1, TILES // 2) as i:
                for b in range(2):
                    fin(2 * i + b, i, b)
            for b in range(2):
                pool.wait_ge(fin_out[b], 16 * (TILES // 2))


_INS = ["x", "fourier_w_in", "fourier_w_out", "router_w", "router_b",
        "expert_w_gate", "expert_w_up", "expert_w_down", "ln_g", "ln_b"]


def kernel(**inputs):
    import concourse.bacc as bacc
    from concourse.bass_utils import run_bass_kernel_spmd

    nc = bacc.Bacc("TRN2", target_bir_lowering=False, num_devices=1)
    arrays, ap = {}, {}

    def declare(name, a):
        arrays[name] = a
        ap[name] = nc.dram_tensor(name, a.shape, mybir.dt.from_np(a.dtype), kind="ExternalInput").ap()

    for name in _INS:
        declare(name, np.ascontiguousarray(inputs[name]))
    packed, const_at, m2, row_of = shape_constants()
    declare("consts", packed)
    declare("second_stage", m2)
    declare("row_of", row_of)
    out = nc.dram_tensor("out", (1, S, D), F32, kind="ExternalOutput").ap()
    trunk_kernel(nc, ap["x"][0], ap["fourier_w_in"][0], ap["fourier_w_out"][0], ap["router_w"],
                 ap["router_b"], ap["expert_w_gate"][0], ap["expert_w_up"][0],
                 ap["expert_w_down"][0], ap["ln_g"][0], ap["ln_b"][0],
                 ap["consts"], const_at, ap["second_stage"], ap["row_of"], out[0])
    r = run_bass_kernel_spmd(nc, [arrays], core_ids=[0])
    return r.results[0]["out"]
```

```python
from contextlib import ExitStack

import numpy as np

import concourse.bass as bass
from concourse import mybir


P = 128
S, D = 4096, 1024
N2 = S // P
GROUP_DIM = 256
NG = D // GROUP_DIM
CH = D // P
HALF = 512
E, EG, EPG = 32, 4, 8
F = 512
FC = F // P
PAIRS = P // 2
GROUPS = PAIRS // 4
TILES = S // P
RANKS = S
BLOCKS = RANKS // P
LANE_BITS = P.bit_length() - 1
ENTRY_BITS = (E * BLOCKS).bit_length() - 1
MAX_TILES = 2 * TILES + 2 * E
SLOTS = 4
PIECES, GU_PIECES = 12, 8
FB = 4
ARENA = 16512
ALPHA = 2.0 ** 0.25
EPS = 1e-5

F32 = mybir.dt.float32
F32R = mybir.dt.float32r
I32 = mybir.dt.int32
ALU = mybir.AluOpType
ACT = mybir.ActivationFunctionType
AX = mybir.AxisListType.X
ds = bass.ds


def shape_constants():
    n1 = np.arange(P)[:, None]
    f1 = np.zeros((P, P))
    for p in range(PAIRS):
        f1[:, 2 * p] = np.cos(2 * np.pi * n1[:, 0] * p / P)
        f1[:, 2 * p + 1] = -np.sin(2 * np.pi * n1[:, 0] * p / P)
    f1[:, 1] = np.cos(np.pi * n1[:, 0])
    f1 /= np.sqrt(S * GROUP_DIM)

    def freqs(p):
        return np.arange(N2) * (P // 2) if p == 0 else p + P * np.arange(N2)

    m2 = np.zeros((P, PAIRS // 2, 2, 2, N2))
    n2 = np.arange(N2)[:, None]
    for p in range(PAIRS):
        th = 2 * np.pi * n2 * freqs(p)[None, :] / S
        c, s = np.cos(th), np.sin(th)
        q, j = p // 2, p % 2
        re, im = slice(j * 64, j * 64 + 32), slice(j * 64 + 32, j * 64 + 64)
        if p:
            m2[re, q, 0, j], m2[im, q, 0, j] = c, s
            m2[re, q, 1, j], m2[im, q, 1, j] = -s, c
        else:
            m2[re, q, 0, j, 0::2], m2[im, q, 0, j, 1::2] = c[:, 0::2], c[:, 1::2]
            m2[re, q, 1, j, 0::2], m2[im, q, 1, j, 1::2] = -s[:, 0::2], -s[:, 1::2]
            alt = (-1.0) ** n2[:, 0]
            m2[re, q, 0, j, 0] = (1 + alt) / 2
            m2[re, q, 1, j, 0] = (1 - alt) / 2
    m2 = m2.reshape(P, PAIRS // 2, P)

    k = np.arange(P)[:, None, None] + P * np.arange(2)[None, :, None]
    ang = 2 * np.pi * k * np.arange(P)[None, None, :] / GROUP_DIM
    cs = np.stack([np.cos(ang), np.sin(ang)], 1)
    alt = np.zeros((P, NG, NG))
    for g in range(NG):
        alt[:, g, g] = (-1.0) ** np.arange(P)
    row_of = np.zeros((P, TILES), np.int32)
    for t in range(TILES):
        for m in range(P):
            kk = freqs(4 * (t // 2) + m // N2)[m % N2]
            row_of[m, t] = kk if t % 2 == 0 else (S - kk if kk else S // 2)
    before = (np.arange(P)[:, None] < np.arange(P)[None, :]) * 1.0
    first = np.tile(EPG - np.arange(EPG), EG)[None, :] * np.ones((P, 1))
    firstg = (EG - np.arange(EG))[None, :] * np.ones((P, 1))
    ebase = (np.arange(E) * RANKS)[None, :] * np.ones((P, 1))
    steps = (np.arange(S // P) * P)[None, :] * np.ones((P, 1))
    parts = [("f1", f1), ("ident", np.eye(P)), ("before", before), ("ones", np.ones((P, P))),
             ("cs", cs), ("alt", alt), ("first", first), ("firstg", firstg),
             ("ebase", ebase), ("steps", steps)]
    at, cols, off = {}, [], 0
    for name, a in parts:
        a = a.reshape(P, -1)
        at[name] = (off, off + a.shape[1])
        off += a.shape[1]
        cols.append(a)
    packed = np.concatenate(cols, 1).astype(np.float32)
    return packed, at, m2.astype(np.float32), row_of


def own_wait(eng, sem, value, gate):
    eng.wait_ge(sem, value)
    eng.sem_inc(gate, 1)


PASSES = ((0, 0), (0, 1), (1, 0))


class Steps:

    def __init__(self, eng, sem):
        self.eng, self.sem, self.start, self.k = eng, sem, 0, 0

    def begin(self, start):
        self.start, self.k = start, 0

    def link(self, ins):
        self.k += 1
        ins.then_inc(self.sem, 1)
        self.eng.wait_ge(self.sem, self.start + self.k)


def jobs_even(j):
    return j // 2 + 1


def jobs_odd(j):
    return (j + 1) // 2


def is_first(g, n=1):
    return isinstance(g, int) and g < n


def s2_base(g):
    if isinstance(g, int):
        return 0 if g == 0 else 4 if g == 1 else 8 * (g - 1)
    return 8 * g - 8


def tr_base(g):
    if isinstance(g, int) and g >= GROUPS - 1:
        return 8 * g if g == GROUPS - 1 else 8 * (GROUPS - 1) + 4
    return 8 * g + 4


def bcast(v, n):
    return bass.AP(v.tensor, v.offset, [[0, n]] + [list(d) for d in v.ap])


def rep_mid(v, n):
    return bass.AP(v.tensor, v.offset, [list(v.ap[0]), [0, n]] + [list(d) for d in v.ap[1:]])


def rep_last(v, n):
    return bass.AP(v.tensor, v.offset, [list(d) for d in v.ap] + [[0, n]])


def trunk_kernel(nc, x, w_in, w_out, router_w, router_b, w_gate, w_up, w_down, ln_g, ln_b,
                 consts, const_at, m2, row_of, out):
    yd = nc.dram_tensor("first_stage", [P, N2, D], F32).ap()
    hd = nc.dram_tensor("h_rows", [S + P, D], F32).ap()
    lists = nc.dram_tensor("expert_lists", [P * E * BLOCKS, 2], I32).ap()
    acc = nc.dram_tensor("sums", [S + P, D], F32).ap()

    with ExitStack() as ctx:
        def at(name, kib, cols, dt=F32):
            t = nc.alloc_sbuf_tensor_at(name, [P, cols], dt, offset=ARENA + int(kib * 1024))
            return t[:, :]

        class Row:

            def __init__(self, kib, end):
                self.byte, self.end = int(kib * 1024), int(end * 1024)

            def take(self, name, cols, dt=F32):
                self.byte, lo = self.byte + (cols * 4 + 31) // 32 * 32, self.byte
                assert self.byte <= self.end, name
                return at(name, lo / 1024, cols, dt)

        def sem(name):
            return ctx.enter_context(nc.semaphore(name))

        A = [at("a_hi", 0, CH * D, F32R), at("a_lo", 32, CH * D, F32R)]
        B = [at("b_hi", 64, CH * D, F32R), at("b_lo", 96, CH * D, F32R)]
        A, B = ([v.rearrange("p (c n) -> p c n", c=CH) for v in w] for w in (A, B))
        fold_t = at("fold", 0, CH * D)
        ych_t = at("ych", 32, 4 * D)
        xch_t = at("xch", 48, 4 * D)
        w_in_t = at("w_in_s", 64, CH * D)
        w_out_t = at("w_out_s", 96, CH * D)
        foldT_t = at("foldT", 128, CH * D)
        T_t = at("T", 160, CH * D)
        midT, T128 = at("midT", 192, D), at("T128", 196, D)
        xt_t = [at("xt_hi", 128, 2 * D, F32R), at("xt_lo", 136, 2 * D, F32R)]
        yt_t = at("yt", 144, 4 * D)
        rows_t = at("rows", 160, 4 * D)
        qs = at("qs", 176, D)
        hT_t = at("hT", 180, D)
        lng, lnb = at("lng", 184, D), at("lnb", 188, D)
        edge = [at("edge_hi", 176, D, F32R), at("edge_lo", 180, D, F32R)]
        edge = [v.rearrange("p (c n) -> p c n", c=CH) for v in edge]
        cmp = at("cmp", 176, D)[0:1, :].rearrange("p (e j) -> p e j", e=E)
        grow = Row(192, 200)
        rw, m2s = grow.take("rw", CH * E), grow.take("m2s", 2 * 2 * P)
        wgu = [[at(f"wgu{b}_{n}", kib, 2 * CH * F, F32R).rearrange("p (m c f) -> p m c f", m=2, c=CH)
                for n, kib in (("hi", lo), ("lo", lo + 32))] for b, lo in enumerate((0, 128))]
        wd = [at(f"wd_{n}", kib, FC * D, F32R).rearrange("p (c f) -> p c f", c=FC)
              for n, kib in (("hi", 64), ("lo", 80))]
        mxT = [at(f"mxT_{n}", kib, D, F32R).rearrange("p (c n) -> p c n", c=CH)
               for n, kib in (("hi", 96), ("lo", 100))]
        hidT = [at(f"hidT_{n}", kib, F, F32R).rearrange("p (c n) -> p c n", c=FC)
                for n, kib in (("hi", 104), ("lo", 106))]
        xrow = at("xrow", 108, D)
        wraw = at("wraw", 112, SLOTS * D).rearrange("p (s d) -> p s d", s=SLOTS)
        yrow, sgate, hid = at("yrow", 192, D), at("sgate", 196, F), at("hid", 198, F)
        fin_r = at("fin_r", 128, FB * D).rearrange("p (b d) -> p b d", b=FB)
        lng2, lnb2 = at("lng2", 160, D), at("lnb2", 164, D)

        keep = Row(200, 207.8)
        cst = keep.take("cst", consts.shape[1])
        rowix = keep.take("rowix", TILES, I32)
        pay = keep.take("pay", TILES, I32)
        base = keep.take("base", E)
        tstart = keep.take("tstart", E + 1, I32)
        desti = keep.take("desti", 4, I32)
        payg = keep.take("payg", 8, I32)
        entry_t = keep.take("entries", 2 * 2 * BLOCKS, I32)
        rowg = keep.take("rowg", FB, I32)
        ixg = keep.take("ixg", 1, I32)
        sx = keep.take("sx", 1, I32)
        sxn = keep.take("sxn", 1, I32)
        eps_c, eps2_c = keep.take("eps_c", 1), keep.take("eps2_c", 1)
        zer = keep.take("zer", E)
        rb = keep.take("rb", E)
        mid = keep.take("mid", CH * NG)
        padl = keep.take("padl", 2 * BLOCKS, I32)

        def small(name, *dims):
            v = (keep if name.startswith("ln") else grow).take(name, int(np.prod(dims)))
            if len(dims) == 2:
                return v.rearrange("p (a b) -> p a b", a=dims[0])
            if len(dims) == 3:
                return v.rearrange("p (a b c) -> p a b c", a=dims[0], b=dims[1])
            return v

        lnst, lnmv = small("lnst", FB, 2, 6), small("lnmv", FB, 2)
        lnstd, lnrs, lnsh = small("lnstd", FB), small("lnrs", FB), small("lnsh", FB)
        sc, sel, sel2, eq, rank, msum = (small(n, 2, E) for n in ("sc", "sel", "sel2", "eq", "rank", "msum"))
        onehot = [small("onehot0", 2, E), small("onehot1", 2, E)]
        top = [small("top0", 2, EG), small("top1", 2, EG)]
        kmax, gsum, geq = (small(n, 2, EG) for n in ("kmax", "gsum", "geq"))
        gmax, gden = small("gmax", 2), small("gden", 2)
        gk, destf = small("gk", 2, 2), small("destf", 2, 2)
        dint, dlane = grow.take("dint", 4, I32), grow.take("dlane", 4, I32)
        ntile, cum = small("ntile", E), small("cum", E + 1)

        def cview(name):
            lo, hi = const_at[name]
            return cst[:, lo:hi]

        f1, ident, before, ones = (cview(n) for n in ("f1", "ident", "before", "ones"))
        first, firstg, ebase, steps = (cview(n) for n in ("first", "firstg", "ebase", "steps"))
        cs = cview("cs").rearrange("p (m k n) -> p m k n", m=2, k=2)
        alt = cview("alt").rearrange("p (g n) -> p g n", g=NG)
        m2t = m2s[:, :].rearrange("p (b q n) -> p b q n", b=2, q=2)
        paygv = payg[:, :].rearrange("p (s k w) -> p s k w", s=2, k=2)
        entries = entry_t.rearrange("p (b r w) -> p b r w", b=2, w=2)
        rwv = rw.rearrange("p (c e) -> p c e", c=CH)

        w_in_s = w_in_t.rearrange("p (c n) -> p c n", c=CH)
        w_in_g = w_in_t.rearrange("p (q n) -> p q n", n=GROUP_DIM)
        w_out_s = w_out_t.rearrange("p (c n) -> p c n", c=CH)
        fold = fold_t.rearrange("p (m c g n) -> p m c g n", m=2, c=CH, g=NG)
        foldq = fold_t.rearrange("p (m q n) -> p m q n", m=2, n=P)
        foldT = foldT_t.rearrange("p (m g d) -> p m g d", m=2, g=NG)
        T = T_t.rearrange("p (m g d) -> p m g d", m=2, g=NG)
        midv = mid[:, :].rearrange("p (c g) -> p c g", c=CH)
        xch = xch_t.rearrange("p (b n d) -> p b n d", b=2, n=2)
        ych = ych_t.rearrange("p (b n d) -> p b n d", b=2, n=2)

        yt = yt_t.rearrange("p (b q d) -> p b q d", b=2, q=2)
        xt = [v.rearrange("p (m c n) -> p m c n", m=2, c=CH) for v in xt_t]
        rows = rows_t.rearrange("p (b s d) -> p b s d", b=2, s=2)
        hT = hT_t.rearrange("p (c n) -> p c n", c=CH)
        xrow_s = xrow.rearrange("p (d c) -> p c d", c=CH)

        pairs = [ctx.enter_context(nc.psum_tensor(f"ps{i}", [P, D], F32)) for i in range(4)]
        bank = [pairs[i // 2][:, (i % 2) * HALF:(i % 2 + 1) * HALF] for i in range(8)]
        psP, psQ, psX, psR = pairs
        psG, psY, psX0, psX1 = bank[0], pairs[1], bank[4], bank[5]
        psU = bank[1][:, 0:F // 2], bank[7][:, 0:F // 2]
        psH = bank[6][:, 0:2 * P], bank[0][:, 0:2 * P]

        c_in = sem("c_in")
        rb_in = sem("rb_in")
        wo_in, wi_in = sem("wo_in"), sem("wi_in")
        folded_e, folded_o = sem("folded_e"), sem("folded_o")
        x_in = [sem("x_in0"), sem("x_in1")]
        y1_out = [sem("y1_out0"), sem("y1_out1")]
        job_ps, job_act, job_dve = sem("job_ps"), sem("job_act"), sem("job_dve")
        yt_in = [sem("yt_in0"), sem("yt_in1")]
        rows_in = [sem("rows_in0"), sem("rows_in1")]
        xj_ps, xj_ev = sem("xj_ps"), sem("xj_ev")
        q_ps, p_ps, q_ev, p_ev, q_used = (sem(n) for n in ("q_ps", "p_ps", "q_ev", "p_ev", "q_used"))
        var_ok, std_ok, nrm_ok, hn_ok, hg_ok, h_ok = (
            sem(n) for n in ("var_ok", "std_ok", "nrm_ok", "hn_ok", "hg_ok", "h_ok"))
        h_out = [sem("h_out0"), sem("h_out1")]
        lg_ps, sg_ok, m_ok, rk_ps, gate_ok, dest_ok, list_out = (
            sem(n) for n in ("lg_ps", "sg_ok", "m_ok", "rk_ps", "gate_ok", "dest_ok", "list_out"))
        pad_made, pad_out, pay_made = sem("pad_made"), sem("pad_out"), sem("pay_made")
        ln_in, rowg_ok, payg_ok, made = (sem(n) for n in ("ln_in", "rowg_ok", "payg_ok", "made"))
        dve_step = sem("dve_step")
        dve_gate, pool_gate = sem("dve_gate"), sem("pool_gate")
        edge_ok, edge_read, edge_zero = sem("edge_ok"), sem("edge_read"), sem("edge_zero")
        tab_ok = sem("tab_ok")
        ab_ps, ab_hi, ab_lo, xl_ev = sem("ab_ps"), sem("ab_hi"), sem("ab_lo"), sem("xl_ev")
        wraw_in = [sem(f"wraw_in{n}") for n in range(SLOTS)]
        whi_ok, wlo_ok = sem("whi_ok"), sem("wlo_ok")
        entries_in, spare_out = [sem("entries_in0"), sem("entries_in1")], sem("spare_out")
        xrow_in, y_out, ixg_ok, sx_ok = sem("xrow_in"), sem("y_out"), sem("ixg_ok"), sem("sx_ok")
        g_ps, ua_ps, ub_ps, x0_ps, x1_ps, xh_ev, xlo_ev = (
            sem(n) for n in ("g_ps", "ua_ps", "ub_ps", "x0_ps", "x1_ps", "xh_ev", "xlo_ev"))
        silu_ok, hida_ok, hidb_ok, h0_ps, h1_ps, hh_ev, hl_ev = (
            sem(n) for n in ("silu_ok", "hida_ok", "hidb_ok", "h0_ps", "h1_ps", "hh_ev", "hl_ev"))
        y0_ps, y1_ps, ya_ok, yd_ok = (sem(n) for n in ("y0_ps", "y1_ps", "ya_ok", "yd_ok"))
        ln2_in = sem("ln2_in")
        fin_in = [sem(f"fin_in{b}") for b in range(FB)]
        fstd_ok, fn_ok, fnn_ok, fg_ok, fb_ok, fh_ok = (
            sem(n) for n in ("fstd_ok", "fn_ok", "fnn_ok", "fg_ok", "fb_ok", "fh_ok"))
        fin_out = [sem(f"fin_out{b}") for b in range(FB)]

        JOB_TR = 18
        JOB_S1 = JOB_TR + 18
        JOB_AB = JOB_S1 + 2 * N2
        AB_JOBS = 4 * CH

        def phase0_dst(j):
            h = slice(j % 2 * HALF, (j % 2 + 1) * HALF)
            if j < JOB_TR - 2:
                return T[:, j // 8, j % 8 // 2, h]
            if j < JOB_TR:
                return T128[0:NG, h]
            t = j - JOB_TR
            return foldT[:, t // 8, t % 8 // 2, h] if t < 16 else midT[0:NG, h]

        def ab_dst(j, part):
            return (A, B)[j // 16][part][:, j % 16 // 2, j % 2 * HALF:(j % 2 + 1) * HALF]

        def s2_src(jj):
            return psX[:, (jj % 2) * HALF:(jj % 2 + 1) * HALF].rearrange(
                "p (c q m n) -> p c q m n", c=2, q=2, m=2)

        def s2_dst(part, m, jj):
            return xt[part][:, m, 2 * jj:2 * jj + 2, :].rearrange("p c (q n) -> p c q n", q=2)

        def gu_piece(b, part, j):
            w = wgu[b][part][:, j // 4]
            return w[:, 2 * (j % 4):2 * (j % 4) + 2, :].rearrange("p c f -> p (c f)")

        def block_of(t, lo):
            return (t - lo).with_bounds(min_val=0, max_val=BLOCKS - 1) if t is not lo else 0

        def gate_of(t, b, lo):
            return entries[:, b, ds(block_of(t, lo), 1), 1].bitcast(F32)

        def entries_there(eng, e, b, kind):
            if kind == 0:
                eng.wait_ge(entries_in[b], 8 * e + 16 - 8 * b)

        def expert_tiles(eng, tile):
            def expert(i, b, last=False):
                lo = eng.value_load(tstart[0:1, ds(2 * i + b, 1)], min_val=0, max_val=MAX_TILES)
                hi = eng.value_load(tstart[0:1, ds(2 * i + b + 1, 1)], min_val=2, max_val=MAX_TILES)
                tile(lo, 2 * i + b, b, lo, 0, last)
                tile(lo + 1, 2 * i + b, b, lo, 1, last)
                with eng.If(hi > lo + 2):
                    with eng.Fori(lo + 2, hi) as t:
                        tile(t, 2 * i + b, b, lo, 2, last)

            with eng.Fori(0, E // 2 - 1) as i:
                for b in range(2):
                    expert(i, b)
            expert(E // 2 - 1, 0)
            expert(E // 2 - 1, 1, last=True)

        block = ctx.enter_context(nc.Block())

        @block.sync
        def _(sp):
            for b in range(2):
                sp.sem_inc(y1_out[b], 16)
            sp.dma_start(cst[:, :], consts).then_inc(c_in, 16)
            sp.dma_start(w_out_s, w_out.rearrange("(c p) n -> p c n", p=P)).then_inc(wo_in, 16)
            sp.dma_start(w_in_s, w_in.rearrange("(c p) n -> p c n", p=P)).then_inc(wi_in, 16)
            x_v = x.rearrange("(p n) d -> p n d", n=N2)

            def load_x(i, b):
                sp.dma_start(xch[:, b], x_v[:, ds(4 * i + 2 * b, 2), :]).then_inc(x_in[b], 16)

            load_x(0, 0)
            load_x(0, 1)
            sp.dma_start(rowix[:, :], row_of).then_inc(c_in, 16)
            sp.dma_start(rb[:, :], bcast(router_b, P)).then_inc(rb_in, 16)
            sp.wait_ge(pad_made, 1)
            sp.dma_start(lists.rearrange("(p e r) w -> p e (r w)", p=P, e=E),
                         bass.AP(padl.tensor, padl.offset,
                                 [list(padl.ap[0]), [0, E], [1, 2 * BLOCKS]])).then_inc(pad_out, 16)

            def store_y(i, b):
                sp.wait_ge(job_act, jobs_even(JOB_S1 + 4 * b + 3) + 4 * i)
                sp.wait_ge(job_dve, jobs_odd(JOB_S1 + 4 * b + 3) + 4 * i)
                sp.dma_start(yd[:, ds(4 * i + 2 * b, 2), :], ych[:, b]).then_inc(y1_out[b], 16)

            STEPS = N2 // 4
            with sp.Fori(0, STEPS - 1) as i:
                for b in range(2):
                    sp.wait_ge(job_ps, JOB_S1 + 8 * i + 4 * b + 4)
                    load_x(i + 1, b)
                    store_y(i, b)
            for b in range(2):
                store_y(STEPS - 1, b)
            for b in range(2):
                sp.wait_ge(y1_out[b], 16 * STEPS + 16)

            def load_yt(g, i, b, first=False):
                if not first:
                    sp.wait_ge(xj_ps, s2_base(g - 2) + 4)
                sp.dma_start(yt[:, b], yd_v[:, ds(2 * g, 2), :]).then_inc(yt_in[b], 16)
                sp.dma_start(m2t[:, b], m2[:, ds(2 * g, 2), :]).then_inc(yt_in[b], 16)

            yd_v = yd.rearrange("(q a) n d -> (a n) q d", a=4)

            def store_h(g, b):
                sp.wait_ge(h_ok, 2 * g + 2)
                sp.dma_start(hd_v[:, ds(2 * g, 2), :], rows[:, b]).then_inc(h_out[b], 16)
                sp.dma_start(acc_v[:, ds(2 * g, 2), :], rows[:, b]).then_inc(h_out[b], 16)

            hd_v = hd[0:S, :].rearrange("(t p) d -> p t d", p=P)
            acc_v = acc[0:S, :].rearrange("(t p) d -> p t d", p=P)
            sp.wait_ge(ab_ps, AB_JOBS)
            load_yt(0, 0, 0, first=True)
            load_yt(1, 0, 1, first=True)
            sp.dma_start(rwv, router_w.rearrange("(c p) e -> p c e", p=P)).then_inc(rb_in, 16)
            sp.dma_start(lng[:, :], bcast(ln_g[0], P)).then_inc(ln_in, 16)
            sp.dma_start(lnb[:, :], bcast(ln_b[0], P)).then_inc(ln_in, 16)
            for b in range(2):
                load_yt(2 + b, 1, b)
                store_h(b, b)
            with sp.Fori(1, GROUPS // 2 - 1) as i:
                for b in range(2):
                    load_yt(2 * i + 2 + b, i + 1, b)
                    store_h(2 * i + b, b)
            for b in range(2):
                store_h(GROUPS - 2 + b, b)

            wg_v = w_gate.rearrange("e (p h c) f -> p e h (c f)", p=P, h=4)
            wu_v = w_up.rearrange("e (p h c) f -> p e h (c f)", p=P, h=4)
            wd_v = w_down.rearrange("e (c p) f -> p e c f", p=P)

            lists_v = lists.rearrange("(p e r) w -> p e (r w)", p=P, e=E)

            def load_entries(e, b):
                sp.dma_start(entry_t[:, b * 2 * BLOCKS:(b + 1) * 2 * BLOCKS].rearrange(
                    "p (o w) -> p o w", o=1), lists_v[:, ds(e, 1), :]).then_inc(entries_in[b], 16)

            def load_expert(e, b):
                for j in range(PIECES):
                    if not is_first(e) or j >= SLOTS:
                        sp.wait_ge(wlo_ok, PIECES * e + j - SLOTS + 1)
                    w, h = (wg_v, wu_v, wd_v)[j // 4], j % 4
                    sp.dma_start(wraw[:, j % SLOTS:j % SLOTS + 1, :], w[:, ds(e, 1), h, :]
                                 ).then_inc(wraw_in[j % SLOTS], 16)
                    if j == 4 and not is_first(e, 2):
                        done = sp.value_load(tstart[0:1, ds(e - 1, 1)], min_val=2, max_val=MAX_TILES)
                        sp.wait_ge(ya_ok, done + 2)
                        sp.wait_ge(yd_ok, done + 2)
                        load_entries(e, b)

            sp.wait_ge(p_ps, GROUPS)
            load_expert(0, 0)
            sp.wait_ge(list_out, 64 * GROUPS)
            load_entries(0, 0)
            load_entries(1, 1)
            sp.wait_ge(tab_ok, 1)
            load_expert(1, 1)
            with sp.Fori(1, E // 2) as i:
                for b in range(2):
                    load_expert(2 * i + b, b)

            total = sp.value_load(tstart[0:1, E:E + 1], min_val=2 * E, max_val=MAX_TILES)
            sp.wait_ge(y_out, total * 16 + 32)
            sp.dma_start(lng2, bcast(ln_g[1], P)).then_inc(ln2_in, 16)
            sp.dma_start(lnb2, bcast(ln_b[1], P)).then_inc(ln2_in, 16)

            def load_fin(t, i, b):
                if not is_first(i):
                    sp.wait_ge(fin_out[b], 16 * i)
                sp.dma_start(fin_r[:, b:b + 1, :], acc_v[:, ds(t, 1), :]).then_inc(fin_in[b], 16)

            for b in range(FB):
                load_fin(b, 0, b)
            with sp.Fori(1, TILES // FB) as i:
                for b in range(FB):
                    load_fin(FB * i + b, i, b)

        @block.tensor
        def _(pe):
            def bank_free(j):
                if j < 8:
                    return
                if j % 2 == 0:
                    pe.wait_ge(job_act, jobs_even(j - 8))
                else:
                    pe.wait_ge(job_dve, jobs_odd(j - 8))

            pe.wait_ge(c_in, 32)
            pe.wait_ge(wo_in, 16)
            j = 0
            for m in range(2):
                for g in range(NG):
                    for h in range(2):
                        bank_free(j)
                        for k in range(2):
                            mm = nc.tensor.matmul(bank[j % 8], cs[:, m, k, :],
                                                  w_out_s[:, 2 * g + k, h * HALF:(h + 1) * HALF],
                                                  start=(k == 0), stop=(k == 1))
                        mm.then_inc(job_ps, 1)
                        j += 1
            for h in range(2):
                bank_free(j)
                for c in range(CH):
                    mm = nc.tensor.matmul(bank[j % 8][0:NG, :], alt[:, c // 2, :],
                                          w_out_s[:, c, h * HALF:(h + 1) * HALF],
                                          start=(c == 0), stop=(c == CH - 1))
                mm.then_inc(job_ps, 1)
                j += 1
            for m in range(2):
                pe.wait_ge(folded_e if m == 0 else folded_o, 3 if m == 0 else 2)
                for g in range(NG):
                    for h in range(2):
                        bank_free(j)
                        for c in range(4):
                            mm = nc.tensor.transpose(bank[j % 8][:, c * P:(c + 1) * P],
                                                     fold[:, m, 4 * h + c, g, :], ident)
                        mm.then_inc(job_ps, 1)
                        j += 1
            for h in range(2):
                bank_free(j)
                for c in range(4):
                    mm = nc.tensor.transpose(bank[j % 8][0:NG, c * P:(c + 1) * P],
                                             midv[:, 4 * h + c, :], ident)
                mm.then_inc(job_ps, 1)
                j += 1
            with pe.Fori(0, N2 // 4) as i:
                for b in range(2):
                    pe.wait_ge(x_in[b], 16 * i + 16)
                    for n in range(2):
                        for h in range(2):
                            jj = 4 * b + 2 * n + h
                            if (JOB_S1 + jj) % 2 == 0:
                                pe.wait_ge(job_act, jobs_even(JOB_S1 + jj - 8) + 4 * i)
                            else:
                                pe.wait_ge(job_dve, jobs_odd(JOB_S1 + jj - 8) + 4 * i)
                            nc.tensor.matmul(bank[(JOB_S1 + jj) % 8], f1,
                                             xch[:, b, n, h * HALF:(h + 1) * HALF],
                                             start=True, stop=True).then_inc(job_ps, 1)
            pe.wait_ge(job_act, jobs_even(JOB_AB - 1))
            pe.wait_ge(job_dve, jobs_odd(JOB_AB - 1))
            j = 0
            for m in range(2):
                for c in range(CH):
                    for h in range(2):
                        if j >= 8:
                            pe.wait_ge(ab_lo, j - 7)
                        for g in range(NG):
                            mm = nc.tensor.matmul(bank[j % 8], foldT[:, m, g, c * P:(c + 1) * P],
                                                  T[:, m, g, h * HALF:(h + 1) * HALF],
                                                  start=(g == 0), stop=(m == 1 and g == NG - 1))
                        if m == 0:
                            mm = nc.tensor.matmul(bank[j % 8], midT[0:NG, c * P:(c + 1) * P],
                                                  T128[0:NG, h * HALF:(h + 1) * HALF],
                                                  start=False, stop=True)
                        mm.then_inc(ab_ps, 1)
                        j += 1
            pe.wait_ge(ab_lo, AB_JOBS)

            def second_stage(g, i, b):
                base_j = s2_base(g)
                pe.wait_ge(yt_in[b], 32 * i + 32)
                for jj in range(4):
                    if not is_first(base_j, 2 - jj):
                        pe.wait_ge(xj_ev, base_j + jj - 1)
                    if jj < 2 and not is_first(g):
                        pe.wait_ge(xl_ev, 4 * g - 2 + jj)
                    elif jj >= 2:
                        pe.wait_ge(xl_ev, 4 * g - 1 + jj)
                    for c in range(2):
                        for q in range(2):
                            lo = (jj % 2) * HALF + c * 256 + q * P
                            cc = 2 * jj + c
                            mm = nc.tensor.matmul(psX[:, lo:lo + P],
                                                  yt[:, b, q, cc * P:(cc + 1) * P],
                                                  m2t[:, b, q, :], start=True, stop=True)
                    mm.then_inc(xj_ps, 1)

            def product(g, m, ps, w, free, done, edge_row=False):
                if not is_first(g):
                    pe.wait_ge(free, g)
                for h in range(2):
                    cols = slice(h * HALF, (h + 1) * HALF)
                    if edge_row:
                        for n, (l, r) in enumerate(PASSES):
                            for c in range(CH):
                                nc.tensor.matmul(ps[:, cols], edge[l][:, c, :], A[r][:, c, cols],
                                                 start=(n == 0 and c == 0), stop=False)
                    for n, (l, r) in enumerate(PASSES):
                        for c in range(CH):
                            mm = nc.tensor.matmul(ps[:, cols], xt[l][:, m, c, :], w[r][:, c, cols],
                                                  start=(n == 0 and c == 0 and not edge_row),
                                                  stop=(n == 2 and c == CH - 1))
                mm.then_inc(done, 1)

            def turn_rows(g, b, base_j):
                for s in range(2):
                    pe.wait_ge(h_ok, 2 * g + 1 + s)
                    for hh in range(2):
                        jj = 2 * s + hh
                        pe.wait_ge(xj_ev, base_j + jj - 1)
                        if jj < 2 and not (isinstance(g, int) and g >= GROUPS - 2):
                            pe.wait_ge(xl_ev, 4 * g + 11 + jj)
                        for c in range(4):
                            lo = (jj % 2) * HALF + c * P
                            cc = 4 * hh + c
                            mm = nc.tensor.transpose(psX[:, lo:lo + P],
                                                     rows[:, b, s, cc * P:(cc + 1) * P], ident)
                        mm.then_inc(xj_ps, 1)
                    pe.wait_ge(xj_ev, base_j + 2 * s + 2)
                    if s == 0 and not is_first(g):
                        pe.wait_ge(sg_ok, g)
                    for c in range(CH):
                        mm = nc.tensor.matmul(psR[:, s * E:(s + 1) * E], hT[:, c, :], rwv[:, c, :],
                                              start=(c == 0), stop=(c == CH - 1))
                    mm.then_inc(lg_ps, 1)

            def ranks(g):
                pe.wait_ge(m_ok, g + 1)
                r0, r1, r2 = (psR[:, HALF + i * E:HALF + (i + 1) * E] for i in range(3))
                nc.tensor.matmul(r0, before, msum[:, 0], start=True, stop=True)
                nc.tensor.matmul(r1, before, msum[:, 1], start=True, stop=False)
                nc.tensor.matmul(r1, ones, msum[:, 0], start=False, stop=True)
                nc.tensor.matmul(r2, ones, msum[:, 0], start=True, stop=False)
                nc.tensor.matmul(r2, ones, msum[:, 1], start=False, stop=True).then_inc(rk_ps, 1)

            def group(g, i, b):
                pe.wait_ge(xj_ev, s2_base(g) + 4)
                pe.wait_ge(xl_ev, 4 * g + 4)
                if is_first(g):
                    pe.wait_ge(edge_ok, 2)
                product(g, 1, psQ, B, q_ev, q_ps, edge_row=is_first(g))
                if not is_first(g, 2):
                    ranks(g - 2)
                product(g, 0, psP, A, p_ev, p_ps)
                if not (isinstance(g, int) and g == GROUPS - 1):
                    second_stage(g + 1, i if b == 0 else i + 1, 1 - b)
                if not is_first(g):
                    turn_rows(g - 1, 1 - b, tr_base(g))

            second_stage(0, 0, 0)
            pe.wait_ge(rb_in, 32)
            group(0, 0, 0)
            group(1, 0, 1)
            with pe.Fori(1, GROUPS // 2 - 1) as i:
                for b in range(2):
                    group(2 * i + b, i, b)
            for b in range(2):
                group(GROUPS - 2 + b, GROUPS // 2 - 1, b)
            ranks(GROUPS - 2)
            turn_rows(GROUPS - 1, 1, tr_base(GROUPS))
            ranks(GROUPS - 1)

            pe.sem_inc(x1_ps, 1)
            pe.sem_inc(y1_ps, 1)
            pe.wait_ge(p_ev, GROUPS)
            pe.wait_ge(q_ev, GROUPS)
            pe.wait_ge(xj_ev, tr_base(GROUPS) + 4)
            pe.wait_ge(tab_ok, 1)

            def turn_x(half, done):
                for c in range(4):
                    mm = nc.tensor.transpose(psX0[:, c * P:(c + 1) * P] if half == 0 else
                                             psX1[:, c * P:(c + 1) * P],
                                             xrow_s[:, 4 * half + c, :], ident)
                mm.then_inc(done, 1)

            def turn_hidden(half, done):
                for c in range(2 * half, 2 * half + 2):
                    mm = nc.tensor.transpose(psH[half][:, (c % 2) * P:(c % 2 + 1) * P],
                                             hid[:, c * P:(c + 1) * P], ident)
                mm.then_inc(done, 1)

            def up_or_gate(ps, b, m, lo, hi):
                for n, (l, r) in enumerate(PASSES):
                    for c in range(CH):
                        mm = nc.tensor.matmul(ps, mxT[l][:, c, :],
                                              wgu[b][r][:, m, c, lo:hi],
                                              start=(n == 0 and c == 0), stop=(n == 2 and c == CH - 1))
                return mm

            def tile(t, e, b, lo, kind, last):
                pe.wait_ge(xh_ev, 2 * t + 2)
                pe.wait_ge(xlo_ev, 2 * t + 2)
                pe.wait_ge(wlo_ok, PIECES * e + 4)
                up_or_gate(psG, b, 0, 0, F).then_inc(g_ps, 1)
                pe.wait_ge(wlo_ok, PIECES * e + GU_PIECES)
                up_or_gate(psU[0], b, 1, 0, F // 2).then_inc(ua_ps, 1)
                up_or_gate(psU[1], b, 1, F // 2, F).then_inc(ub_ps, 1)
                pe.wait_ge(hida_ok, t + 1)
                turn_hidden(0, h0_ps)
                pe.wait_ge(xrow_in, 16 * t + 32)
                turn_x(0, x0_ps)
                pe.wait_ge(hidb_ok, t + 1)
                turn_hidden(1, h1_ps)
                turn_x(1, x1_ps)
                pe.wait_ge(wlo_ok, PIECES * e + PIECES)
                pe.wait_ge(ya_ok, t + 2)
                pe.wait_ge(yd_ok, t + 2)
                for h in range(2):
                    cols = slice(h * HALF, (h + 1) * HALF)
                    for n, (l, r) in enumerate(PASSES):
                        if h == 0 and n != 1:
                            pe.wait_ge(hh_ev if n == 0 else hl_ev, 2 * t + 2)
                        for c in range(FC):
                            mm = nc.tensor.matmul(psY[:, cols], hidT[l][:, c, :],
                                                  wd[r][:, c, cols],
                                                  start=(n == 0 and c == 0),
                                                  stop=(n == 2 and c == FC - 1))
                    mm.then_inc(y0_ps if h == 0 else y1_ps, 1)

            pe.wait_ge(xrow_in, 16)
            turn_x(0, x0_ps)
            turn_x(1, x1_ps)
            expert_tiles(pe, tile)

        @block.scalar
        def _(act):
            def empty(dst, src, j):
                act.wait_ge(job_ps, j + 1)
                nc.scalar.copy(dst, src).then_inc(job_act, 1)

            for j in range(0, JOB_S1, 2):
                dst = phase0_dst(j)
                empty(dst, bank[j % 8][0:dst.shape[0], :], j)
            with act.Fori(0, N2 // 4) as i:
                for b in range(2):
                    for jj in range(4 * b, 4 * b + 4):
                        if (JOB_S1 + jj) % 2 == 0:
                            if jj % 4 < 2:
                                act.wait_ge(y1_out[b], 16 * i + 16)
                            act.wait_ge(job_ps, JOB_S1 + 8 * i + jj + 1)
                            n, h = (jj % 4) // 2, jj % 2
                            nc.scalar.copy(ych[:, b, n, h * HALF:(h + 1) * HALF],
                                           bank[(JOB_S1 + jj) % 8]).then_inc(job_act, 1)
            act.wait_ge(job_ps, JOB_AB)
            for j in range(AB_JOBS):
                act.wait_ge(ab_ps, j + 1)
                nc.scalar.copy(ab_dst(j, 0), bank[j % 8]).then_inc(ab_hi, 1)

            def empty_s2(g):
                for jj in range(4):
                    act.wait_ge(xj_ps, s2_base(g) + jj + 1)
                    for m in range(2):
                        a = nc.scalar.copy(s2_dst(0, m, jj), s2_src(jj)[:, :, :, m, :])
                    a.then_inc(xj_ev, 1)

            def empty_turn(base_j, g):
                for jj in range(4):
                    act.wait_ge(xj_ps, base_j + jj + 1)
                    if jj == 2 or (jj == 0 and not is_first(g)):
                        act.wait_ge(lg_ps, 2 * g + jj // 2)
                    hh = jj % 2
                    nc.scalar.copy(hT[:, 4 * hh:4 * hh + 4, :].rearrange("p c n -> p (c n)"),
                                   psX[:, (jj % 2) * HALF:(jj % 2 + 1) * HALF]).then_inc(xj_ev, 1)

            def scores(g):
                act.wait_ge(lg_ps, 2 * g + 2)
                if not is_first(g):
                    act.wait_ge(dest_ok, g)
                nc.scalar.activation(sc.rearrange("p s e -> p (s e)"), psR[:, 0:2 * E],
                                     ACT.Sigmoid).then_inc(sg_ok, 1)

            def group(g, b, last=False):
                act.wait_ge(q_ps, g + 1)
                if not is_first(g):
                    act.wait_ge(q_used, g)
                nc.scalar.copy(qs, psQ[:, :]).then_inc(q_ev, 1)
                if not last:
                    empty_s2(g + 1)
                if not is_first(g):
                    empty_turn(tr_base(g), g - 1)
                    scores(g - 1)
                act.wait_ge(var_ok, g + 1)
                nc.scalar.activation(lnstd[:, 0:2], lnmv[:, 0:2, 1], ACT.Sqrt, bias=eps_c).then_inc(std_ok, 1)
                act.wait_ge(nrm_ok, g + 1)
                for s in range(2):
                    nc.scalar.activation(rows[:, b, s, :], rows[:, b, s, :], ACT.Identity,
                                         bias=lnsh[:, s:s + 1], scale=lnrs[:, s:s + 1]
                                         ).then_inc(hn_ok, 1)

            empty_s2(0)
            act.wait_ge(xj_ev, 4)
            act.wait_ge(edge_zero, 2)
            nc.scalar.copy(edge[0][:, :, 0], xt[0][:, 1, :, 0].bitcast(F32)).then_inc(edge_read, 1)
            act.wait_ge(edge_read, 1)
            act.wait_ge(xl_ev, 4)
            nc.scalar.copy(xt[0][:, 1, :, 0], zer[:, 0:CH]).then_inc(edge_ok, 1)
            group(0, 0)
            group(1, 1)
            with act.Fori(1, GROUPS // 2 - 1) as i:
                for b in range(2):
                    group(2 * i + b, b)
            group(GROUPS - 2, 0)
            group(GROUPS - 1, 1, last=True)
            empty_turn(tr_base(GROUPS), GROUPS - 1)
            scores(GROUPS - 1)

            def split(e, j, dst):
                act.wait_ge(wraw_in[j % SLOTS], 16 * (PIECES // SLOTS * e + j // SLOTS + 1))
                nc.scalar.copy(dst, wraw[:, j % SLOTS, :]).then_inc(whi_ok, 1)

            def split_gu(e, b, js):
                for j in js:
                    split(e, j, gu_piece(b, 0, j))

            def turn_x(t):
                for half, ps, done in ((0, psX0, x0_ps), (1, psX1, x1_ps)):
                    act.wait_ge(done, t + 1 + half)
                    nc.scalar.copy(mxT[0][:, 4 * half:4 * half + 4, :].rearrange("p c n -> p (c n)"),
                                   ps).then_inc(xh_ev, 1)

            def tile(t, e, b, lo, kind, last):
                if kind == 0:
                    act.wait_ge(y1_ps, lo + 1)
                    for c in range(FC):
                        split(e, GU_PIECES + c, wd[0][:, c, :])
                act.wait_ge(g_ps, t + 1)
                nc.scalar.activation(sgate, psG, ACT.Silu).then_inc(silu_ok, 1)
                if kind < 2 and not last:
                    split_gu(e + 1, 1 - b, range(4 * kind, 4 * kind + 2))
                for half, done in ((0, h0_ps), (1, h1_ps)):
                    act.wait_ge(done, t + 1)
                    nc.scalar.copy(hidT[0][:, 2 * half:2 * half + 2, :].rearrange("p c n -> p (c n)"),
                                   psH[half]).then_inc(hh_ev, 1)
                turn_x(t + 1)
                if kind < 2 and not last:
                    split_gu(e + 1, 1 - b, range(4 * kind + 2, 4 * kind + 4))
                act.wait_ge(y0_ps, t + 1)
                entries_there(act, e, b, kind)
                act.wait_ge(y_out, 16 * t + 32)
                nc.scalar.mul(yrow[:, 0:HALF], psY[:, 0:HALF], gate_of(t, b, lo)).then_inc(ya_ok, 1)

            act.wait_ge(p_ps, GROUPS)
            split_gu(0, 0, range(GU_PIECES))
            act.wait_ge(tab_ok, 1)
            turn_x(0)
            expert_tiles(act, tile)

            def deviation(t, b):
                act.wait_ge(fn_ok, t + 1)
                nc.scalar.activation(lnstd[:, b:b + 1], lnmv[:, b, 1:2], ACT.Sqrt,
                                     bias=eps2_c).then_inc(fstd_ok, 1)

            def normalize(t, b):
                act.wait_ge(fnn_ok, t + 1)
                nc.scalar.activation(fin_r[:, b, :], fin_r[:, b, :], ACT.Identity,
                                     bias=lnsh[:, b:b + 1], scale=lnrs[:, b:b + 1]).then_inc(fg_ok, 1)

            with act.Fori(0, TILES // FB) as i:
                for b in range(FB):
                    deviation(FB * i + b, b)
                    normalize(FB * i + b, b)

        @block.vector
        def _(dve):
            step = Steps(dve, dve_step)
            link = step.link
            nc.vector.memset(eps_c, EPS)
            nc.vector.memset(eps2_c, EPS / ALPHA ** 2)
            nc.vector.memset(base[:, :], 0.0)
            nc.vector.memset(zer, 0.0).then_inc(made, 1)
            dve.wait_ge(c_in, 32)
            dve.wait_ge(wi_in, 16)
            nc.vector.tensor_tensor(foldq[:, 0, :, 1:P], w_in_g[:, :, 1:P],
                                    w_in_g[:, :, GROUP_DIM - 1:P:-1], ALU.add).then_inc(folded_e, 1)
            nc.vector.tensor_copy(foldq[:, 0, :, 0:1], w_in_g[:, :, 0:1]).then_inc(folded_e, 1)
            nc.vector.tensor_copy(midv.rearrange("p c g -> p (c g)").rearrange("p (q o) -> p q o", o=1),
                                  w_in_g[:, :, P:P + 1]).then_inc(folded_e, 1)

            def empty(dst, src, j):
                dve.wait_ge(job_ps, j + 1)
                nc.vector.tensor_copy(dst, src).then_inc(job_dve, 1)

            for j in range(1, JOB_S1, 2):
                dst = phase0_dst(j)
                empty(dst, bank[j % 8][0:dst.shape[0], :], j)
            with dve.Fori(0, N2 // 4) as i:
                for b in range(2):
                    for jj in range(4 * b, 4 * b + 4):
                        if (JOB_S1 + jj) % 2 == 1:
                            if jj % 4 < 2:
                                dve.wait_ge(y1_out[b], 16 * i + 16)
                            dve.wait_ge(job_ps, JOB_S1 + 8 * i + jj + 1)
                            n, h = (jj % 4) // 2, jj % 2
                            nc.vector.tensor_copy(ych[:, b, n, h * HALF:(h + 1) * HALF],
                                                  bank[(JOB_S1 + jj) % 8]).then_inc(job_dve, 1)
            for b in range(2):
                dve.wait_ge(y1_out[b], 16 * (N2 // 4) + 16)
            for j in range(AB_JOBS):
                dve.wait_ge(ab_hi, j + 1)
                nc.vector.tensor_tensor(ab_dst(j, 1), bank[j % 8], ab_dst(j, 0).bitcast(F32),
                                        ALU.subtract).then_inc(ab_lo, 1)
            dve.wait_ge(ab_ps, AB_JOBS)
            nc.vector.memset(edge[0][:, :, :].bitcast(F32), 0.0).then_inc(edge_zero, 1)
            nc.vector.memset(edge[1][:, :, :].bitcast(F32), 0.0).then_inc(edge_zero, 1)

            def empty_s2(g):
                for jj in range(4):
                    dve.wait_ge(xj_ev, s2_base(g) + jj + 1)
                    for m in range(2):
                        a = nc.vector.tensor_tensor(s2_dst(1, m, jj), s2_src(jj)[:, :, :, m, :],
                                                    s2_dst(0, m, jj).bitcast(F32), ALU.subtract)
                    a.then_inc(xl_ev, 1)

            def statistics(src, s):
                nc.vector.bn_stats(lnst[:, s, 0, :], src[:, 0:HALF])
                link(nc.vector.bn_stats(lnst[:, s, 1, :], src[:, HALF:D]))
                dve.sem_inc(dve_gate, 1)
                return nc.vector.bn_aggr(lnmv[:, s, :], lnst[:, s].rearrange("p h w -> p (h w)"))

            def rows_ready(g, b, i):
                dve.wait_ge(p_ps, g + 1)
                dve.wait_ge(rows_in[b], 32 * i + 32)
                for s in range(2):
                    a = nc.vector.scalar_tensor_tensor(rows[:, b, s, :], rows[:, b, s, :], ALPHA,
                                                       psP[:, :], ALU.mult, ALU.add)
                a.then_inc(p_ev, 1)
                dve.wait_ge(p_ev, g + 1)
                dve.wait_ge(q_ev, g + 1)
                nc.vector.tensor_tensor(rows[:, b, 0, :], rows[:, b, 0, :], qs, ALU.add)
                nc.vector.tensor_tensor(rows[:, b, 1, :], rows[:, b, 1, :], qs,
                                        ALU.subtract).then_inc(q_used, 1)
                dve.wait_ge(q_used, g + 1)
                for s in range(2):
                    a = statistics(rows[:, b, s, :], s)
                a.then_inc(var_ok, 1)
                dve.wait_ge(std_ok, g + 1)
                link(nc.vector.reciprocal(lnrs[:, 0:2], lnstd[:, 0:2]))
                nc.vector.scalar_tensor_tensor(lnsh[:, 0:2], lnmv[:, 0:2, 0], -1.0, lnrs[:, 0:2],
                                               ALU.mult, ALU.mult).then_inc(nrm_ok, 1)
                for s in range(2):
                    dve.wait_ge(hn_ok, 2 * g + s + 1)
                    nc.vector.tensor_tensor(rows[:, b, s, :], rows[:, b, s, :], lng[:, :],
                                            ALU.mult).then_inc(hg_ok, 1)

            def grp(v):
                return v.rearrange("p s (g j) -> p s g j", j=EPG)

            first_g = bass.AP(first.tensor, first.offset,
                              [list(first.ap[0]), [0, 2], [EPG, EG], [1, EPG]])

            def choose(g):
                dve.wait_ge(sg_ok, g + 1)
                link(nc.vector.tensor_tensor(sel, sc, rep_mid(rb[:, :], 2), ALU.add))
                cur = sel
                for k in range(2):
                    link(nc.vector.tensor_reduce(top[k], grp(cur), AX, ALU.max))
                    link(nc.vector.tensor_tensor(grp(eq), grp(cur), rep_last(top[k], EPG), ALU.is_equal))
                    link(nc.vector.tensor_tensor(eq, eq, rep_mid(first, 2), ALU.mult))
                    link(nc.vector.tensor_reduce(kmax, grp(eq), AX, ALU.max))
                    link(nc.vector.tensor_tensor(grp(onehot[k]), first_g, rep_last(kmax, EPG),
                                                 ALU.is_equal))
                    if k == 0:
                        link(nc.vector.scalar_tensor_tensor(
                            sel2.rearrange("p s e -> p (s e)"), onehot[0].rearrange("p s e -> p (s e)"),
                            -1e30, sel.rearrange("p s e -> p (s e)"), ALU.mult, ALU.add))
                        cur = sel2
                link(nc.vector.tensor_tensor(gsum, top[0], top[1], ALU.add))
                link(nc.vector.tensor_reduce(gmax, gsum, AX, ALU.max))
                link(nc.vector.tensor_tensor(geq, gsum, rep_last(gmax, EG), ALU.is_equal))
                link(nc.vector.tensor_tensor(geq, geq, rep_mid(firstg, 2), ALU.mult))
                link(nc.vector.tensor_reduce(gmax, geq, AX, ALU.max))
                link(nc.vector.tensor_tensor(geq, rep_mid(firstg, 2), rep_last(gmax, EG), ALU.is_equal))
                for k in range(2):
                    link(nc.vector.tensor_tensor(grp(onehot[k]), grp(onehot[k]), rep_last(geq, EPG),
                                                 ALU.mult))
                nc.vector.tensor_tensor(msum, onehot[0], onehot[1], ALU.add).then_inc(m_ok, 1)

            def place(g):
                for k in range(2):
                    link(nc.vector.tensor_tensor(eq, sc, onehot[k], ALU.mult))
                    link(nc.vector.tensor_reduce(gk[:, :, k], eq, AX, ALU.add))
                link(nc.vector.tensor_tensor(gden, gk[:, :, 0], gk[:, :, 1], ALU.add))
                link(nc.vector.tensor_scalar(gden, gden, ALPHA, None, ALU.mult))
                link(nc.vector.reciprocal(gden, gden))
                if not is_first(g):
                    dve.wait_ge(list_out, 64 * g)
                nc.vector.tensor_tensor(paygv[:, :, :, 1].bitcast(F32), gk, rep_last(gden, 2),
                                        ALU.mult).then_inc(gate_ok, 1)
                dve.wait_ge(rk_ps, g + 1)
                link(nc.vector.tensor_tensor(
                    rank, psR[:, HALF:HALF + 2 * E].rearrange("p (s e) -> p s e", s=2),
                    rep_mid(base[:, :], 2), ALU.add))
                link(nc.vector.tensor_tensor(base[:, :], base[:, :],
                                             psR[:, HALF + 2 * E:HALF + 3 * E], ALU.add))
                link(nc.vector.tensor_tensor(rank, rank, rep_mid(ebase, 2), ALU.add))
                for k in range(2):
                    link(nc.vector.tensor_tensor(eq, rank, onehot[k], ALU.mult))
                    link(nc.vector.tensor_reduce(
                        destf[:, :, k], eq, AX, ALU.add))
                link(nc.vector.tensor_copy(dint, destf.rearrange("p s k -> p (s k)")))
                link(nc.vector.tensor_scalar(dlane, dint, P - 1, ENTRY_BITS, ALU.bitwise_and,
                                             ALU.logical_shift_left))
                link(nc.vector.tensor_scalar(dint, dint, LANE_BITS, None, ALU.logical_shift_right))
                nc.vector.tensor_tensor(desti[:, :], dint, dlane, ALU.bitwise_or).then_inc(dest_ok, 1)
                dve.wait_ge(dest_ok, g + 1)

            ROWS_STEPS, ROUTE_STEPS = 3, 37

            def group(g, b, i):
                if not is_first(g, 2):
                    step.begin(2 * ROWS_STEPS + (ROUTE_STEPS + ROWS_STEPS) * (g - 2))
                    choose(g - 2)
                    place(g - 2)
                    assert step.k == ROUTE_STEPS, step.k
                if not (isinstance(g, int) and g == GROUPS - 1):
                    empty_s2(g + 1)
                rows_ready(g, b, i)
                if not is_first(g, 2):
                    assert step.k == ROUTE_STEPS + ROWS_STEPS

            empty_s2(0)
            dve.wait_ge(edge_read, 1)
            dve.wait_ge(edge_zero, 2)
            dve.wait_ge(xl_ev, 4)
            nc.vector.tensor_copy(edge[1][:, :, 0], xt[1][:, 1, :, 0].bitcast(F32)).then_inc(edge_read, 1)
            dve.wait_ge(edge_read, 2)
            nc.vector.tensor_copy(xt[1][:, 1, :, 0], zer[:, 0:CH]).then_inc(edge_ok, 1)
            dve.wait_ge(rb_in, 32)
            dve.wait_ge(ln_in, 32)
            group(0, 0, 0)
            group(1, 1, 0)
            with dve.Fori(1, GROUPS // 2 - 1) as i:
                for b in range(2):
                    group(2 * i + b, b, i)
            for b in range(2):
                group(GROUPS - 2 + b, b, GROUPS // 2 - 1)
            for g in (GROUPS - 2, GROUPS - 1):
                choose(g)
                place(g)
            link(nc.vector.tensor_tensor(
                cmp, rep_last(base[0:1, :], S // P), rep_mid(steps[0:1, :], E), ALU.is_gt))
            link(nc.vector.tensor_reduce(ntile[0:1, :], cmp, AX, ALU.add))
            link(nc.vector.tensor_scalar_max(ntile[0:1, :], ntile[0:1, :], 2.0))
            nc.vector.memset(cum[0:1, 0:1], 0.0)
            link(nc.vector.tensor_tensor_scan(cum[0:1, 1:E + 1], ntile[0:1, :], zer[0:1, 0:E], 0.0,
                                              ALU.add, ALU.add))
            nc.vector.tensor_copy(tstart[0:1, :], cum[0:1, :]).then_inc(tab_ok, 1)
            dve.wait_ge(tab_ok, 1)

            def split(e, j, hi, lo):
                dve.wait_ge(whi_ok, PIECES * e + j + 1)
                nc.vector.tensor_tensor(lo, wraw[:, j % SLOTS, :], hi.bitcast(F32),
                                        ALU.subtract).then_inc(wlo_ok, 1)

            def split_gu(e, b, js):
                for j in js:
                    split(e, j, gu_piece(b, 0, j), gu_piece(b, 1, j))

            def turn_x(t):
                for half, ps in ((0, psX0), (1, psX1)):
                    hi, lo = (mxT[n][:, 4 * half:4 * half + 4, :].rearrange("p c n -> p (c n)")
                              for n in range(2))
                    dve.wait_ge(xh_ev, 2 * t + half + 1)
                    nc.vector.tensor_tensor(lo, ps, hi.bitcast(F32), ALU.subtract).then_inc(xlo_ev, 1)

            def tile(t, e, b, lo_t, kind, last):
                if kind == 0:
                    for c in range(FC):
                        split(e, GU_PIECES + c, wd[0][:, c, :], wd[1][:, c, :])
                if kind < 2 and not last:
                    split_gu(e + 1, 1 - b, range(4 * kind, 4 * kind + 2))
                for half, done, ok in ((0, ua_ps, hida_ok), (1, ub_ps, hidb_ok)):
                    cols = slice(half * F // 2, (half + 1) * F // 2)
                    dve.wait_ge(done, t + 1)
                    if half == 0:
                        dve.wait_ge(silu_ok, t + 1)
                    nc.vector.tensor_tensor(hid[:, cols], sgate[:, cols], psU[half],
                                            ALU.mult).then_inc(ok, 1)
                for half in range(2):
                    hi, lo = (hidT[n][:, 2 * half:2 * half + 2, :].rearrange("p c n -> p (c n)")
                              for n in range(2))
                    dve.wait_ge(hh_ev, 2 * t + half + 1)
                    nc.vector.tensor_tensor(lo, psH[half],
                                            hi.bitcast(F32), ALU.subtract).then_inc(hl_ev, 1)
                turn_x(t + 1)
                if kind < 2 and not last:
                    split_gu(e + 1, 1 - b, range(4 * kind + 2, 4 * kind + 4))
                dve.wait_ge(y1_ps, t + 2)
                entries_there(dve, e, b, kind)
                dve.wait_ge(y_out, 16 * t + 32)
                nc.vector.tensor_scalar(yrow[:, HALF:D], psY[:, HALF:D], gate_of(t, b, lo_t), None,
                                        ALU.mult).then_inc(yd_ok, 1)

            split_gu(0, 0, range(GU_PIECES))
            turn_x(0)
            expert_tiles(dve, tile)

            dve.wait_ge(ln2_in, 32)

            def invert(t, b):
                dve.wait_ge(fstd_ok, t + 1)
                link(nc.vector.reciprocal(lnrs[:, b:b + 1], lnstd[:, b:b + 1]))
                nc.vector.scalar_tensor_tensor(lnsh[:, b:b + 1], lnmv[:, b, 0:1], -1.0,
                                               lnrs[:, b:b + 1], ALU.mult, ALU.mult).then_inc(fnn_ok, 1)

            def normal(t, i, b):
                dve.wait_ge(fin_in[b], 16 * i + 16)
                statistics(fin_r[:, b, :], b).then_inc(fn_ok, 1)

            def gain(t, b):
                dve.wait_ge(fg_ok, t + 1)
                nc.vector.tensor_tensor(fin_r[:, b, :], fin_r[:, b, :], lng2,
                                        ALU.mult).then_inc(fb_ok, 1)

            def fin(t, i, b):
                step.begin(start + 2 * t if is_first(t) else start + 2 * t - 1)
                normal(t, i, b)
                if not is_first(t):
                    invert(t - 1, (b - 1) % FB)
                    gain(t - 1, (b - 1) % FB)

            start = step.start + step.k
            for b in range(FB):
                fin(b, 0, b)
            with dve.Fori(1, TILES // FB) as i:
                for b in range(FB):
                    fin(FB * i + b, i, b)
            step.begin(start + 2 * TILES - 1)
            invert(TILES - 1, FB - 1)
            gain(TILES - 1, FB - 1)

        @block.gpsimd
        def _(pool):
            nc.gpsimd.iota(padl.rearrange("p (r w) -> p r w", w=2), [[0, BLOCKS], [0, 2]], base=S,
                           channel_multiplier=1).then_inc(pad_made, 1)
            nc.gpsimd.iota(pay[:, :], [[P, TILES]], base=0, channel_multiplier=1).then_inc(pay_made, 1)
            pool.wait_ge(wi_in, 16)
            nc.gpsimd.memset(foldq[:, 1, :, 0:1], 0.0).then_inc(folded_o, 1)
            nc.gpsimd.tensor_tensor(foldq[:, 1, :, 1:P], w_in_g[:, :, 1:P],
                                    w_in_g[:, :, GROUP_DIM - 1:P:-1], ALU.subtract).then_inc(folded_o, 1)

            def fetch(g, i, b):
                if not is_first(g, 2):
                    pool.wait_ge(xj_ps, tr_base(g - 1) + 4)
                    pool.wait_ge(h_out[b], 32 * i)
                nc.gpsimd.tensor_copy(rowg[:, 2 * b:2 * b + 2], rowix[:, ds(2 * g, 2)]
                                      ).then_inc(rowg_ok, 1)
                own_wait(pool, rowg_ok, g + 1, pool_gate)
                for s in range(2):
                    pool.indirect_dma_start(
                        rows[:, b, s, :], None, x,
                        bass.IndirectOffsetOnAxis(ap=rowg[:, 2 * b + s:2 * b + s + 1], axis=0)
                    ).then_inc(rows_in[b], 16)

            def list_tokens(g):
                if not is_first(g):
                    pool.wait_ge(list_out, 64 * g)
                nc.gpsimd.tensor_copy(paygv[:, :, :, 0], rep_last(pay[:, ds(2 * g, 2)], 2)
                                      ).then_inc(payg_ok, 1)
                pool.wait_ge(payg_ok, g + 1)
                pool.wait_ge(gate_ok, g + 1)
                own_wait(pool, dest_ok, g + 1, pool_gate)
                for s in range(2):
                    for k in range(2):
                        pool.indirect_dma_start(
                            lists, bass.IndirectOffsetOnAxis(ap=desti[:, 2 * s + k:2 * s + k + 1], axis=0),
                            payg[:, 4 * s + 2 * k:4 * s + 2 * k + 2], None).then_inc(list_out, 16)

            def shift(g, b):
                for s in range(2):
                    pool.wait_ge(hg_ok, 2 * g + s + 1)
                    nc.gpsimd.tensor_tensor(rows[:, b, s, :], rows[:, b, s, :], lnb[:, :],
                                            ALU.add).then_inc(h_ok, 1)

            def group(g, b, i):
                fetch(g, i, b)
                if not is_first(g, 2):
                    list_tokens(g - 2)
                shift(g, b)

            pool.wait_ge(c_in, 32)
            pool.wait_ge(pay_made, 1)
            pool.wait_ge(ab_ps, AB_JOBS)
            pool.wait_ge(ln_in, 32)
            pool.wait_ge(pad_out, 16)
            group(0, 0, 0)
            group(1, 1, 0)
            with pool.Fori(1, GROUPS // 2 - 1) as i:
                for b in range(2):
                    group(2 * i + b, b, i)
            for b in range(2):
                group(GROUPS - 2 + b, b, GROUPS // 2 - 1)
            list_tokens(GROUPS - 2)
            list_tokens(GROUPS - 1)

            pool.wait_ge(p_ps, GROUPS)
            for b in range(2):
                pool.wait_ge(h_out[b], 32 * (GROUPS // 2))
            pool.wait_ge(tab_ok, 1)
            nc.gpsimd.iota(sx[:, :], [[0, 1]], base=S, channel_multiplier=1).then_inc(sx_ok, 1)
            nc.gpsimd.iota(sxn[:, :], [[0, 1]], base=S, channel_multiplier=1).then_inc(sx_ok, 1)
            nc.gpsimd.memset(yrow[:, 0:HALF], 0.0).then_inc(ya_ok, 2)
            nc.gpsimd.memset(yrow[:, HALF:D], 0.0).then_inc(yd_ok, 2)
            pool.wait_ge(ya_ok, 2)
            pool.wait_ge(yd_ok, 2)
            pool.dma_start(acc[S:S + P, :], yrow[:, :]).then_inc(spare_out, 16)
            pool.dma_start(hd[S:S + P, :], yrow[:, :]).then_inc(spare_out, 16)
            pool.wait_ge(spare_out, 32)

            def gather(t):
                own_wait(pool, x1_ps, t + 1, pool_gate)
                pool.indirect_dma_start(xrow, None, hd, bass.IndirectOffsetOnAxis(ap=ixg[:, 0:1], axis=0)
                                        ).then_inc(xrow_in, 16)

            def scatter(t):
                pool.wait_ge(ya_ok, t + 1)
                own_wait(pool, yd_ok, t + 1, pool_gate)
                pool.wait_ge(sx_ok, 2)
                pool.indirect_dma_start(acc, bass.IndirectOffsetOnAxis(ap=sx[:, 0:1], axis=0),
                                        yrow, None, compute_op=ALU.add).then_inc(y_out, 16)
                own_wait(pool, y_out, 16 * t + 16, pool_gate)
                nc.gpsimd.tensor_copy(sx[:, :], sxn[:, :]).then_inc(sx_ok, 1)
                own_wait(pool, sx_ok, 2 * t + 3, pool_gate)

            def tile(t, e, b, lo, kind, last):
                entries_there(pool, e, b, kind)
                own_wait(pool, x1_ps, t + 1, pool_gate)
                nc.gpsimd.tensor_copy(ixg[:, :], entries[:, b, ds(block_of(t, lo), 1), 0]
                                      ).then_inc(ixg_ok, 1)
                own_wait(pool, ixg_ok, t + 1, pool_gate)
                gather(t)
                scatter(t)
                nc.gpsimd.tensor_copy(sxn[:, :], ixg[:, :]).then_inc(sx_ok, 1)
                own_wait(pool, sx_ok, 2 * t + 4, pool_gate)

            expert_tiles(pool, tile)
            total = pool.value_load(tstart[0:1, E:E + 1], min_val=2 * E, max_val=MAX_TILES)
            gather(total)
            scatter(total)
            pool.wait_ge(ya_ok, total + 2)
            own_wait(pool, yd_ok, total + 2, pool_gate)
            pool.indirect_dma_start(acc, bass.IndirectOffsetOnAxis(ap=sx[:, 0:1], axis=0),
                                    yrow, None, compute_op=ALU.add).then_inc(y_out, 16)

            pool.wait_ge(ln2_in, 32)

            def fin(t, i, b):
                pool.wait_ge(fb_ok, t + 1)
                nc.gpsimd.tensor_tensor(fin_r[:, b, :], fin_r[:, b, :], lnb2,
                                        ALU.add).then_inc(fh_ok, 1)
                if not is_first(i):
                    own_wait(pool, fin_out[b], 16 * i, pool_gate)
                nc.gpsimd.tensor_copy(rowg[:, b:b + 1], rowix[:, ds(t, 1)]).then_inc(rowg_ok, 1)
                pool.wait_ge(fh_ok, t + 1)
                own_wait(pool, rowg_ok, GROUPS + t + 1, pool_gate)
                pool.indirect_dma_start(
                    out, bass.IndirectOffsetOnAxis(ap=rowg[:, b:b + 1], axis=0),
                    fin_r[:, b, :], None).then_inc(fin_out[b], 16)

            for b in range(FB):
                fin(b, 0, b)
            with pool.Fori(1, TILES // FB) as i:
                for b in range(FB):
                    fin(FB * i + b, i, b)
            for b in range(FB):
                pool.wait_ge(fin_out[b], 16 * (TILES // FB))


_INS = ["x", "fourier_w_in", "fourier_w_out", "router_w", "router_b",
        "expert_w_gate", "expert_w_up", "expert_w_down", "ln_g", "ln_b"]


def kernel(**inputs):
    import concourse.bacc as bacc
    from concourse.bass_utils import run_bass_kernel_spmd

    nc = bacc.Bacc("TRN2", target_bir_lowering=False, num_devices=1)
    arrays, ap = {}, {}

    def declare(name, a):
        arrays[name] = a
        ap[name] = nc.dram_tensor(name, a.shape, mybir.dt.from_np(a.dtype), kind="ExternalInput").ap()

    for name in _INS:
        declare(name, np.ascontiguousarray(inputs[name]))
    packed, const_at, m2, row_of = shape_constants()
    declare("consts", packed)
    declare("second_stage", m2)
    declare("row_of", row_of)
    out = nc.dram_tensor("out", (1, S, D), F32, kind="ExternalOutput").ap()
    trunk_kernel(nc, ap["x"][0], ap["fourier_w_in"][0], ap["fourier_w_out"][0], ap["router_w"],
                 ap["router_b"], ap["expert_w_gate"][0], ap["expert_w_up"][0],
                 ap["expert_w_down"][0], ap["ln_g"][0], ap["ln_b"][0],
                 ap["consts"], const_at, ap["second_stage"], ap["row_of"], out[0])
    r = run_bass_kernel_spmd(nc, [arrays], core_ids=[0])
    return r.results[0]["out"]
```

```python
from contextlib import ExitStack

import numpy as np

import concourse.bass as bass
from concourse import mybir


P = 128
S, D = 4096, 1024
N2 = S // P
GROUP_DIM = 256
NG = D // GROUP_DIM
CH = D // P
HALF = 512
E, EG, EPG = 32, 4, 8
F = 512
FC = F // P
PAIRS = P // 2
GROUPS = PAIRS // 4
TILES = S // P
RANKS = S
BLOCKS = RANKS // P
LANE_BITS = P.bit_length() - 1
ENTRY_BITS = (E * BLOCKS).bit_length() - 1
MAX_TILES = 2 * TILES + 2 * E
SLOTS = 4
PIECES, GU_PIECES = 12, 8
FB = 8
LB = 4
ARENA = 16512
ALPHA = 2.0 ** 0.25
EPS = 1e-5

F32 = mybir.dt.float32
F32R = mybir.dt.float32r
I32 = mybir.dt.int32
ALU = mybir.AluOpType
ACT = mybir.ActivationFunctionType
AX = mybir.AxisListType.X
ds = bass.ds


def shape_constants():
    n1 = np.arange(P)[:, None]
    f1 = np.zeros((P, P))
    for p in range(PAIRS):
        f1[:, 2 * p] = np.cos(2 * np.pi * n1[:, 0] * p / P)
        f1[:, 2 * p + 1] = -np.sin(2 * np.pi * n1[:, 0] * p / P)
    f1[:, 1] = np.cos(np.pi * n1[:, 0])
    f1 /= np.sqrt(S * GROUP_DIM)

    def freqs(p):
        return np.arange(N2) * (P // 2) if p == 0 else p + P * np.arange(N2)

    m2 = np.zeros((P, PAIRS // 2, 2, 2, N2))
    n2 = np.arange(N2)[:, None]
    for p in range(PAIRS):
        th = 2 * np.pi * n2 * freqs(p)[None, :] / S
        c, s = np.cos(th), np.sin(th)
        q, j = p // 2, p % 2
        re, im = slice(j * 64, j * 64 + 32), slice(j * 64 + 32, j * 64 + 64)
        if p:
            m2[re, q, 0, j], m2[im, q, 0, j] = c, s
            m2[re, q, 1, j], m2[im, q, 1, j] = -s, c
        else:
            m2[re, q, 0, j, 0::2], m2[im, q, 0, j, 1::2] = c[:, 0::2], c[:, 1::2]
            m2[re, q, 1, j, 0::2], m2[im, q, 1, j, 1::2] = -s[:, 0::2], -s[:, 1::2]
            alt = (-1.0) ** n2[:, 0]
            m2[re, q, 0, j, 0] = (1 + alt) / 2
            m2[re, q, 1, j, 0] = (1 - alt) / 2
    m2 = m2.reshape(P, PAIRS // 2, P)

    k = np.arange(P)[:, None, None] + P * np.arange(2)[None, :, None]
    ang = 2 * np.pi * k * np.arange(P)[None, None, :] / GROUP_DIM
    cs = np.stack([np.cos(ang), np.sin(ang)], 1)
    alt = np.zeros((P, NG, NG))
    for g in range(NG):
        alt[:, g, g] = (-1.0) ** np.arange(P)
    row_of = np.zeros((P, TILES), np.int32)
    for t in range(TILES):
        for m in range(P):
            kk = freqs(4 * (t // 2) + m // N2)[m % N2]
            row_of[m, t] = kk if t % 2 == 0 else (S - kk if kk else S // 2)
    before = (np.arange(P)[:, None] < np.arange(P)[None, :]) * 1.0
    first = np.tile(EPG - np.arange(EPG), EG)[None, :] * np.ones((P, 1))
    firstg = (EG - np.arange(EG))[None, :] * np.ones((P, 1))
    ebase = (np.arange(E) * RANKS)[None, :] * np.ones((P, 1))
    steps = (np.arange(S // P) * P)[None, :] * np.ones((P, 1))
    parts = [("f1", f1), ("ident", np.eye(P)), ("before", before), ("ones", np.ones((P, P))),
             ("cs", cs), ("alt", alt), ("first", first), ("firstg", firstg),
             ("ebase", ebase), ("steps", steps)]
    at, cols, off = {}, [], 0
    for name, a in parts:
        a = a.reshape(P, -1)
        at[name] = (off, off + a.shape[1])
        off += a.shape[1]
        cols.append(a)
    packed = np.concatenate(cols, 1).astype(np.float32)
    return packed, at, m2.astype(np.float32), row_of


def own_wait(eng, sem, value, gate):
    eng.wait_ge(sem, value)
    eng.sem_inc(gate, 1)


PASSES = ((0, 0), (0, 1), (1, 0))


class Steps:

    def __init__(self, eng, sem):
        self.eng, self.sem, self.start, self.k = eng, sem, 0, 0

    def begin(self, start):
        self.start, self.k = start, 0

    def link(self, ins):
        self.k += 1
        ins.then_inc(self.sem, 1)
        self.eng.wait_ge(self.sem, self.start + self.k)


def jobs_even(j):
    return j // 2 + 1


def jobs_odd(j):
    return (j + 1) // 2


def is_first(g, n=1):
    return isinstance(g, int) and g < n


def s2_base(g):
    if isinstance(g, int):
        return 0 if g == 0 else 4 if g == 1 else 8 * (g - 1)
    return 8 * g - 8


def tr_base(g):
    if isinstance(g, int) and g >= GROUPS - 1:
        return 8 * g if g == GROUPS - 1 else 8 * (GROUPS - 1) + 4
    return 8 * g + 4


def bcast(v, n):
    return bass.AP(v.tensor, v.offset, [[0, n]] + [list(d) for d in v.ap])


def rep_mid(v, n):
    return bass.AP(v.tensor, v.offset, [list(v.ap[0]), [0, n]] + [list(d) for d in v.ap[1:]])


def rep_last(v, n):
    return bass.AP(v.tensor, v.offset, [list(d) for d in v.ap] + [[0, n]])


def trunk_kernel(nc, x, w_in, w_out, router_w, router_b, w_gate, w_up, w_down, ln_g, ln_b,
                 consts, const_at, m2, row_of, out):
    yd = nc.dram_tensor("first_stage", [P, N2, D], F32).ap()
    hd = nc.dram_tensor("h_rows", [S + P, D], F32).ap()
    lists = nc.dram_tensor("expert_lists", [P * E * BLOCKS, 2], I32).ap()
    acc = nc.dram_tensor("sums", [S + P, D], F32).ap()

    with ExitStack() as ctx:
        def at(name, kib, cols, dt=F32):
            t = nc.alloc_sbuf_tensor_at(name, [P, cols], dt, offset=ARENA + int(kib * 1024))
            return t[:, :]

        class Row:

            def __init__(self, kib, end):
                self.byte, self.end = int(kib * 1024), int(end * 1024)

            def take(self, name, cols, dt=F32):
                self.byte, lo = self.byte + (cols * 4 + 31) // 32 * 32, self.byte
                assert self.byte <= self.end, name
                return at(name, lo / 1024, cols, dt)

        def sem(name):
            return ctx.enter_context(nc.semaphore(name))

        A = [at("a_hi", 0, CH * D, F32R), at("a_lo", 32, CH * D, F32R)]
        B = [at("b_hi", 64, CH * D, F32R), at("b_lo", 96, CH * D, F32R)]
        A, B = ([v.rearrange("p (c n) -> p c n", c=CH) for v in w] for w in (A, B))
        fold_t = at("fold", 0, CH * D)
        ych_t = at("ych", 32, 4 * D)
        xch_t = at("xch", 48, 4 * D)
        w_in_t = at("w_in_s", 64, CH * D)
        w_out_t = at("w_out_s", 96, CH * D)
        foldT_t = at("foldT", 128, CH * D)
        T_t = at("T", 160, CH * D)
        midT, T128 = at("midT", 192, D), at("T128", 196, D)
        xt_t = [at("xt_hi", 128, 2 * D, F32R), at("xt_lo", 136, 2 * D, F32R)]
        yt_t = at("yt", 144, 4 * D)
        rows_t = at("rows", 160, 4 * D)
        hT_t = at("hT", 176, 2 * D)
        lng, lnb = at("lng", 184, D), at("lnb", 188, D)
        edge = [at("edge_hi", 176, D, F32R), at("edge_lo", 180, D, F32R)]
        edge = [v.rearrange("p (c n) -> p c n", c=CH) for v in edge]
        cmp = at("cmp", 176, D)[0:1, :].rearrange("p (e j) -> p e j", e=E)
        grow = Row(192, 200)
        rw, m2s = grow.take("rw", CH * E), grow.take("m2s", 2 * 2 * P)
        wgu = [[at(f"wgu{b}_{n}", kib, 2 * CH * F, F32R).rearrange("p (m c f) -> p m c f", m=2, c=CH)
                for n, kib in (("hi", lo), ("lo", lo + 32))] for b, lo in enumerate((0, 128))]
        wd = [at(f"wd_{n}", kib, FC * D, F32R).rearrange("p (c f) -> p c f", c=FC)
              for n, kib in (("hi", 64), ("lo", 80))]
        mxT = [at(f"mxT_{n}", kib, D, F32R).rearrange("p (c n) -> p c n", c=CH)
               for n, kib in (("hi", 96), ("lo", 100))]
        hidT = [at(f"hidT_{n}", kib, F, F32R).rearrange("p (c n) -> p c n", c=FC)
                for n, kib in (("hi", 104), ("lo", 106))]
        xrow = at("xrow", 108, D)
        wraw = at("wraw", 112, SLOTS * D).rearrange("p (s d) -> p s d", s=SLOTS)
        yrow, sgate, hid = at("yrow", 192, D), at("sgate", 196, F), at("hid", 198, F)
        fin_r = at("fin_r", 128, FB * D).rearrange("p (b d) -> p b d", b=FB)
        lng2, lnb2 = at("lng2", 160, D), at("lnb2", 164, D)

        keep = Row(200, 207.8)
        cst = keep.take("cst", consts.shape[1])
        rowix = keep.take("rowix", TILES, I32)
        base = keep.take("base", E)
        tstart = keep.take("tstart", E + 1, I32)
        desti = keep.take("desti", 4, I32)
        payg = keep.take("payg", 8, I32)
        entry_t = keep.take("entries", 2 * 2 * BLOCKS, I32)
        rowg = keep.take("rowg", 4, I32)
        ixg = keep.take("ixg", 1, I32)
        sx = keep.take("sx", 1, I32)
        sxn = keep.take("sxn", 1, I32)
        eps_c, eps2_c = keep.take("eps_c", 1), keep.take("eps2_c", 1)
        zer = keep.take("zer", E)
        rb = keep.take("rb", E)
        mid = keep.take("mid", CH * NG)
        padl = keep.take("padl", 2 * BLOCKS, I32)

        def small(name, *dims):
            v = (keep if name.startswith("ln") else grow).take(name, int(np.prod(dims)))
            if len(dims) == 2:
                return v.rearrange("p (a b) -> p a b", a=dims[0])
            if len(dims) == 3:
                return v.rearrange("p (a b c) -> p a b c", a=dims[0], b=dims[1])
            return v

        lnst, lnmv = small("lnst", LB, 2, 6), small("lnmv", LB, 2)
        lnstd, lnrs, lnsh = small("lnstd", LB), small("lnrs", LB), small("lnsh", LB)
        scT = grow.take("scT", 2 * P)[0:E, :]
        sc, sel, sel2, eq, rank, msum = (small(n, 2, E) for n in ("sc", "sel", "sel2", "eq", "rank", "msum"))
        onehot = [small("onehot0", 2, E), small("onehot1", 2, E)]
        top = [small("top0", 2, EG), small("top1", 2, EG)]
        kmax, gsum, geq = (small(n, 2, EG) for n in ("kmax", "gsum", "geq"))
        gmax, gden = small("gmax", 2), small("gden", 2)
        gk, destf = small("gk", 2, 2), small("destf", 2, 2)
        dint, dlane = grow.take("dint", 4, I32), grow.take("dlane", 4, I32)
        ntile, cum = small("ntile", E), small("cum", E + 1)

        def cview(name):
            lo, hi = const_at[name]
            return cst[:, lo:hi]

        f1, ident, before, ones = (cview(n) for n in ("f1", "ident", "before", "ones"))
        first, firstg, ebase, steps = (cview(n) for n in ("first", "firstg", "ebase", "steps"))
        cs = cview("cs").rearrange("p (m k n) -> p m k n", m=2, k=2)
        alt = cview("alt").rearrange("p (g n) -> p g n", g=NG)
        m2t = m2s[:, :].rearrange("p (b q n) -> p b q n", b=2, q=2)
        paygv = payg[:, :].rearrange("p (s k w) -> p s k w", s=2, k=2)
        entries = entry_t.rearrange("p (b r w) -> p b r w", b=2, w=2)
        rwv = rw.rearrange("p (c e) -> p c e", c=CH)

        w_in_s = w_in_t.rearrange("p (c n) -> p c n", c=CH)
        w_in_g = w_in_t.rearrange("p (q n) -> p q n", n=GROUP_DIM)
        w_out_s = w_out_t.rearrange("p (c n) -> p c n", c=CH)
        fold = fold_t.rearrange("p (m c g n) -> p m c g n", m=2, c=CH, g=NG)
        foldq = fold_t.rearrange("p (m q n) -> p m q n", m=2, n=P)
        foldT = foldT_t.rearrange("p (m g d) -> p m g d", m=2, g=NG)
        T = T_t.rearrange("p (m g d) -> p m g d", m=2, g=NG)
        midv = mid[:, :].rearrange("p (c g) -> p c g", c=CH)
        xch = xch_t.rearrange("p (b n d) -> p b n d", b=2, n=2)
        ych = ych_t.rearrange("p (b n d) -> p b n d", b=2, n=2)

        yt = yt_t.rearrange("p (b q d) -> p b q d", b=2, q=2)
        xt = [v.rearrange("p (m c n) -> p m c n", m=2, c=CH) for v in xt_t]
        rows = rows_t.rearrange("p (b s d) -> p b s d", b=2, s=2)
        hT = hT_t.rearrange("p (c s n) -> p c s n", c=CH, s=2)
        xrow_s = xrow.rearrange("p (d c) -> p c d", c=CH)

        pairs = [ctx.enter_context(nc.psum_tensor(f"ps{i}", [P, D], F32)) for i in range(4)]
        bank = [pairs[i // 2][:, (i % 2) * HALF:(i % 2 + 1) * HALF] for i in range(8)]
        psP, psQ = pairs[0], pairs[1]
        psX = bank[4], bank[5], bank[7]
        psL, psS, psR = bank[6][0:E, 0:2 * P], bank[6][:, 2 * P:2 * P + 2 * E], bank[6][:, 3 * P:]
        psG, psY, psX0, psX1 = bank[0], pairs[1], bank[4], bank[5]
        psU = bank[1][:, 0:F // 2], bank[7][:, 0:F // 2]
        psH = bank[6][:, 0:2 * P], bank[0][:, 0:2 * P]

        c_in = sem("c_in")
        rb_in = sem("rb_in")
        ix_in = sem("ix_in")
        wo_in, wi_in = [sem(f"wo_in{g}") for g in range(NG)], sem("wi_in")
        folded_e, folded_o = sem("folded_e"), sem("folded_o")
        x_in = [sem("x_in0"), sem("x_in1")]
        y1_out = [sem("y1_out0"), sem("y1_out1")]
        job_ps, job_act, job_dve = sem("job_ps"), sem("job_act"), sem("job_dve")
        yt_in = [sem("yt_in0"), sem("yt_in1")]
        rows_in = [sem("rows_in0"), sem("rows_in1")]
        xj_ps, xj_ev = sem("xj_ps"), sem("xj_ev")
        q_ps, p_ps, q_ev, p_ev = (sem(n) for n in ("q_ps", "p_ps", "q_ev", "p_ev"))
        var_ok, std_ok, nrm_ok, hn_ok, hg_ok, h_ok = (
            sem(n) for n in ("var_ok", "std_ok", "nrm_ok", "hn_ok", "hg_ok", "h_ok"))
        h_out = [sem("h_out0"), sem("h_out1")]
        lg_ps, sg_ok, st_ps, m_ok, rk_ps, rk_ev, gate_ok, dest_ok, list_out = (
            sem(n) for n in ("lg_ps", "sg_ok", "st_ps", "m_ok", "rk_ps", "rk_ev", "gate_ok", "dest_ok",
                             "list_out"))
        pad_made, pad_out = sem("pad_made"), sem("pad_out")
        ln_in, rowg_ok, payg_ok, made = (sem(n) for n in ("ln_in", "rowg_ok", "payg_ok", "made"))
        dve_step = sem("dve_step")
        dve_gate, pool_gate, pe_gate = sem("dve_gate"), sem("pool_gate"), sem("pe_gate")
        edge_ok, edge_read, edge_zero = sem("edge_ok"), sem("edge_read"), sem("edge_zero")
        tab_ok = sem("tab_ok")
        ab_ps, ab_hi, ab_lo, xl_ev = sem("ab_ps"), sem("ab_hi"), sem("ab_lo"), sem("xl_ev")
        wraw_in = [sem(f"wraw_in{n}") for n in range(SLOTS)]
        whi_ok, wlo_ok = sem("whi_ok"), sem("wlo_ok")
        entries_in = [sem("entries_in0"), sem("entries_in1")]
        xrow_in, y_out, ixg_ok, sx_ok = sem("xrow_in"), sem("y_out"), sem("ixg_ok"), sem("sx_ok")
        g_ps, ua_ps, ub_ps, x0_ps, x1_ps, xh_ev, xlo_ev = (
            sem(n) for n in ("g_ps", "ua_ps", "ub_ps", "x0_ps", "x1_ps", "xh_ev", "xlo_ev"))
        silu_ok, hida_ok, hidb_ok, h0_ps, h1_ps, hh_ev, hl_ev = (
            sem(n) for n in ("silu_ok", "hida_ok", "hidb_ok", "h0_ps", "h1_ps", "hh_ev", "hl_ev"))
        y0_ps, y1_ps, ya_ok, yd_ok = (sem(n) for n in ("y0_ps", "y1_ps", "ya_ok", "yd_ok"))
        ln2_in = sem("ln2_in")
        fin_in = [sem(f"fin_in{b}") for b in range(FB)]
        fstd_ok, fn_ok, fnn_ok, fg_ok, fb_ok, fh_ok = (
            sem(n) for n in ("fstd_ok", "fn_ok", "fnn_ok", "fg_ok", "fb_ok", "fh_ok"))
        fin_out = [sem(f"fin_out{b}") for b in range(FB)]

        JOB_TR = 18
        JOB_S1 = JOB_TR + 18
        JOB_END = JOB_S1 + 2 * N2
        STEPS = N2 // 4
        B_JOBS, AB_JOBS = 2 * CH, 4 * CH

        def s1_bank(n):
            return (n + 4) % 6

        def s1_free(n):
            b = s1_bank(n)
            return JOB_S1 + n - 6 if n >= 6 else b + (32 if b < 4 else 24)

        def ab_bank(k):
            if k < B_JOBS:
                return 6 + k % 2
            a = (k - B_JOBS) % 8
            return a if a >= 6 else s1_bank(2 * N2 - 6 + a)

        def phase0_dst(j):
            h = slice(j % 2 * HALF, (j % 2 + 1) * HALF)
            if j < JOB_TR - 2:
                return T[:, j // 8, j % 8 // 2, h]
            if j < JOB_TR:
                return T128[0:NG, h]
            t = j - JOB_TR
            return foldT[:, t // 8, t % 8 // 2, h] if t < 16 else midT[0:NG, h]

        def ab_dst(j, part):
            return (B, A)[j // B_JOBS][part][:, j % B_JOBS // 2, j % 2 * HALF:(j % 2 + 1) * HALF]

        def s2_bank(jj):
            return psX[jj % 3]

        def turn_bank(jj):
            return psX[(jj + 4) % 3]

        def s2_src(jj):
            return s2_bank(jj).rearrange("p (c q m n) -> p c q m n", c=2, q=2, m=2)

        def s2_dst(part, m, jj):
            return xt[part][:, m, 2 * jj:2 * jj + 2, :].rearrange("p c (q n) -> p c q n", q=2)

        def gu_piece(b, part, j):
            w = wgu[b][part][:, j // 4]
            return w[:, 2 * (j % 4):2 * (j % 4) + 2, :].rearrange("p c f -> p (c f)")

        def block_of(t, lo):
            return (t - lo).with_bounds(min_val=0, max_val=BLOCKS - 1) if t is not lo else 0

        def gate_of(t, b, lo):
            return entries[:, b, ds(block_of(t, lo), 1), 1].bitcast(F32)

        EARLY, LATE = ((), (4, 5)), ((0, 1, 2, 3), (6, 7))

        def entries_there(eng, e, b, kind):
            if kind == 0:
                eng.wait_ge(entries_in[b], 8 * e + 16 - 8 * b)

        def expert_tiles(eng, tile):
            def expert(i, b, last=False):
                lo = eng.value_load(tstart[0:1, ds(2 * i + b, 1)], min_val=0, max_val=MAX_TILES)
                hi = eng.value_load(tstart[0:1, ds(2 * i + b + 1, 1)], min_val=2, max_val=MAX_TILES)
                tile(lo, 2 * i + b, b, lo, 0, last)
                tile(lo + 1, 2 * i + b, b, lo, 1, last)
                with eng.If(hi > lo + 2):
                    with eng.Fori(lo + 2, hi) as t:
                        tile(t, 2 * i + b, b, lo, 2, last)

            with eng.Fori(0, E // 2 - 1) as i:
                for b in range(2):
                    expert(i, b)
            expert(E // 2 - 1, 0)
            expert(E // 2 - 1, 1, last=True)

        block = ctx.enter_context(nc.Block())

        @block.sync
        def _(sp):
            for b in range(2):
                sp.sem_inc(y1_out[b], 16)
            sp.dma_start(cst[:, :], consts).then_inc(c_in, 16)
            w_out_v = w_out.rearrange("(c p) n -> p c n", p=P)
            for g in range(NG):
                sp.dma_start(w_out_s[:, 2 * g:2 * g + 2, :], w_out_v[:, 2 * g:2 * g + 2, :]
                             ).then_inc(wo_in[g], 16)
            sp.dma_start(w_in_s, w_in.rearrange("(c p) n -> p c n", p=P)).then_inc(wi_in, 16)
            x_v = x.rearrange("(p n) d -> p n d", n=N2)

            def load_x(i, b):
                n = 4 * i + 2 * b
                sp.dma_start(xch[:, b], x_v[:, n:n + 2, :]).then_inc(x_in[b], 16)

            load_x(0, 0)
            load_x(0, 1)
            sp.dma_start(rowix[:, :], row_of).then_inc(ix_in, 16)
            sp.dma_start(rb[:, :], bcast(router_b, P)).then_inc(rb_in, 16)
            sp.wait_ge(pad_made, 1)
            sp.dma_start(lists.rearrange("(p e r) w -> p e (r w)", p=P, e=E),
                         bass.AP(padl.tensor, padl.offset,
                                 [list(padl.ap[0]), [0, E], [1, 2 * BLOCKS]])).then_inc(pad_out, 16)
            sp.dma_start(acc[S:S + P, :], x[0:P, :]).then_inc(pad_out, 16)
            sp.dma_start(hd[S:S + P, :], x[0:P, :]).then_inc(pad_out, 16)

            def store_y(i, b):
                n = 4 * i + 2 * b
                sp.wait_ge(job_act, jobs_even(JOB_S1 + 2 * n + 3))
                sp.wait_ge(job_dve, jobs_odd(JOB_S1 + 2 * n + 3))
                sp.dma_start(yd[:, n:n + 2, :], ych[:, b]).then_inc(y1_out[b], 16)

            for i in range(STEPS):
                for b in range(2):
                    if i < STEPS - 1:
                        sp.wait_ge(job_ps, JOB_S1 + 8 * i + 4 * b + 4)
                        load_x(i + 1, b)
                    store_y(i, b)
            for b in range(2):
                sp.wait_ge(y1_out[b], 16 * STEPS + 16)

            def load_yt(g, b):
                sp.dma_start(yt[:, b], yd_v[:, ds(2 * g, 2), :]).then_inc(yt_in[b], 16)

            def load_m2(g, b):
                sp.dma_start(m2t[:, b], m2[:, ds(2 * g, 2), :]).then_inc(yt_in[b], 16)

            def load_group(g, b):
                sp.wait_ge(xj_ps, s2_base(g - 2) + 4)
                load_yt(g, b)
                load_m2(g, b)

            yd_v = yd.rearrange("(q a) n d -> (a n) q d", a=4)

            sp.wait_ge(ab_ps, B_JOBS)
            load_yt(0, 0)
            load_yt(1, 1)
            sp.dma_start(lng[:, :], bcast(ln_g[0], P)).then_inc(ln_in, 16)
            sp.dma_start(lnb[:, :], bcast(ln_b[0], P)).then_inc(ln_in, 16)
            sp.wait_ge(ab_ps, AB_JOBS)
            load_m2(0, 0)
            load_m2(1, 1)
            sp.dma_start(rwv, router_w.rearrange("(c p) e -> p c e", p=P)).then_inc(rb_in, 16)
            for b in range(2):
                load_group(2 + b, b)
            with sp.Fori(1, GROUPS // 2 - 1) as i:
                for b in range(2):
                    load_group(2 * i + 2 + b, b)

            wg_v = w_gate.rearrange("e (p h c) f -> p e h (c f)", p=P, h=4)
            wu_v = w_up.rearrange("e (p h c) f -> p e h (c f)", p=P, h=4)
            wd_v = w_down.rearrange("e (c p) f -> p e c f", p=P)

            lists_v = lists.rearrange("(p e r) w -> p e (r w)", p=P, e=E)

            def load_entries(e, b):
                sp.dma_start(entry_t[:, b * 2 * BLOCKS:(b + 1) * 2 * BLOCKS].rearrange(
                    "p (o w) -> p o w", o=1), lists_v[:, ds(e, 1), :]).then_inc(entries_in[b], 16)

            def load_piece(e, j):
                if not is_first(e) or j >= SLOTS:
                    sp.wait_ge(wlo_ok, PIECES * e + j - SLOTS + 1)
                w, h = (wg_v, wu_v, wd_v)[j // 4], j % 4
                sp.dma_start(wraw[:, j % SLOTS:j % SLOTS + 1, :], w[:, ds(e, 1), h, :]
                             ).then_inc(wraw_in[j % SLOTS], 16)

            def load_expert(e, b):
                for j in range(PIECES):
                    load_piece(e, j)
                    if j == 4 and not is_first(e, 2):
                        done = sp.value_load(tstart[0:1, ds(e - 1, 1)], min_val=2, max_val=MAX_TILES)
                        sp.wait_ge(ya_ok, done + 2)
                        sp.wait_ge(yd_ok, done + 2)
                        load_entries(e, b)

            sp.wait_ge(q_ps, GROUPS)
            for j in range(GU_PIECES):
                load_piece(0, j)
            sp.wait_ge(list_out, 64 * GROUPS)
            load_entries(0, 0)
            load_entries(1, 1)
            for j in range(GU_PIECES, PIECES):
                load_piece(0, j)
            sp.wait_ge(tab_ok, 1)
            load_expert(1, 1)
            with sp.Fori(1, E // 2) as i:
                for b in range(2):
                    load_expert(2 * i + b, b)

            total = sp.value_load(tstart[0:1, E:E + 1], min_val=2 * E, max_val=MAX_TILES)
            sp.wait_ge(y_out, total * 16 + 32)

            acc_v = acc[0:S, :].rearrange("(t p) d -> p t d", p=P)
            out_v = out.rearrange("(t p) d -> p t d", p=P)

            def load_fin(t, b):
                sp.dma_start(fin_r[:, b:b + 1, :], acc_v[:, ds(t, 1), :]).then_inc(fin_in[b], 16)

            def store_fin(t, b):
                sp.wait_ge(fh_ok, t + 1)
                sp.dma_start(out_v[:, ds(t, 1), :], fin_r[:, b:b + 1, :]).then_inc(fin_out[b], 16)

            for b in range(FB):
                load_fin(b, b)
                if b == 1:
                    sp.dma_start(lng2, bcast(ln_g[1], P)).then_inc(ln2_in, 16)
                    sp.dma_start(lnb2, bcast(ln_b[1], P)).then_inc(ln2_in, 16)
            for b in range(2):
                store_fin(b, b)
            with sp.Fori(1, TILES // FB) as i:
                for b in range(FB):
                    sp.wait_ge(fin_out[b], 16 * i)
                    load_fin(FB * i + b, b)
                    store_fin(FB * (i - 1) + b + 2, (b + 2) % FB)
            for b in range(2, FB):
                store_fin(TILES - FB + b, b)
            for b in range(FB):
                sp.wait_ge(fin_out[b], 16 * (TILES // FB))

        @block.tensor
        def _(pe):
            def bank_free(j):
                if j < 8:
                    return
                if j % 2 == 0:
                    pe.wait_ge(job_act, jobs_even(j - 8))
                else:
                    pe.wait_ge(job_dve, jobs_odd(j - 8))

            pe.wait_ge(c_in, 16)
            j = 0
            for m in range(2):
                for g in range(NG):
                    pe.wait_ge(wo_in[g], 16)
                    for h in range(2):
                        bank_free(j)
                        for k in range(2):
                            mm = nc.tensor.matmul(bank[j % 8], cs[:, m, k, :],
                                                  w_out_s[:, 2 * g + k, h * HALF:(h + 1) * HALF],
                                                  start=(k == 0), stop=(k == 1))
                        mm.then_inc(job_ps, 1)
                        j += 1
            for h in range(2):
                bank_free(j)
                for c in range(CH):
                    mm = nc.tensor.matmul(bank[j % 8][0:NG, :], alt[:, c // 2, :],
                                          w_out_s[:, c, h * HALF:(h + 1) * HALF],
                                          start=(c == 0), stop=(c == CH - 1))
                mm.then_inc(job_ps, 1)
                j += 1
            for m in range(2):
                pe.wait_ge(folded_e if m == 0 else folded_o, 3 if m == 0 else 2)
                for g in range(NG):
                    for h in range(2):
                        bank_free(j)
                        for c in range(4):
                            mm = nc.tensor.transpose(bank[j % 8][:, c * P:(c + 1) * P],
                                                     fold[:, m, 4 * h + c, g, :], ident)
                        mm.then_inc(job_ps, 1)
                        j += 1
            for h in range(2):
                bank_free(j)
                for c in range(4):
                    mm = nc.tensor.transpose(bank[j % 8][0:NG, c * P:(c + 1) * P],
                                             midv[:, 4 * h + c, :], ident)
                mm.then_inc(job_ps, 1)
                j += 1
            def fold_product(k):
                m, c, h = 1 - k // B_JOBS, k % B_JOBS // 2, k % 2
                if 2 <= k < B_JOBS:
                    pe.wait_ge(ab_lo, k - 1)
                elif B_JOBS <= k < B_JOBS + 6:
                    n = JOB_END - 6 + k - B_JOBS
                    pe.wait_ge(job_act if n % 2 == 0 else job_dve,
                               jobs_even(n) if n % 2 == 0 else jobs_odd(n))
                elif k >= B_JOBS:
                    pe.wait_ge(ab_lo, k - 7)
                dst = bank[ab_bank(k)]
                for g in range(NG):
                    mm = nc.tensor.matmul(dst, foldT[:, m, g, c * P:(c + 1) * P],
                                          T[:, m, g, h * HALF:(h + 1) * HALF],
                                          start=(g == 0), stop=(m == 1 and g == NG - 1))
                if m == 0:
                    mm = nc.tensor.matmul(dst, midT[0:NG, c * P:(c + 1) * P],
                                          T128[0:NG, h * HALF:(h + 1) * HALF],
                                          start=False, stop=True)
                mm.then_inc(ab_ps, 1)

            for i in range(STEPS):
                for b in range(2):
                    pe.wait_ge(x_in[b], 16 * i + 16)
                    for n in range(8 * i + 4 * b, 8 * i + 4 * b + 4):
                        before_n = s1_free(n)
                        if before_n % 2 == 0:
                            pe.wait_ge(job_act, jobs_even(before_n))
                        else:
                            pe.wait_ge(job_dve, jobs_odd(before_n))
                        nc.tensor.matmul(bank[s1_bank(n)], f1,
                                         xch[:, b, n % 4 // 2, n % 2 * HALF:(n % 2 + 1) * HALF],
                                         start=True, stop=True).then_inc(job_ps, 1)
                    if i == b == 0:
                        pe.wait_ge(job_act, jobs_even(JOB_S1 - 1))
                        pe.wait_ge(job_dve, jobs_odd(JOB_S1 - 1))
                    fold_product(2 * i + b)
            for k in range(B_JOBS, AB_JOBS):
                fold_product(k)
            pe.wait_ge(ab_lo, AB_JOBS)

            def second_stage(g, i, b):
                base_j = s2_base(g)
                pe.wait_ge(yt_in[b], 32 * i + 32)
                for jj in range(4):
                    if jj < 2 and not is_first(g, 3):
                        pe.wait_ge(xj_ev, base_j - 1 + jj)
                    elif jj == 3:
                        pe.wait_ge(xj_ev, base_j + 1)
                        pe.wait_ge(xl_ev, 4 * g + 1)
                    for c in range(2):
                        for q in range(2):
                            lo = c * 256 + q * P
                            cc = 2 * jj + c
                            mm = nc.tensor.matmul(s2_bank(jj)[:, lo:lo + P],
                                                  yt[:, b, q, cc * P:(cc + 1) * P],
                                                  m2t[:, b, q, :], start=True, stop=True)
                    mm.then_inc(xj_ps, 1)

            def product(g, m, ps, w, free, done, edge_row=False):
                if not is_first(g):
                    pe.wait_ge(free, g)
                for h in range(2):
                    cols = slice(h * HALF, (h + 1) * HALF)
                    if edge_row:
                        for n, (l, r) in enumerate(PASSES):
                            for c in range(CH):
                                nc.tensor.matmul(ps[:, cols], edge[l][:, c, :], A[r][:, c, cols],
                                                 start=(n == 0 and c == 0), stop=False)
                    for n, (l, r) in enumerate(PASSES):
                        for c in range(CH):
                            mm = nc.tensor.matmul(ps[:, cols], xt[l][:, m, c, :], w[r][:, c, cols],
                                                  start=(n == 0 and c == 0 and not edge_row),
                                                  stop=(n == 2 and c == CH - 1))
                mm.then_inc(done, 1)

            def turn_rows(g, b, base_j):
                last = isinstance(g, int) and g >= GROUPS - 2
                for hh in range(2):
                    for s in range(2):
                        jj = 2 * hh + s
                        if hh == 0:
                            pe.wait_ge(h_ok, 2 * g + 1 + s)
                        if jj < 3:
                            pe.wait_ge(xj_ev, base_j if last and jj == 0 else base_j - 2 + jj)
                            if not last:
                                pe.wait_ge(xl_ev, 4 * g + 10 + jj)
                        else:
                            pe.wait_ge(xj_ev, base_j + 1)
                        for c in range(4):
                            cc = 4 * hh + c
                            mm = nc.tensor.transpose(turn_bank(jj)[:, c * P:(c + 1) * P],
                                                     rows[:, b, s, cc * P:(cc + 1) * P], ident)
                        mm.then_inc(xj_ps, 1)

            def router(g, base_j):
                if is_first(g):
                    pe.wait_ge(rb_in, 32)
                else:
                    pe.wait_ge(rk_ev, g)
                for c in range(CH):
                    if c % 4 == 0:
                        pe.wait_ge(xj_ev, base_j + 2 + c // 2)
                    mm = nc.tensor.matmul(psL, rwv[:, c, :], hT[:, c, :, :].rearrange("p s n -> p (s n)"),
                                          start=(c == 0), stop=(c == CH - 1))
                mm.then_inc(lg_ps, 1)

            def turn_scores(g):
                own_wait(pe, sg_ok, g + 1, pe_gate)
                for s in range(2):
                    mm = nc.tensor.transpose(psS[:, s * E:(s + 1) * E], scT[:, s * P:(s + 1) * P],
                                             ident[0:E, 0:E])
                mm.then_inc(st_ps, 1)

            def ranks(g):
                pe.wait_ge(m_ok, g + 1)
                r0, r1, r2 = (psR[:, i * E:(i + 1) * E] for i in range(3))
                nc.tensor.matmul(r0, before, msum[:, 0], start=True, stop=True)
                nc.tensor.matmul(r1, before, msum[:, 1], start=True, stop=False)
                nc.tensor.matmul(r1, ones, msum[:, 0], start=False, stop=True)
                nc.tensor.matmul(r2, ones, msum[:, 0], start=True, stop=False)
                nc.tensor.matmul(r2, ones, msum[:, 1], start=False, stop=True).then_inc(rk_ps, 1)

            def group(g, i, b):
                pe.wait_ge(xj_ev, s2_base(g) + 4)
                pe.wait_ge(xl_ev, 4 * g + 4)
                if is_first(g):
                    pe.wait_ge(edge_ok, 2)
                product(g, 1, psQ, B, q_ev, q_ps, edge_row=is_first(g))
                if not is_first(g, 2):
                    turn_scores(g - 2)
                product(g, 0, psP, A, p_ev, p_ps)
                if not (isinstance(g, int) and g == GROUPS - 1):
                    second_stage(g + 1, i if b == 0 else i + 1, 1 - b)
                if not is_first(g, 2):
                    ranks(g - 2)
                if not is_first(g):
                    turn_rows(g - 1, 1 - b, tr_base(g))
                    router(g - 1, tr_base(g))

            second_stage(0, 0, 0)
            group(0, 0, 0)
            group(1, 0, 1)
            with pe.Fori(1, GROUPS // 2 - 1) as i:
                for b in range(2):
                    group(2 * i + b, i, b)
            for b in range(2):
                group(GROUPS - 2 + b, GROUPS // 2 - 1, b)
            turn_scores(GROUPS - 2)
            ranks(GROUPS - 2)
            turn_rows(GROUPS - 1, 1, tr_base(GROUPS))
            router(GROUPS - 1, tr_base(GROUPS))
            turn_scores(GROUPS - 1)
            ranks(GROUPS - 1)

            pe.sem_inc(x1_ps, 1)
            pe.sem_inc(y1_ps, 1)
            pe.wait_ge(p_ev, GROUPS)
            pe.wait_ge(q_ev, GROUPS)
            pe.wait_ge(xj_ev, tr_base(GROUPS) + 4)
            pe.wait_ge(tab_ok, 1)

            def turn_x(half, done):
                for c in range(4):
                    mm = nc.tensor.transpose(psX0[:, c * P:(c + 1) * P] if half == 0 else
                                             psX1[:, c * P:(c + 1) * P],
                                             xrow_s[:, 4 * half + c, :], ident)
                mm.then_inc(done, 1)

            def turn_hidden(half, done):
                for c in range(2 * half, 2 * half + 2):
                    mm = nc.tensor.transpose(psH[half][:, (c % 2) * P:(c % 2 + 1) * P],
                                             hid[:, c * P:(c + 1) * P], ident)
                mm.then_inc(done, 1)

            def up_or_gate(ps, b, m, lo, hi):
                for n, (l, r) in enumerate(PASSES):
                    for c in range(CH):
                        mm = nc.tensor.matmul(ps, mxT[l][:, c, :],
                                              wgu[b][r][:, m, c, lo:hi],
                                              start=(n == 0 and c == 0), stop=(n == 2 and c == CH - 1))
                return mm

            def tile(t, e, b, lo, kind, last):
                pe.wait_ge(xh_ev, 2 * t + 2)
                pe.wait_ge(xlo_ev, 2 * t + 2)
                pe.wait_ge(wlo_ok, PIECES * e + 4)
                up_or_gate(psG, b, 0, 0, F).then_inc(g_ps, 1)
                pe.wait_ge(wlo_ok, PIECES * e + GU_PIECES)
                up_or_gate(psU[0], b, 1, 0, F // 2).then_inc(ua_ps, 1)
                up_or_gate(psU[1], b, 1, F // 2, F).then_inc(ub_ps, 1)
                pe.wait_ge(hida_ok, t + 1)
                turn_hidden(0, h0_ps)
                pe.wait_ge(xrow_in, 16 * t + 32)
                turn_x(0, x0_ps)
                pe.wait_ge(hidb_ok, t + 1)
                turn_hidden(1, h1_ps)
                turn_x(1, x1_ps)
                pe.wait_ge(wlo_ok, PIECES * e + PIECES)
                pe.wait_ge(ya_ok, t + 2)
                pe.wait_ge(yd_ok, t + 2)
                for h in range(2):
                    cols = slice(h * HALF, (h + 1) * HALF)
                    for n, (l, r) in enumerate(PASSES):
                        for c in range(FC):
                            if h == 0 and n != 1 and c % 2 == 0:
                                pe.wait_ge(hh_ev if n == 0 else hl_ev, 2 * t + 1 + c // 2)
                            mm = nc.tensor.matmul(psY[:, cols], hidT[l][:, c, :],
                                                  wd[r][:, c, cols],
                                                  start=(n == 0 and c == 0),
                                                  stop=(n == 2 and c == FC - 1))
                    mm.then_inc(y0_ps if h == 0 else y1_ps, 1)

            pe.wait_ge(xrow_in, 16)
            turn_x(0, x0_ps)
            turn_x(1, x1_ps)
            expert_tiles(pe, tile)

        @block.scalar
        def _(act):
            def empty(dst, src, j):
                act.wait_ge(job_ps, j + 1)
                nc.scalar.copy(dst, src).then_inc(job_act, 1)

            def take_hi(k):
                act.wait_ge(ab_ps, k + 1)
                nc.scalar.copy(ab_dst(k, 0), bank[ab_bank(k)]).then_inc(ab_hi, 1)

            for j in range(0, JOB_S1, 2):
                dst = phase0_dst(j)
                empty(dst, bank[j % 8][0:dst.shape[0], :], j)
            for i in range(STEPS):
                for b in range(2):
                    act.wait_ge(y1_out[b], 16 * i + 16)
                    for n in range(8 * i + 4 * b, 8 * i + 4 * b + 4, 2):
                        empty(ych[:, b, n % 4 // 2, 0:HALF], bank[s1_bank(n)], JOB_S1 + n)
                    take_hi(2 * i + b)
            for k in range(B_JOBS, AB_JOBS):
                take_hi(k)

            def empty_s2(g):
                for jj in range(4):
                    act.wait_ge(xj_ps, s2_base(g) + jj + 1)
                    for m in range(2):
                        a = nc.scalar.copy(s2_dst(0, m, jj), s2_src(jj)[:, :, :, m, :])
                    a.then_inc(xj_ev, 1)

            def empty_turn(base_j, g):
                for jj in range(4):
                    act.wait_ge(xj_ps, base_j + jj + 1)
                    if jj == 0 and not is_first(g):
                        act.wait_ge(lg_ps, g)
                    hh = jj // 2
                    nc.scalar.copy(hT[:, 4 * hh:4 * hh + 4, jj % 2, :],
                                   turn_bank(jj).rearrange("p (c n) -> p c n", c=4)).then_inc(xj_ev, 1)

            def scores(g):
                act.wait_ge(lg_ps, g + 1)
                if not is_first(g):
                    act.wait_ge(st_ps, g)
                nc.scalar.activation(scT, psL, ACT.Sigmoid).then_inc(sg_ok, 1)

            def group(g, b, last=False):
                if not last:
                    empty_s2(g + 1)
                if not is_first(g):
                    empty_turn(tr_base(g), g - 1)
                    scores(g - 1)
                act.wait_ge(var_ok, g + 1)
                nc.scalar.activation(lnstd[:, 0:2], lnmv[:, 0:2, 1], ACT.Sqrt, bias=eps_c).then_inc(std_ok, 1)
                act.wait_ge(nrm_ok, g + 1)
                for s in range(2):
                    nc.scalar.activation(rows[:, b, s, :], rows[:, b, s, :], ACT.Identity,
                                         bias=lnsh[:, s:s + 1], scale=lnrs[:, s:s + 1]
                                         ).then_inc(hn_ok, 1)

            empty_s2(0)
            act.wait_ge(xj_ev, 4)
            act.wait_ge(edge_zero, 2)
            nc.scalar.copy(edge[0][:, :, 0], xt[0][:, 1, :, 0].bitcast(F32)).then_inc(edge_read, 1)
            act.wait_ge(edge_read, 1)
            act.wait_ge(xl_ev, 4)
            nc.scalar.copy(xt[0][:, 1, :, 0], zer[:, 0:CH]).then_inc(edge_ok, 1)
            group(0, 0)
            group(1, 1)
            with act.Fori(1, GROUPS // 2 - 1) as i:
                for b in range(2):
                    group(2 * i + b, b)
            group(GROUPS - 2, 0)
            group(GROUPS - 1, 1, last=True)
            act.wait_ge(p_ps, GROUPS)

            def split(e, j, dst):
                act.wait_ge(wraw_in[j % SLOTS], 16 * (PIECES // SLOTS * e + j // SLOTS + 1))
                nc.scalar.copy(dst, wraw[:, j % SLOTS, :]).then_inc(whi_ok, 1)

            def split_gu(e, b, js):
                for j in js:
                    split(e, j, gu_piece(b, 0, j))

            def turn_x(t):
                for half, ps, done in ((0, psX0, x0_ps), (1, psX1, x1_ps)):
                    act.wait_ge(done, t + 1 + half)
                    nc.scalar.copy(mxT[0][:, 4 * half:4 * half + 4, :].rearrange("p c n -> p (c n)"),
                                   ps).then_inc(xh_ev, 1)

            def tile(t, e, b, lo, kind, last):
                if kind == 0:
                    act.wait_ge(y1_ps, lo + 1)
                    for c in range(FC):
                        split(e, GU_PIECES + c, wd[0][:, c, :])
                act.wait_ge(g_ps, t + 1)
                nc.scalar.activation(sgate, psG, ACT.Silu).then_inc(silu_ok, 1)
                if kind < 2 and not last:
                    split_gu(e + 1, 1 - b, EARLY[kind])
                for half, done in ((0, h0_ps), (1, h1_ps)):
                    act.wait_ge(done, t + 1)
                    nc.scalar.copy(hidT[0][:, 2 * half:2 * half + 2, :].rearrange("p c n -> p (c n)"),
                                   psH[half]).then_inc(hh_ev, 1)
                turn_x(t + 1)
                if kind < 2 and not last:
                    split_gu(e + 1, 1 - b, LATE[kind])
                act.wait_ge(y0_ps, t + 1)
                entries_there(act, e, b, kind)
                act.wait_ge(y_out, 16 * t + 32)
                nc.scalar.mul(yrow[:, 0:HALF], psY[:, 0:HALF], gate_of(t, b, lo)).then_inc(ya_ok, 1)

            split_gu(0, 0, range(4))
            empty_turn(tr_base(GROUPS), GROUPS - 1)
            scores(GROUPS - 1)
            split_gu(0, 0, range(4, GU_PIECES))
            act.wait_ge(tab_ok, 1)
            turn_x(0)
            expert_tiles(act, tile)

            def deviation(t, b):
                act.wait_ge(fn_ok, t + 1)
                nc.scalar.activation(lnstd[:, b % LB:b % LB + 1], lnmv[:, b % LB, 1:2], ACT.Sqrt,
                                     bias=eps2_c).then_inc(fstd_ok, 1)

            def normalize(t, b):
                act.wait_ge(fnn_ok, t + 1)
                nc.scalar.activation(fin_r[:, b, :], fin_r[:, b, :], ACT.Identity,
                                     bias=lnsh[:, b % LB:b % LB + 1],
                                     scale=lnrs[:, b % LB:b % LB + 1]).then_inc(fg_ok, 1)

            def fin(t, b):
                deviation(t, b)
                if not is_first(t):
                    normalize(t - 1, (b - 1) % FB)

            for b in range(FB):
                fin(b, b)
            with act.Fori(1, TILES // FB) as i:
                for b in range(FB):
                    fin(FB * i + b, b)
            normalize(TILES - 1, FB - 1)

        @block.vector
        def _(dve):
            step = Steps(dve, dve_step)
            link = step.link
            nc.vector.memset(eps_c, EPS)
            nc.vector.memset(eps2_c, EPS / ALPHA ** 2)
            nc.vector.memset(base[:, :], 0.0)
            nc.vector.memset(zer, 0.0).then_inc(made, 1)
            def fold_even():
                dve.wait_ge(wi_in, 16)
                nc.vector.tensor_tensor(foldq[:, 0, :, 1:P], w_in_g[:, :, 1:P],
                                        w_in_g[:, :, GROUP_DIM - 1:P:-1], ALU.add).then_inc(folded_e, 1)
                nc.vector.tensor_copy(foldq[:, 0, :, 0:1], w_in_g[:, :, 0:1]).then_inc(folded_e, 1)
                nc.vector.tensor_copy(midv.rearrange("p c g -> p (c g)").rearrange("p (q o) -> p q o", o=1),
                                      w_in_g[:, :, P:P + 1]).then_inc(folded_e, 1)

            def empty(dst, src, j):
                dve.wait_ge(job_ps, j + 1)
                nc.vector.tensor_copy(dst, src).then_inc(job_dve, 1)

            for j in range(1, JOB_S1, 2):
                if j == 11:
                    fold_even()
                dst = phase0_dst(j)
                empty(dst, bank[j % 8][0:dst.shape[0], :], j)
            def take_lo(k):
                dve.wait_ge(ab_hi, k + 1)
                nc.vector.tensor_tensor(ab_dst(k, 1), bank[ab_bank(k)], ab_dst(k, 0).bitcast(F32),
                                        ALU.subtract).then_inc(ab_lo, 1)

            for i in range(STEPS):
                for b in range(2):
                    dve.wait_ge(y1_out[b], 16 * i + 16)
                    for n in range(8 * i + 4 * b + 1, 8 * i + 4 * b + 4, 2):
                        empty(ych[:, b, n % 4 // 2, HALF:D], bank[s1_bank(n)], JOB_S1 + n)
                    take_lo(2 * i + b)
            for b in range(2):
                dve.wait_ge(y1_out[b], 16 * STEPS + 16)
            for k in range(B_JOBS, AB_JOBS):
                take_lo(k)
            dve.wait_ge(ab_ps, AB_JOBS)
            nc.vector.memset(edge[0][:, :, :].bitcast(F32), 0.0).then_inc(edge_zero, 1)
            nc.vector.memset(edge[1][:, :, :].bitcast(F32), 0.0).then_inc(edge_zero, 1)

            def empty_s2(g):
                for jj in range(4):
                    dve.wait_ge(xj_ev, s2_base(g) + jj + 1)
                    for m in range(2):
                        a = nc.vector.tensor_tensor(s2_dst(1, m, jj), s2_src(jj)[:, :, :, m, :],
                                                    s2_dst(0, m, jj).bitcast(F32), ALU.subtract)
                    a.then_inc(xl_ev, 1)

            def statistics(src, s):
                nc.vector.bn_stats(lnst[:, s, 0, :], src[:, 0:HALF])
                link(nc.vector.bn_stats(lnst[:, s, 1, :], src[:, HALF:D]))
                dve.sem_inc(dve_gate, 1)
                return nc.vector.bn_aggr(lnmv[:, s, :], lnst[:, s].rearrange("p h w -> p (h w)"))

            def rows_ready(g, b, i):
                dve.wait_ge(q_ps, g + 1)
                dve.wait_ge(rows_in[b], 32 * i + 32)
                nc.vector.scalar_tensor_tensor(rows[:, b, 0, :], rows[:, b, 0, :], ALPHA,
                                               psQ[:, :], ALU.mult, ALU.add)
                nc.vector.scalar_tensor_tensor(rows[:, b, 1, :], rows[:, b, 1, :], ALPHA,
                                               psQ[:, :], ALU.mult, ALU.subtract).then_inc(q_ev, 1)
                dve.wait_ge(p_ps, g + 1)
                dve.wait_ge(q_ev, g + 1)
                for s in range(2):
                    a = nc.vector.tensor_tensor(rows[:, b, s, :], rows[:, b, s, :], psP[:, :], ALU.add)
                a.then_inc(p_ev, 1)
                dve.wait_ge(p_ev, g + 1)
                for s in range(2):
                    a = statistics(rows[:, b, s, :], s)
                a.then_inc(var_ok, 1)

            def rows_finish(g, b):
                dve.wait_ge(std_ok, g + 1)
                link(nc.vector.reciprocal(lnrs[:, 0:2], lnstd[:, 0:2]))
                nc.vector.scalar_tensor_tensor(lnsh[:, 0:2], lnmv[:, 0:2, 0], -1.0, lnrs[:, 0:2],
                                               ALU.mult, ALU.mult).then_inc(nrm_ok, 1)
                for s in range(2):
                    dve.wait_ge(hn_ok, 2 * g + s + 1)
                    nc.vector.tensor_tensor(rows[:, b, s, :], rows[:, b, s, :], lng[:, :],
                                            ALU.mult).then_inc(hg_ok, 1)

            def grp(v):
                return v.rearrange("p s (g j) -> p s g j", j=EPG)

            first_g = bass.AP(first.tensor, first.offset,
                              [list(first.ap[0]), [0, 2], [EPG, EG], [1, EPG]])

            def choose(g):
                dve.wait_ge(st_ps, g + 1)
                link(nc.vector.tensor_copy(sc.rearrange("p s e -> p (s e)"), psS))
                link(nc.vector.tensor_tensor(sel, sc, rep_mid(rb[:, :], 2), ALU.add))
                cur = sel
                for k in range(2):
                    link(nc.vector.tensor_reduce(top[k], grp(cur), AX, ALU.max))
                    link(nc.vector.tensor_tensor(grp(eq), grp(cur), rep_last(top[k], EPG), ALU.is_equal))
                    link(nc.vector.tensor_tensor(eq, eq, rep_mid(first, 2), ALU.mult))
                    link(nc.vector.tensor_reduce(kmax, grp(eq), AX, ALU.max))
                    link(nc.vector.tensor_tensor(grp(onehot[k]), first_g, rep_last(kmax, EPG),
                                                 ALU.is_equal))
                    if k == 0:
                        link(nc.vector.scalar_tensor_tensor(
                            sel2.rearrange("p s e -> p (s e)"), onehot[0].rearrange("p s e -> p (s e)"),
                            -1e30, sel.rearrange("p s e -> p (s e)"), ALU.mult, ALU.add))
                        cur = sel2
                link(nc.vector.tensor_tensor(gsum, top[0], top[1], ALU.add))
                link(nc.vector.tensor_reduce(gmax, gsum, AX, ALU.max))
                link(nc.vector.tensor_tensor(geq, gsum, rep_last(gmax, EG), ALU.is_equal))
                link(nc.vector.tensor_tensor(geq, geq, rep_mid(firstg, 2), ALU.mult))
                link(nc.vector.tensor_reduce(gmax, geq, AX, ALU.max))
                link(nc.vector.tensor_tensor(geq, rep_mid(firstg, 2), rep_last(gmax, EG), ALU.is_equal))
                for k in range(2):
                    link(nc.vector.tensor_tensor(grp(onehot[k]), grp(onehot[k]), rep_last(geq, EPG),
                                                 ALU.mult))
                nc.vector.tensor_tensor(msum, onehot[0], onehot[1], ALU.add).then_inc(m_ok, 1)

            def take_ranks(g):
                dve.wait_ge(rk_ps, g + 1)
                link(nc.vector.tensor_tensor(
                    rank, psR[:, 0:2 * E].rearrange("p (s e) -> p s e", s=2),
                    rep_mid(base[:, :], 2), ALU.add))
                nc.vector.tensor_tensor(base[:, :], base[:, :], psR[:, 2 * E:3 * E],
                                        ALU.add).then_inc(rk_ev, 1)
                dve.wait_ge(rk_ev, g + 1)
                link(nc.vector.tensor_tensor(rank, rank, rep_mid(ebase, 2), ALU.add))

            def place(g):
                for k in range(2):
                    link(nc.vector.tensor_tensor(eq, sc, onehot[k], ALU.mult))
                    link(nc.vector.tensor_reduce(gk[:, :, k], eq, AX, ALU.add))
                link(nc.vector.tensor_tensor(gden, gk[:, :, 0], gk[:, :, 1], ALU.add))
                link(nc.vector.tensor_scalar(gden, gden, ALPHA, None, ALU.mult))
                link(nc.vector.reciprocal(gden, gden))
                if not is_first(g):
                    dve.wait_ge(list_out, 64 * g)
                nc.vector.tensor_tensor(paygv[:, :, :, 1].bitcast(F32), gk, rep_last(gden, 2),
                                        ALU.mult).then_inc(gate_ok, 1)
                for k in range(2):
                    link(nc.vector.tensor_tensor(eq, rank, onehot[k], ALU.mult))
                    link(nc.vector.tensor_reduce(
                        destf[:, :, k], eq, AX, ALU.add))
                link(nc.vector.tensor_copy(dint, destf.rearrange("p s k -> p (s k)")))
                link(nc.vector.tensor_scalar(dlane, dint, P - 1, ENTRY_BITS, ALU.bitwise_and,
                                             ALU.logical_shift_left))
                link(nc.vector.tensor_scalar(dint, dint, LANE_BITS, None, ALU.logical_shift_right))
                nc.vector.tensor_tensor(desti[:, :], dint, dlane, ALU.bitwise_or).then_inc(dest_ok, 1)
                dve.wait_ge(dest_ok, g + 1)

            ROWS_STEPS, ROUTE_STEPS = 3, 37

            def group(g, b, i):
                if not is_first(g, 2):
                    step.begin(2 * ROWS_STEPS + (ROUTE_STEPS + ROWS_STEPS) * (g - 2))
                    choose(g - 2)
                if not (isinstance(g, int) and g == GROUPS - 1):
                    empty_s2(g + 1)
                if not is_first(g, 2):
                    take_ranks(g - 2)
                rows_ready(g, b, i)
                last = isinstance(g, int) and g == GROUPS - 1
                if last:
                    rows_finish(g, b)
                if not is_first(g, 2):
                    place(g - 2)
                if not last:
                    rows_finish(g, b)
                if not is_first(g, 2):
                    assert step.k == ROUTE_STEPS + ROWS_STEPS, step.k

            empty_s2(0)
            dve.wait_ge(edge_read, 1)
            dve.wait_ge(edge_zero, 2)
            dve.wait_ge(xl_ev, 4)
            nc.vector.tensor_copy(edge[1][:, :, 0], xt[1][:, 1, :, 0].bitcast(F32)).then_inc(edge_read, 1)
            dve.wait_ge(edge_read, 2)
            nc.vector.tensor_copy(xt[1][:, 1, :, 0], zer[:, 0:CH]).then_inc(edge_ok, 1)
            dve.wait_ge(rb_in, 32)
            dve.wait_ge(ln_in, 32)
            group(0, 0, 0)
            group(1, 1, 0)
            with dve.Fori(1, GROUPS // 2 - 1) as i:
                for b in range(2):
                    group(2 * i + b, b, i)
            for b in range(2):
                group(GROUPS - 2 + b, b, GROUPS // 2 - 1)
            def split(e, j, hi, lo):
                dve.wait_ge(whi_ok, PIECES * e + j + 1)
                nc.vector.tensor_tensor(lo, wraw[:, j % SLOTS, :], hi.bitcast(F32),
                                        ALU.subtract).then_inc(wlo_ok, 1)

            def split_gu(e, b, js):
                for j in js:
                    split(e, j, gu_piece(b, 0, j), gu_piece(b, 1, j))

            for g in (GROUPS - 2, GROUPS - 1):
                choose(g)
                if g == GROUPS - 1:
                    split_gu(0, 0, (0, 1))
                take_ranks(g)
                place(g)
            link(nc.vector.tensor_tensor(
                cmp, rep_last(base[0:1, :], S // P), rep_mid(steps[0:1, :], E), ALU.is_gt))
            link(nc.vector.tensor_reduce(ntile[0:1, :], cmp, AX, ALU.add))
            link(nc.vector.tensor_scalar_max(ntile[0:1, :], ntile[0:1, :], 2.0))
            nc.vector.memset(cum[0:1, 0:1], 0.0)
            link(nc.vector.tensor_tensor_scan(cum[0:1, 1:E + 1], ntile[0:1, :], zer[0:1, 0:E], 0.0,
                                              ALU.add, ALU.add))
            nc.vector.tensor_copy(tstart[0:1, :], cum[0:1, :]).then_inc(tab_ok, 1)
            dve.wait_ge(tab_ok, 1)

            def turn_x(t):
                for half, ps in ((0, psX0), (1, psX1)):
                    hi, lo = (mxT[n][:, 4 * half:4 * half + 4, :].rearrange("p c n -> p (c n)")
                              for n in range(2))
                    dve.wait_ge(xh_ev, 2 * t + half + 1)
                    nc.vector.tensor_tensor(lo, ps, hi.bitcast(F32), ALU.subtract).then_inc(xlo_ev, 1)

            def tile(t, e, b, lo_t, kind, last):
                if kind == 0:
                    for c in range(FC):
                        split(e, GU_PIECES + c, wd[0][:, c, :], wd[1][:, c, :])
                if kind < 2 and not last:
                    split_gu(e + 1, 1 - b, EARLY[kind])
                for half, done, ok in ((0, ua_ps, hida_ok), (1, ub_ps, hidb_ok)):
                    cols = slice(half * F // 2, (half + 1) * F // 2)
                    dve.wait_ge(done, t + 1)
                    if half == 0:
                        dve.wait_ge(silu_ok, t + 1)
                    nc.vector.tensor_tensor(hid[:, cols], sgate[:, cols], psU[half],
                                            ALU.mult).then_inc(ok, 1)
                for half in range(2):
                    hi, lo = (hidT[n][:, 2 * half:2 * half + 2, :].rearrange("p c n -> p (c n)")
                              for n in range(2))
                    dve.wait_ge(hh_ev, 2 * t + half + 1)
                    nc.vector.tensor_tensor(lo, psH[half],
                                            hi.bitcast(F32), ALU.subtract).then_inc(hl_ev, 1)
                turn_x(t + 1)
                if kind < 2 and not last:
                    split_gu(e + 1, 1 - b, LATE[kind])
                dve.wait_ge(y1_ps, t + 2)
                entries_there(dve, e, b, kind)
                dve.wait_ge(y_out, 16 * t + 32)
                nc.vector.tensor_scalar(yrow[:, HALF:D], psY[:, HALF:D], gate_of(t, b, lo_t), None,
                                        ALU.mult).then_inc(yd_ok, 1)

            split_gu(0, 0, range(2, GU_PIECES))
            turn_x(0)
            expert_tiles(dve, tile)

            def invert(t, b):
                b %= LB
                dve.wait_ge(fstd_ok, t + 1)
                link(nc.vector.reciprocal(lnrs[:, b:b + 1], lnstd[:, b:b + 1]))
                nc.vector.scalar_tensor_tensor(lnsh[:, b:b + 1], lnmv[:, b, 0:1], -1.0,
                                               lnrs[:, b:b + 1], ALU.mult, ALU.mult).then_inc(fnn_ok, 1)

            def normal(t, i, b):
                dve.wait_ge(fin_in[b], 16 * i + 16)
                statistics(fin_r[:, b, :], b % LB).then_inc(fn_ok, 1)

            def gain(t, b):
                if is_first(t):
                    dve.wait_ge(ln2_in, 32)
                dve.wait_ge(fg_ok, t + 1)
                nc.vector.tensor_tensor(fin_r[:, b, :], fin_r[:, b, :], lng2,
                                        ALU.mult).then_inc(fb_ok, 1)

            def fin(t, i, b):
                step.begin(start + 2 * t if is_first(t) else start + 2 * t - 1)
                normal(t, i, b)
                if not is_first(t):
                    invert(t - 1, (b - 1) % FB)
                if not is_first(t, 2):
                    gain(t - 2, (b - 2) % FB)

            start = step.start + step.k
            for b in range(FB):
                fin(b, 0, b)
            with dve.Fori(1, TILES // FB) as i:
                for b in range(FB):
                    fin(FB * i + b, i, b)
            step.begin(start + 2 * TILES - 1)
            invert(TILES - 1, FB - 1)
            gain(TILES - 2, FB - 2)
            gain(TILES - 1, FB - 1)

        @block.gpsimd
        def _(pool):
            nc.gpsimd.iota(padl.rearrange("p (r w) -> p r w", w=2), [[0, BLOCKS], [0, 2]], base=S,
                           channel_multiplier=1).then_inc(pad_made, 1)
            pool.wait_ge(wi_in, 16)
            nc.gpsimd.memset(foldq[:, 1, :, 0:1], 0.0).then_inc(folded_o, 1)
            nc.gpsimd.tensor_tensor(foldq[:, 1, :, 1:P], w_in_g[:, :, 1:P],
                                    w_in_g[:, :, GROUP_DIM - 1:P:-1], ALU.subtract).then_inc(folded_o, 1)

            def fetch(g, i, b):
                if not is_first(g, 2):
                    pool.wait_ge(xj_ps, tr_base(g - 1) + 4)
                    pool.wait_ge(h_out[b], 64 * i)
                nc.gpsimd.tensor_copy(rowg[:, 2 * b:2 * b + 2], rowix[:, ds(2 * g, 2)]
                                      ).then_inc(rowg_ok, 1)
                own_wait(pool, rowg_ok, g + 1, pool_gate)
                for s in range(2):
                    pool.indirect_dma_start(
                        rows[:, b, s, :], None, x,
                        bass.IndirectOffsetOnAxis(ap=rowg[:, 2 * b + s:2 * b + s + 1], axis=0)
                    ).then_inc(rows_in[b], 16)

            def list_tokens(g):
                if not is_first(g):
                    pool.wait_ge(list_out, 64 * g)
                nc.gpsimd.tensor_copy(paygv[:, :, :, 0], rep_last(rowix[:, ds(2 * g, 2)], 2)
                                      ).then_inc(payg_ok, 1)
                pool.wait_ge(payg_ok, g + 1)
                pool.wait_ge(gate_ok, g + 1)
                own_wait(pool, dest_ok, g + 1, pool_gate)
                for s in range(2):
                    for k in range(2):
                        pool.indirect_dma_start(
                            lists, bass.IndirectOffsetOnAxis(ap=desti[:, 2 * s + k:2 * s + k + 1], axis=0),
                            payg[:, 4 * s + 2 * k:4 * s + 2 * k + 2], None).then_inc(list_out, 16)

            def shift(g, b):
                for s in range(2):
                    pool.wait_ge(hg_ok, 2 * g + s + 1)
                    nc.gpsimd.tensor_tensor(rows[:, b, s, :], rows[:, b, s, :], lnb[:, :],
                                            ALU.add).then_inc(h_ok, 1)

            def store_h(g, b):
                own_wait(pool, h_ok, 2 * g + 2, pool_gate)
                for s in range(2):
                    for dst in (hd, acc):
                        pool.indirect_dma_start(
                            dst, bass.IndirectOffsetOnAxis(ap=rowg[:, 2 * b + s:2 * b + s + 1], axis=0),
                            rows[:, b, s, :], None).then_inc(h_out[b], 16)

            def group(g, b, i):
                last = isinstance(g, int) and g == GROUPS - 1
                if not (is_first(g) or last):
                    fetch(g + 1, i if b == 0 else i + 1, 1 - b)
                if last:
                    shift(g, b)
                if not is_first(g, 2):
                    list_tokens(g - 2)
                if not last:
                    shift(g, b)
                store_h(g, b)

            pool.wait_ge(ix_in, 16)
            pool.wait_ge(ab_ps, AB_JOBS)
            pool.wait_ge(ln_in, 32)
            pool.wait_ge(pad_out, 48)
            fetch(0, 0, 0)
            fetch(1, 0, 1)
            group(0, 0, 0)
            group(1, 1, 0)
            with pool.Fori(1, GROUPS // 2 - 1) as i:
                for b in range(2):
                    group(2 * i + b, b, i)
            for b in range(2):
                group(GROUPS - 2 + b, b, GROUPS // 2 - 1)
            list_tokens(GROUPS - 2)
            list_tokens(GROUPS - 1)

            pool.wait_ge(p_ps, GROUPS)
            for b in range(2):
                pool.wait_ge(h_out[b], 64 * (GROUPS // 2))
            pool.wait_ge(tab_ok, 1)
            nc.gpsimd.iota(sx[:, :], [[0, 1]], base=S, channel_multiplier=1).then_inc(sx_ok, 1)
            nc.gpsimd.iota(sxn[:, :], [[0, 1]], base=S, channel_multiplier=1).then_inc(sx_ok, 1)
            nc.gpsimd.memset(yrow[:, 0:HALF], 0.0).then_inc(ya_ok, 2)
            nc.gpsimd.memset(yrow[:, HALF:D], 0.0).then_inc(yd_ok, 2)
            pool.wait_ge(ya_ok, 2)
            pool.wait_ge(yd_ok, 2)

            def gather(t):
                own_wait(pool, x1_ps, t + 1, pool_gate)
                pool.indirect_dma_start(xrow, None, hd, bass.IndirectOffsetOnAxis(ap=ixg[:, 0:1], axis=0)
                                        ).then_inc(xrow_in, 16)

            def scatter(t):
                pool.wait_ge(ya_ok, t + 1)
                own_wait(pool, yd_ok, t + 1, pool_gate)
                pool.wait_ge(sx_ok, 2)
                pool.indirect_dma_start(acc, bass.IndirectOffsetOnAxis(ap=sx[:, 0:1], axis=0),
                                        yrow, None, compute_op=ALU.add).then_inc(y_out, 16)
                own_wait(pool, y_out, 16 * t + 16, pool_gate)
                nc.gpsimd.tensor_copy(sx[:, :], sxn[:, :]).then_inc(sx_ok, 1)
                own_wait(pool, sx_ok, 2 * t + 3, pool_gate)

            def tile(t, e, b, lo, kind, last):
                entries_there(pool, e, b, kind)
                own_wait(pool, x1_ps, t + 1, pool_gate)
                nc.gpsimd.tensor_copy(ixg[:, :], entries[:, b, ds(block_of(t, lo), 1), 0]
                                      ).then_inc(ixg_ok, 1)
                own_wait(pool, ixg_ok, t + 1, pool_gate)
                gather(t)
                scatter(t)
                nc.gpsimd.tensor_copy(sxn[:, :], ixg[:, :]).then_inc(sx_ok, 1)
                own_wait(pool, sx_ok, 2 * t + 4, pool_gate)

            expert_tiles(pool, tile)
            total = pool.value_load(tstart[0:1, E:E + 1], min_val=2 * E, max_val=MAX_TILES)
            gather(total)
            scatter(total)
            pool.wait_ge(ya_ok, total + 2)
            own_wait(pool, yd_ok, total + 2, pool_gate)
            pool.indirect_dma_start(acc, bass.IndirectOffsetOnAxis(ap=sx[:, 0:1], axis=0),
                                    yrow, None, compute_op=ALU.add).then_inc(y_out, 16)

            pool.wait_ge(ln2_in, 32)

            def fin(t, b):
                pool.wait_ge(fb_ok, t + 1)
                nc.gpsimd.tensor_tensor(fin_r[:, b, :], fin_r[:, b, :], lnb2,
                                        ALU.add).then_inc(fh_ok, 1)

            with pool.Fori(0, TILES // FB) as i:
                for b in range(FB):
                    fin(FB * i + b, b)


_INS = ["x", "fourier_w_in", "fourier_w_out", "router_w", "router_b",
        "expert_w_gate", "expert_w_up", "expert_w_down", "ln_g", "ln_b"]


def kernel(**inputs):
    import concourse.bacc as bacc
    from concourse.bass_utils import run_bass_kernel_spmd

    nc = bacc.Bacc("TRN2", target_bir_lowering=False, num_devices=1)
    arrays, ap = {}, {}

    def declare(name, a):
        arrays[name] = a
        ap[name] = nc.dram_tensor(name, a.shape, mybir.dt.from_np(a.dtype), kind="ExternalInput").ap()

    for name in _INS:
        declare(name, np.ascontiguousarray(inputs[name]))
    packed, const_at, m2, row_of = shape_constants()
    declare("consts", packed)
    declare("second_stage", m2)
    declare("row_of", row_of)
    out = nc.dram_tensor("out", (1, S, D), F32, kind="ExternalOutput").ap()
    trunk_kernel(nc, ap["x"][0], ap["fourier_w_in"][0], ap["fourier_w_out"][0], ap["router_w"],
                 ap["router_b"], ap["expert_w_gate"][0], ap["expert_w_up"][0],
                 ap["expert_w_down"][0], ap["ln_g"][0], ap["ln_b"][0],
                 ap["consts"], const_at, ap["second_stage"], ap["row_of"], out[0])
    r = run_bass_kernel_spmd(nc, [arrays], core_ids=[0])
    return r.results[0]["out"]
```
